# Optimizing a Trainium2 kernel written in Bass

```python
import math
import jax, jax.numpy as jnp
from jax import lax
import numpy as np

D_MODEL = 2048
BATCH = 1
SEQ = 256
DEPTH = 1

MEM_LEN = 256
MEM_HEADS = 4
MEM_HEAD_DIM = D_MODEL // MEM_HEADS

BLOCK_Q = 128

SB_HEADS = 8
SB_HEAD_DIM = D_MODEL // 16
SB_WIDTH = SB_HEADS * SB_HEAD_DIM

DIFF_HEADS = 8
DIFF_V_DIM = D_MODEL // 16
DIFF_QK_DIM = DIFF_V_DIM // 2
DIFF_Q_WIDTH = DIFF_HEADS * 2 * DIFF_QK_DIM
DIFF_WIDTH = DIFF_HEADS * DIFF_V_DIM

MIX_WIDTH = SB_WIDTH + DIFF_WIDTH
IN_SPLITS = (SB_WIDTH, SB_WIDTH, SB_WIDTH, DIFF_Q_WIDTH, DIFF_Q_WIDTH, DIFF_WIDTH)
IN_WIDTH = sum(IN_SPLITS)

ROPE_DIM = DIFF_QK_DIM // 4
ROPE_THETA = 500000.0

PEER_HEADS = 8
N_KEYS = 128
N_EXPERTS = N_KEYS * N_KEYS
PEER_TOPK = 16
PEER_QUERY_DIM = 256
PEER_HALF = PEER_QUERY_DIM // 2
PEER_TOKEN_BLOCK = 128

LN_EPS = 1e-5
RMS_EPS = 1e-6
DEEPNORM_ALPHA = (2 * DEPTH) ** 0.25
DEEPNORM_BETA = (8 * DEPTH) ** -0.25

kernel_name = "hybrid_stickbreak_diffattn_peer_deepnorm"

def layer_norm(x, g, b):
    xf = x.astype(jnp.float32)
    mu = jnp.mean(xf, axis=-1, keepdims=True)
    var = jnp.mean(jnp.square(xf - mu), axis=-1, keepdims=True)
    return ((xf - mu) * lax.rsqrt(var + LN_EPS) * g.astype(jnp.float32)
            + b.astype(jnp.float32)).astype(x.dtype)

def rms_norm(x, g):
    xf = x.astype(jnp.float32)
    xf = xf * lax.rsqrt(jnp.mean(jnp.square(xf), axis=-1, keepdims=True) + RMS_EPS)
    return (xf * g.astype(jnp.float32)).astype(x.dtype)

def rope_partial(t, positions):
    half = ROPE_DIM // 2
    inv_freq = jnp.power(ROPE_THETA, -jnp.arange(half, dtype=jnp.float32) * 2.0 / ROPE_DIM)
    ang = positions.astype(jnp.float32)[:, None] * inv_freq[None, :]
    cos = jnp.cos(ang).astype(t.dtype)
    sin = jnp.sin(ang).astype(t.dtype)
    t1 = t[..., :half]
    t2 = t[..., half:ROPE_DIM]
    rest = t[..., ROPE_DIM:]
    return jnp.concatenate([t1 * cos - t2 * sin, t2 * cos + t1 * sin, rest], axis=-1)

def to_query_blocks(t):
    b, h, s, d = t.shape
    return t.reshape(b, h, s // BLOCK_Q, BLOCK_Q, d).transpose(2, 0, 1, 3, 4)

def from_query_blocks(o):
    nb, b, h, q, d = o.shape
    return o.transpose(1, 0, 3, 2, 4).reshape(b, nb * q, h, d)

def stick_breaking_attention(q, k, v):
    s_len, d = q.shape[2], q.shape[3]
    scale = 1.0 / math.sqrt(d)
    key_pos = jnp.arange(s_len)
    starts = jnp.arange(s_len // BLOCK_Q) * BLOCK_Q

    def block(args):
        qb, start = args
        z = jnp.einsum('bhqd,bhkd->bhqk', qb, k).astype(jnp.float32) * scale
        q_pos = start + jnp.arange(BLOCK_Q)
        before = key_pos[None, :] < q_pos[:, None]
        log_beta = jax.nn.log_sigmoid(z)
        log_keep = jnp.where(before, jax.nn.log_sigmoid(-z), 0.0)
        log_stick = lax.cumsum(log_keep, axis=3, reverse=True) - log_keep
        w = jnp.where(before, jnp.exp(log_beta + log_stick), 0.0)
        return jnp.einsum('bhqk,bhkd->bhqd', w.astype(v.dtype), v)

    return from_query_blocks(lax.map(block, (to_query_blocks(q), starts)))

def differential_attention(q1, k1, q2, k2, v, lam):
    s_len = q1.shape[2]
    scale = 1.0 / math.sqrt(DIFF_QK_DIM)
    key_pos = jnp.arange(s_len)
    starts = jnp.arange(s_len // BLOCK_Q) * BLOCK_Q

    def block(args):
        q1b, q2b, start = args
        q_pos = start + jnp.arange(BLOCK_Q)
        causal = key_pos[None, :] <= q_pos[:, None]
        s1 = jnp.einsum('bhqd,bhkd->bhqk', q1b, k1).astype(jnp.float32) * scale
        s2 = jnp.einsum('bhqd,bhkd->bhqk', q2b, k2).astype(jnp.float32) * scale
        p1 = jax.nn.softmax(jnp.where(causal, s1, -jnp.inf), axis=-1)
        p2 = jax.nn.softmax(jnp.where(causal, s2, -jnp.inf), axis=-1)
        w = p1 - lam * p2
        return jnp.einsum('bhqk,bhkd->bhqd', w.astype(v.dtype), v)

    out = lax.map(block, (to_query_blocks(q1), to_query_blocks(q2), starts))
    return from_query_blocks(out)

def hybrid_mixer(x, positions, w_in, sb_norm_gain, df_lambda, df_subln_gain, w_o, lambda_init):
    b, s, _ = x.shape
    proj = x @ w_in
    offsets = list(np.cumsum(IN_SPLITS)[:-1])
    sb_q, sb_k, sb_v, df_q, df_k, df_v = jnp.split(proj, offsets, axis=-1)

    def heads(t, h, d):
        return t.reshape(b, s, h, d).transpose(0, 2, 1, 3)

    sb_o = stick_breaking_attention(heads(sb_q, SB_HEADS, SB_HEAD_DIM),
                                    heads(sb_k, SB_HEADS, SB_HEAD_DIM),
                                    heads(sb_v, SB_HEADS, SB_HEAD_DIM))
    sb_o = rms_norm(sb_o, sb_norm_gain)

    dq = df_q.reshape(b, s, DIFF_HEADS, 2, DIFF_QK_DIM).transpose(3, 0, 2, 1, 4)
    dk = df_k.reshape(b, s, DIFF_HEADS, 2, DIFF_QK_DIM).transpose(3, 0, 2, 1, 4)
    q1, q2 = rope_partial(dq[0], positions), rope_partial(dq[1], positions)
    k1, k2 = rope_partial(dk[0], positions), rope_partial(dk[1], positions)
    lf = df_lambda.astype(jnp.float32)
    lam = (jnp.exp(jnp.sum(lf[0] * lf[1])) - jnp.exp(jnp.sum(lf[2] * lf[3]))
           + lambda_init)
    df_o = differential_attention(q1, k1, q2, k2, heads(df_v, DIFF_HEADS, DIFF_V_DIM), lam)
    df_o = rms_norm(df_o, df_subln_gain) * (1.0 - lambda_init)

    mixed = jnp.concatenate([sb_o.reshape(b, s, SB_WIDTH),
                             df_o.reshape(b, s, DIFF_WIDTH)], axis=-1)
    return mixed @ w_o

def memory_cross_attention(x, mem, w_mq, w_mkv, w_mo):
    b, s, _ = x.shape
    m = mem.shape[1]
    q = (x @ w_mq).reshape(b, s, MEM_HEADS, MEM_HEAD_DIM)
    kv = (mem @ w_mkv).reshape(b, m, 2, MEM_HEADS, MEM_HEAD_DIM)
    k, v = kv[:, :, 0], kv[:, :, 1]
    scores = jnp.einsum('bshd,bmhd->bhsm', q, k).astype(jnp.float32) / math.sqrt(MEM_HEAD_DIM)
    p = jax.nn.softmax(scores, axis=-1)
    o = jnp.einsum('bhsm,bmhd->bshd', p.astype(v.dtype), v).reshape(b, s, D_MODEL)
    return o @ w_mo

def peer_ffn(x, w_pq, sub_keys, expert_u, expert_v):
    b, s, d = x.shape
    q = (x @ w_pq).reshape(b, s, PEER_HEADS, 2, PEER_HALF)
    s1 = jnp.einsum('bshd,nd->bshn', q[..., 0, :], sub_keys[0]).astype(jnp.float32)
    s2 = jnp.einsum('bshd,nd->bshn', q[..., 1, :], sub_keys[1]).astype(jnp.float32)
    v1, i1 = lax.top_k(s1, PEER_TOPK)
    v2, i2 = lax.top_k(s2, PEER_TOPK)
    cand = (v1[..., :, None] + v2[..., None, :]).reshape(b, s, PEER_HEADS, PEER_TOPK * PEER_TOPK)
    cand_idx = (i1[..., :, None] * N_KEYS + i2[..., None, :]).reshape(
        b, s, PEER_HEADS, PEER_TOPK * PEER_TOPK)
    top, pos = lax.top_k(cand, PEER_TOPK)
    idx = jnp.take_along_axis(cand_idx, pos, axis=-1)
    g = jax.nn.softmax(top, axis=-1)

    n_blk = (b * s) // PEER_TOKEN_BLOCK
    xb = x.reshape(n_blk, PEER_TOKEN_BLOCK, d)
    ib = idx.reshape(n_blk, PEER_TOKEN_BLOCK, PEER_HEADS, PEER_TOPK)
    gb = g.reshape(n_blk, PEER_TOKEN_BLOCK, PEER_HEADS, PEER_TOPK)

    def block(args):
        xt, it, gt = args
        u = jnp.take(expert_u, it, axis=0)
        h = jnp.einsum('chkd,cd->chk', u, xt).astype(jnp.float32)
        a = gt * jax.nn.gelu(h, approximate=False)
        vv = jnp.take(expert_v, it, axis=0)
        return jnp.einsum('chk,chkd->cd', a.astype(x.dtype), vv)

    return lax.map(block, (xb, ib, gb)).reshape(b, s, d)

def setup_inputs(seed: int = 0) -> dict:
    key = jax.random.key(seed)
    ks = jax.random.split(key, 24)
    f32 = jnp.float32
    beta = DEEPNORM_BETA
    nrm = lambda k, shape: jax.random.normal(k, shape, dtype=f32)

    col_scale = jnp.concatenate([jnp.ones((2 * SB_WIDTH,), f32), beta * jnp.ones((SB_WIDTH,), f32),
                                 jnp.ones((2 * DIFF_Q_WIDTH,), f32), beta * jnp.ones((DIFF_WIDTH,), f32)])
    mkv_scale = jnp.concatenate([jnp.ones((D_MODEL,), f32), beta * jnp.ones((D_MODEL,), f32)])
    return {
        "x": nrm(ks[0], (BATCH, SEQ, D_MODEL)),
        "mem": nrm(ks[1], (BATCH, MEM_LEN, D_MODEL)),
        "w_in": nrm(ks[2], (DEPTH, D_MODEL, IN_WIDTH)) * (D_MODEL ** -0.5) * col_scale,
        "sb_norm_gain": 1.0 + 0.02 * nrm(ks[3], (DEPTH, SB_HEADS, SB_HEAD_DIM)),
        "df_lambda": 0.1 * nrm(ks[4], (DEPTH, 4, DIFF_QK_DIM)),
        "df_subln_gain": 1.0 + 0.02 * nrm(ks[5], (DEPTH, DIFF_V_DIM)),
        "w_o": nrm(ks[6], (DEPTH, MIX_WIDTH, D_MODEL)) * (MIX_WIDTH ** -0.5) * beta,
        "ln1_gain": 1.0 + 0.02 * nrm(ks[7], (DEPTH, D_MODEL)),
        "ln1_bias": 0.02 * nrm(ks[8], (DEPTH, D_MODEL)),
        "w_mq": nrm(ks[9], (DEPTH, D_MODEL, D_MODEL)) * (D_MODEL ** -0.5),
        "w_mkv": nrm(ks[10], (DEPTH, D_MODEL, 2 * D_MODEL)) * (D_MODEL ** -0.5) * mkv_scale,
        "w_mo": nrm(ks[11], (DEPTH, D_MODEL, D_MODEL)) * (D_MODEL ** -0.5) * beta,
        "ln2_gain": 1.0 + 0.02 * nrm(ks[12], (DEPTH, D_MODEL)),
        "ln2_bias": 0.02 * nrm(ks[13], (DEPTH, D_MODEL)),
        "w_pq": nrm(ks[14], (DEPTH, D_MODEL, PEER_HEADS * PEER_QUERY_DIM)) * (D_MODEL ** -0.5),
        "peer_sub_keys": nrm(ks[15], (DEPTH, 2, N_KEYS, PEER_HALF)) * (PEER_HALF ** -0.5),
        "peer_u": nrm(ks[16], (DEPTH, N_EXPERTS, D_MODEL)) * (D_MODEL ** -0.5),
        "peer_v": nrm(ks[17], (DEPTH, N_EXPERTS, D_MODEL)) * beta,
        "ln3_gain": 1.0 + 0.02 * nrm(ks[18], (DEPTH, D_MODEL)),
        "ln3_bias": 0.02 * nrm(ks[19], (DEPTH, D_MODEL)),
    }

def reference(x, mem, w_in, sb_norm_gain, df_lambda, df_subln_gain, w_o, ln1_gain, ln1_bias,
              w_mq, w_mkv, w_mo, ln2_gain, ln2_bias, w_pq, peer_sub_keys, peer_u, peer_v,
              ln3_gain, ln3_bias):
    positions = jnp.arange(x.shape[1])
    for l in range(DEPTH):
        lambda_init = 0.8 - 0.6 * math.exp(-0.3 * l)
        mix = hybrid_mixer(x, positions, w_in[l], sb_norm_gain[l], df_lambda[l],
                           df_subln_gain[l], w_o[l], lambda_init)
        x = layer_norm(DEEPNORM_ALPHA * x + mix, ln1_gain[l], ln1_bias[l])
        xa = memory_cross_attention(x, mem, w_mq[l], w_mkv[l], w_mo[l])
        x = layer_norm(DEEPNORM_ALPHA * x + xa, ln2_gain[l], ln2_bias[l])
        ff = peer_ffn(x, w_pq[l], peer_sub_keys[l], peer_u[l], peer_v[l])
        x = layer_norm(DEEPNORM_ALPHA * x + ff, ln3_gain[l], ln3_bias[l])
    return x


_drawn_inputs = setup_inputs


def setup_inputs(seed=0):
    import zlib

    import numpy as np

    out = dict(_drawn_inputs(seed))
    spreads = {}
    factors = {'df_lambda': 3.234,
     'ln3_gain': 23.036,
     'ln3_bias': 23.541,
     'df_subln_gain': 2.676,
     'sb_norm_gain': 2.927}
    for name, (base, spread) in spreads.items():
        noise = np.random.default_rng([zlib.crc32(name.encode()), seed]).standard_normal(out[name].shape)
        drawn = base * np.exp(spread * noise) if base else spread * noise
        out[name] = __import__('jax').numpy.asarray(drawn.astype(out[name].dtype))
    for name, factor in factors.items():
        out[name] = (out[name] * factor).astype(out[name].dtype)
    return out
```

```python
import math
from contextlib import ExitStack

import concourse.bass as bass
from concourse import mybir

F32 = mybir.dt.float32
U32 = mybir.dt.uint32
ALU = mybir.AluOpType
ACT = mybir.ActivationFunctionType
AX_X = mybir.AxisListType.X

P = 128
BANK = 512
NEG_BIG = -1.0e30
NEG_MAX = -3.0e38
ROPE_THETA = 500000.0
LAMBDA_INIT = 0.8 - 0.6 * math.exp(-0.3 * 0)
LN_EPS, RMS_EPS = 1e-5, 1e-6
ALPHA = 2.0 ** 0.25


class Steps:

    def __init__(self, eng, sem):
        self.eng, self.sem, self.base, self.n = eng, sem, 0, 0

    def did(self, ins):
        ins.then_inc(self.sem, 1)
        self.n += 1

    def wait(self):
        self.eng.wait_ge(self.sem, self.base + self.n)

    def enter(self, i, per):
        self.start, self.per = self.base + self.n, per
        self.base, self.n = self.start + i * per, 0

    def leave(self, times):
        assert self.n == self.per, (self.n, self.per)
        self.base, self.n = self.start + times * self.per, 0


def layer_program(nc, x, mem, w_in, sb_gain, df_lambda, df_gain, w_o, ln1_g, ln1_b, w_mq, w_mkv,
                  w_mo, ln2_g, ln2_b, w_pq, sub_keys, peer_u, peer_v, ln3_g, ln3_b, rope, out):
    D = x.shape[2]
    NT = x.shape[1] // P
    T = NT * P
    KB = D // P
    HK = KB // 2
    NP = D // BANK
    SBH, DH = sb_gain.shape[1], sb_gain.shape[2]
    SBW = SBH * DH
    QD = df_lambda.shape[2]
    ROT = rope.shape[1] // 2
    PH = w_pq.shape[2] // (2 * P)
    NKEY = sub_keys.shape[2]
    TOPK = 16
    MH = 4
    MB = KB // MH
    SB_SCALE, DF_SCALE, M_SCALE = DH ** -0.5, QD ** -0.5, (D // MH) ** -0.5
    assert (P, T, KB, NP) == (DH, 2 * P, 16, 4) and NKEY == P and PH == SBH == 8

    x_rows = x[0].rearrange("(t p) n -> p t n", p=P)
    mem_rows = mem[0].rearrange("(t p) n -> p t n", p=P)
    out_rows = out[0].rearrange("(t p) n -> p t n", p=P)

    with ExitStack() as ctx:
        def sb(name, cols, dt=F32):
            return ctx.enter_context(nc.sbuf_tensor(name, [P, cols], dt))

        def sem(name):
            return ctx.enter_context(nc.semaphore(name))

        RC = NT * D
        r0, r1, r2, r3, r4, r5, r6 = [sb(f"region{n}", RC) for n in range(7)]
        ring = sb("weight_ring", 4 * HK * BANK)

        def blocks(r):
            return r[:, :].rearrange("p (k t) -> p k t", k=KB)

        def rows(r):
            return r[:, :].rearrange("p (t n) -> p t n", t=NT)

        xT, mixedT, cqT = blocks(r0), blocks(r0), blocks(r0)
        sb_qkT, coT = blocks(r1), blocks(r1)
        z1 = rows(r1)
        sb_v, df_v = rows(r2)[:, :, 0:SBW], rows(r2)[:, :, SBW:D]
        x1 = rows(r2)
        df_qk = rows(r3)
        gain_b, bias_b = r3[:, 0:D], r3[:, D:2 * D]
        memT, x1T, x2T = blocks(r4), blocks(r4), blocks(r4)
        x_in, mkT, x2 = rows(r5), blocks(r5), rows(r5)
        mem_in, mv, key_scores = rows(r6), rows(r6), rows(r6)
        half_panel = [ring[:, s * HK * BANK:(s + 1) * HK * BANK].rearrange("p (k n) -> p k n", k=HK)
                      for s in range(4)]
        free = [ring[:, s * D:(s + 1) * D] for s in range(8)]
        u_ring = free
        v_ring = [r[:, s * D:(s + 1) * D] for r in (r0, r1, r2, r4) for s in range(2)]
        NU = NV = 8
        y_out = ring[:, 0:RC].rearrange("p (t n) -> p t n", t=NT)

        ident = sb("ident", P)
        before = sb("before", P)
        neg_after = sb("neg_after", P)
        neg_ones = sb("neg_ones", P)
        causal = sb("causal", T)
        rope_cs = sb("rope_cs", NT * 2 * ROT)
        sbg = sb("sbg", SBW)
        dfg = sb("dfg", DH)
        keysT = sb("keysT", 2 * NKEY)
        iota = sb("iota", TOPK)
        small = sb("small", 128)
        ta = sb("temps", 5632)

        cos2 = rope_cs[:, :].rearrange("p (t c) -> p t c", t=NT)[:, :, 0:ROT]
        sin2 = rope_cs[:, :].rearrange("p (t c) -> p t c", t=NT)[:, :, ROT:2 * ROT]
        HR = ROT // 2
        k_st = ta[:, 0:512]
        df_st = ta[:, 512:1536].rearrange("p (t q c) -> p t q c", t=NT, q=2)
        ZC = 3 * P
        e_z = [ta[:, 1536 + n * ZC:1536 + (n + 1) * ZC] for n in range(2)]
        sp_z = [ta[:, 2304 + n * ZC:2304 + (n + 1) * ZC] for n in range(2)]
        sb_n = ta[:, 1536:2048].rearrange("p (b c) -> p b c", b=4)
        dfT = [ta[:, 3072 + n * 512:3584 + n * 512] for n in range(2)]
        pT = [ta[:, 3072 + n * 512:3072 + n * 512 + ZC] for n in range(2)]
        s_t0 = ta[:, 4096:4608].rearrange("p (b c) -> p b c", b=4)
        df_n = ta[:, 4096:4608].rearrange("p (b c) -> p b c", b=4)
        s_t1 = [ta[:, 4608 + n * 512:5120 + n * 512].rearrange("p (s c) -> p s c", s=2) for n in range(2)]
        c_p = ta[:, 0:MH * NT * T].rearrange("p (h t m) -> p h t m", h=MH, t=NT)
        c_pT = ta[:, 2048:4096].rearrange("p (h m q) -> p h m q", h=MH, m=NT)
        pq_st = [ta[:, 2048 + s * 1024:3072 + s * 1024].rearrange("p (b t) -> p b t", b=4) for s in range(2)]
        keys_in = ta[:, 0:2 * NKEY]
        diag = ta[:, 0:TOPK * P].rearrange("p (j c) -> p j c", j=TOPK)
        tk = ta[:, 2048:5632]
        sc, sc_left = tk[:, 0:256], tk[:, 256:512]
        cand, cand_left = tk[:, 512:768], tk[:, 768:1024]
        hot, hot_v = tk[:, 1024:1280], tk[:, 1280:1536]
        val = tk[:, 1536:1568]
        ixf = tk[:, 1568:1600]
        top = tk[:, 1600:1616]
        ijf = tk[:, 1616:1648]
        picked = tk[:, 1648:1680]
        gate = [tk[:, 1680 + 16 * t:1696 + 16 * t] for t in range(NT)]
        hdot = [tk[:, 1712 + 16 * t:1728 + 16 * t] for t in range(NT)]
        act_h = [tk[:, 1744 + 16 * t:1760 + 16 * t] for t in range(NT)]
        weight = [tk[:, 1776 + 16 * t:1792 + 16 * t] for t in range(NT)]
        gsum, ntop = tk[:, 1808:1809], tk[:, 1809:1810]
        ints = tk[:, 1856:2048].bitcast(U32)
        ix, pos, ij = ints[:, 0:32], ints[:, 32:48], ints[:, 48:80]
        next_idx = [ints[:, 80 + 16 * t:96 + 16 * t] for t in range(NT)]
        idx_all = ints[:, 112:144]
        idx = [idx_all[:, 16 * t:16 * t + 16] for t in range(NT)]

        lam_in = ta[:, 0:4 * QD]
        lam_pr = ta[:, 4 * QD:5 * QD]
        neg_lam = small[:, 0:1]
        lam_s = small[:, 1:3]
        lam_e = small[:, 3:5]
        nhalf = small[:, 5:9]
        ss, rs = small[:, 9:13], small[:, 13:17]
        dss, drs = small[:, 17:21], small[:, 21:25]
        mx, nmx, dsum, rsum, c2 = [small[:, 25 + 8 * n:33 + 8 * n] for n in range(5)]
        stats = small[:, 65:113].rearrange("p (t q c) -> p t q c", t=NT, c=6)
        mvar = small[:, 113:117].rearrange("p (t c) -> p t c", t=NT)
        veps, rstd = small[:, 117:119], small[:, 119:121]

        ps = ctx.enter_context(nc.psum_tensor("ps", [P, 8, BANK], F32))

        def bank(b, n=1):
            return ps[:, b:b + n, :].rearrange("p b c -> p (b c)")

        x_landed, mem_landed, small_landed = sem("x_landed"), sem("mem_landed"), sem("small_landed")
        w_landed = [sem(f"w_landed{s}") for s in range(4)]
        w_used = [sem(f"w_used{s}") for s in range(4)]
        pool_step, dve_step, act_step = sem("pool_step"), sem("dve_step"), sem("act_step")
        consts_ready = sem("consts_ready")
        turned, turned_taken = sem("turned"), sem("turned_taken")
        proj_taken = sem("proj_taken")
        roped = sem("roped")
        k_staged, df_staged = sem("k_staged"), sem("df_staged")
        z_ready, dfT_ready, dfT_copied = sem("z_ready"), sem("dfT_ready"), sem("dfT_copied")
        e_ready, sp_ready = sem("e_ready"), sem("sp_ready")
        s_ready, stick_ready = sem("s_ready"), sem("stick_ready")
        smax_ready, p_ready, wexp_in, wexp_out = sem("smax_ready"), sem("p_ready"), sem("wexp_in"), sem("wexp_out")
        w_ready, pw_ready = sem("w_ready"), sem("pw_ready")
        o_ready, pT_ready, pT_copied = sem("o_ready"), sem("pT_ready"), sem("pT_copied")
        ss_ready, ms_ready, rms_ready, o_normed = sem("ss_ready"), sem("ms_ready"), sem("rms_ready"), sem("o_normed")
        do_ready, oT_ready, oT_copied = sem("do_ready"), sem("oT_ready"), sem("oT_copied")
        z_landed, gb_landed = sem("z_landed"), sem("gb_landed")
        var_ready, rstd_ready, x_ready = sem("var_ready"), sem("rstd_ready"), sem("x_ready")
        cs_ready, cmax_ready, cp_ready, cn_ready = sem("cs_ready"), sem("cmax_ready"), sem("cp_ready"), sem("cn_ready")
        cT_ready, cT_copied, co_ready, co_copied = sem("cT_ready"), sem("cT_copied"), sem("co_ready"), sem("co_copied")
        keys_landed, keysT_ready, keysT_copied = sem("keys_landed"), sem("keysT_ready"), sem("keysT_copied")
        ks_ready, ks_copied = sem("ks_ready"), sem("ks_copied")
        top_ready, gexp_ready, idx_ready = sem("top_ready"), sem("gexp_ready"), sem("idx_ready")
        u_landed = [sem(f"u_landed{s}") for s in range(NU)]
        v_landed = [sem(f"v_landed{s}") for s in range(NV)]
        u_used, v_used, v_issued = sem("u_used"), sem("v_used"), sem("v_issued")
        slots_freed = sem("slots_freed")
        h_ready, gelu_ready, a_ready, diag_ready = sem("h_ready"), sem("gelu_ready"), sem("a_ready"), sem("diag_ready")
        acc_done, y_ready, y_stored = sem("acc_done"), sem("y_ready"), sem("y_stored")

        IN_PAIRS = w_in.shape[2] // (2 * BANK)
        MKV0 = IN_PAIRS
        WO0 = MKV0 + w_mkv.shape[2] // (2 * BANK)
        MQ0 = WO0 + NP // 2
        MO0 = MQ0 + NP // 2
        PQ0 = MO0 + NP // 2
        BODIES = SBH // 2
        CREDIT = 2
        RING_CREDIT = 16

        block = ctx.enter_context(nc.Block())

        @block.sync
        def _(sp):
            sp.dma_start(x_in, x_rows).then_inc(x_landed, 16)

            def load_pair(w, i, pair, first=False):
                for s in range(4):
                    if not first:
                        sp.wait_ge(w_used[s], pair)
                    cols = w[0][:, bass.ds(i * 2 * BANK + (s // 2) * BANK, BANK)]
                    src = cols.rearrange("(h k p) n -> h p k n", h=2, p=P)[s % 2]
                    sp.dma_start(half_panel[s], src).then_inc(w_landed[s], 16)

            load_pair(w_in, 0, 0, first=True)
            sp.dma_start(mem_in, mem_rows).then_inc(mem_landed, 16)
            with sp.Fori(1, IN_PAIRS) as i:
                load_pair(w_in, i, i)
            for w, first_pair in ((w_mkv, MKV0), (w_o, WO0), (w_mq, MQ0), (w_mo, MO0), (w_pq, PQ0)):
                with sp.Fori(0, w.shape[2] // (2 * BANK)) as i:
                    load_pair(w, i, i + first_pair)
            for t in range(NT):
                sp.wait_ge(y_ready, t + 1)
                sp.dma_start(out_rows[:, t, :], y_out[:, t, :]).then_inc(y_stored, 16)
            sp.wait_ge(y_stored, 16 * NT)

        @block.tensor
        def _(pe):
            def turn(src, group, nth):
                if nth >= 4:
                    pe.wait_ge(turned_taken, nth - 3)
                for k in (2 * group, 2 * group + 1):
                    for t in range(NT):
                        c = (k % 2) * T + t * P
                        m = nc.tensor.transpose(ps[:, 4 + nth % 4, c:c + P], src[:, t, k * P:(k + 1) * P], ident[:, :])
                m.then_inc(turned, 1)

            def half(kind, s, pair, acts, par, spare):
                h, b0 = s % 2, 2 * par
                if h == 0:
                    pe.wait_ge(proj_taken, pair * 2 + s // 2 + CREDIT - spare)
                pe.wait_ge(w_landed[s], pair * 16 + 16)
                for k in range(HK):
                    kk = h * HK + k
                    first, last = kk == 0, kk == KB - 1
                    if kind == "rows":
                        for t in range(NT):
                            m = nc.tensor.matmul(ps[:, b0 + t, :], acts[:, kk, t * P:(t + 1) * P],
                                                 half_panel[s][:, k, :], start=first, stop=last)
                    else:
                        for nb in range(4):
                            m = nc.tensor.matmul(ps[:, b0 + nb // 2, (nb % 2) * T:(nb % 2 + 1) * T],
                                                 half_panel[s][:, k, nb * P:(nb + 1) * P], acts[:, kk, :],
                                                 start=first and nb % 2 == 0, stop=last and nb % 2 == 1,
                                                 skip_group_check=True)
                m.then_inc(w_used[s], 1)

            def panel(kind, s, pair, acts):
                half(kind, 2 * s, pair, acts, s, 1)
                half(kind, 2 * s + 1, pair, acts, s, 1)

            def section(kind, first_pair, pairs, acts):
                with pe.Fori(first_pair, first_pair + pairs) as pair:
                    for s in range(2):
                        panel(kind, s, pair, acts)

            pe.wait_ge(consts_ready, 1)
            pe.wait_ge(x_landed, 16)
            for g in range(8):
                turn(x_in, g, g)
            pe.wait_ge(turned_taken, 8)
            section("cols", 0, 2, xT)
            section("rows", 2, 4, xT)
            pe.wait_ge(mem_landed, 16)
            for g in range(8):
                turn(mem_in, g, 8 + g)
            pe.wait_ge(turned_taken, 16)

            def attention_body(b, kind):
                pair = b + MKV0
                pe.wait_ge(k_staged, b + 1)
                pe.wait_ge(oT_copied, b * 2 + CREDIT)
                for hh in range(2):
                    q0 = (b * 2 + hh) * T
                    nc.tensor.matmul(ps[:, 2 + hh, 0:T], k_st[:, hh * T:hh * T + P], r1[:, bass.ds(q0, T)],
                                     start=True, stop=True)
                    nc.tensor.matmul(ps[:, 2 + hh, T:ZC], k_st[:, hh * T + P:(hh + 1) * T], r1[:, bass.ds(q0 + P, P)],
                                     start=True, stop=True).then_inc(z_ready, 1)
                pe.wait_ge(df_staged, b + 1)
                pe.wait_ge(pT_copied, b * 2 + CREDIT)
                for hh in range(2):
                    for q in range(2):
                        for t in range(NT):
                            m = nc.tensor.transpose(ps[:, 4 + hh, (q * NT + t) * P:(q * NT + t + 1) * P],
                                                    df_st[:, t, q, hh * P:(hh + 1) * P], ident[:, :])
                    m.then_inc(dfT_ready, 1)
                half(kind, 0, pair, memT, 0, 0)
                pe.wait_ge(dfT_copied, b * 2 + 2)
                pe.wait_ge(o_normed, b * 2 + CREDIT)
                for hh in range(2):
                    for st in range(2):
                        q = dfT[hh][st * QD:(st + 1) * QD, :]
                        nc.tensor.matmul(ps[:, 4 + st, hh * T:(hh + 1) * T], q[:, P:2 * P], q[:, T:2 * T],
                                         start=True, stop=True)
                        m = nc.tensor.matmul(ps[:, 6 + st, hh * P:(hh + 1) * P], q[:, 0:P], q[:, T:T + P],
                                             start=True, stop=True)
                m.then_inc(s_ready, 1)
                for hh in range(2):
                    pe.wait_ge(sp_ready, b * 2 + hh + 1)
                    nc.tensor.matmul(ps[:, 2 + hh, 0:ZC], neg_after[:, :], sp_z[hh], start=True, stop=False,
                                     skip_group_check=True)
                    nc.tensor.matmul(ps[:, 2 + hh, P:T], neg_ones[:, :], sp_z[hh][:, T:ZC], start=False, stop=True,
                                     skip_group_check=True).then_inc(stick_ready, 1)
                half(kind, 1, pair, memT, 0, 0)
                for hh in range(2):
                    pe.wait_ge(w_ready, b * 2 + hh + 1)
                    v0 = (b * 2 + hh) * DH
                    w = sp_z[hh]
                    nc.tensor.matmul(ps[:, 7, hh * T:hh * T + P], w[:, 0:P], r2[:, bass.ds(v0, DH)], start=True, stop=True)
                    nc.tensor.matmul(ps[:, 7, hh * T + P:(hh + 1) * T], w[:, P:T], r2[:, bass.ds(v0, DH)],
                                     start=True, stop=False)
                    m = nc.tensor.matmul(ps[:, 7, hh * T + P:(hh + 1) * T], w[:, T:ZC], r2[:, bass.ds(v0 + D, DH)],
                                         start=False, stop=True)
                m.then_inc(o_ready, 1)
                for hh in range(2):
                    pe.wait_ge(pw_ready, b * 2 + hh + 1)
                    for c, src in enumerate((s_t0[:, 2 * hh, :], s_t1[hh][:, 0, 0:P], s_t1[hh][:, 0, P:T])):
                        m = nc.tensor.transpose(ps[:, 4 + hh, c * P:(c + 1) * P], src, ident[:, :])
                    m.then_inc(pT_ready, 1)
                half(kind, 2, pair, memT, 0, 0)
                for hh in range(2):
                    pe.wait_ge(pT_copied, b * 2 + hh + 1 + CREDIT)
                    v0 = (b * 2 + hh) * DH + SBW
                    nc.tensor.matmul(ps[:, 6, hh * T:hh * T + P], pT[hh][:, 0:P], r2[:, bass.ds(v0, DH)],
                                     start=True, stop=True)
                    nc.tensor.matmul(ps[:, 6, hh * T + P:(hh + 1) * T], pT[hh][:, P:T], r2[:, bass.ds(v0, DH)],
                                     start=True, stop=False)
                    m = nc.tensor.matmul(ps[:, 6, hh * T + P:(hh + 1) * T], pT[hh][:, T:ZC],
                                         r2[:, bass.ds(v0 + D, DH)], start=False, stop=True)
                m.then_inc(do_ready, 1)
                pe.wait_ge(o_normed, b * 2 + 1 + CREDIT)
                for c in range(4):
                    m = nc.tensor.transpose(ps[:, 2, c * P:(c + 1) * P], sb_n[:, c, :], ident[:, :])
                m.then_inc(oT_ready, 1)
                half(kind, 3, pair, memT, 0, 0)
                pe.wait_ge(o_normed, b * 2 + 2 + CREDIT)
                for c in range(4):
                    m = nc.tensor.transpose(ps[:, 7, c * P:(c + 1) * P], df_n[:, c, :], ident[:, :])
                m.then_inc(oT_ready, 1)

            with pe.Fori(0, BODIES // 2) as b:
                attention_body(b, "cols")
            with pe.Fori(BODIES // 2, BODIES) as b:
                attention_body(b, "rows")
            pe.wait_ge(oT_copied, 2 * BODIES + CREDIT)
            pe.wait_ge(proj_taken, 2 * WO0 + CREDIT)
            section("rows", WO0, NP // 2, mixedT)

            def turn_norm(src, nth, first_chunk):
                for g in range(8):
                    if g % 2 == 0:
                        pe.wait_ge(x_ready, first_chunk + g // 2 + 1)
                    turn(src, g, nth + g)
                pe.wait_ge(turned_taken, nth + 8)

            turn_norm(x1, 16, 0)
            section("cols", MQ0, NP // 2, x1T)
            pe.wait_ge(proj_taken, 2 * MO0 + CREDIT)
            for h in range(MH):
                for t in range(NT):
                    for kb in range(MB):
                        m = nc.tensor.matmul(ps[:, 4 + h, t * T:(t + 1) * T], cqT[:, h * MB + kb, t * P:(t + 1) * P],
                                             mkT[:, h * MB + kb, :], start=kb == 0, stop=kb == MB - 1)
                m.then_inc(cs_ready, 1)
            for h in range(MH):
                pe.wait_ge(cn_ready, h + 1)
                for m_t in range(NT):
                    for t in range(NT):
                        m = nc.tensor.transpose(ps[:, h, m_t * T + t * P:m_t * T + (t + 1) * P],
                                                c_p[:, h, t, m_t * P:(m_t + 1) * P], ident[:, :])
                m.then_inc(cT_ready, 1)
            for g in range(KB // 2):
                if g % (MB // 2) == 0:
                    pe.wait_ge(cT_copied, g // (MB // 2) + 1)
                if g >= 4:
                    pe.wait_ge(co_copied, g - 3)
                for n in range(2):
                    blk = 2 * g + n
                    for m_t in range(NT):
                        m = nc.tensor.matmul(ps[:, 4 + g % 4, n * T:(n + 1) * T], mv[:, m_t, blk * P:(blk + 1) * P],
                                             c_pT[:, blk // MB, m_t, :], start=m_t == 0, stop=m_t == NT - 1)
                m.then_inc(co_ready, 1)
            pe.wait_ge(co_copied, KB // 2)
            section("rows", MO0, NP // 2, coT)
            pe.wait_ge(keys_landed, 16)
            for n in range(2):
                m = nc.tensor.transpose(ps[:, 7, n * P:(n + 1) * P], keys_in[:, n * NKEY:(n + 1) * NKEY], ident[:, :])
            m.then_inc(keysT_ready, 1)
            pe.wait_ge(keysT_copied, 1)
            turn_norm(x2, 24, 4)

            def key_products(pair, s):
                pe.wait_ge(proj_taken, pair * 2 + s + 1 + CREDIT)
                pe.wait_ge(ks_copied, pair * 2 + s - 2 * PQ0 + CREDIT - 1)
                for t in range(NT):
                    for n in range(4):
                        m = nc.tensor.matmul(ps[:, 4 + 2 * s + t, n * P:(n + 1) * P], pq_st[s][:, n, t * P:(t + 1) * P],
                                             keysT[:, (n % 2) * NKEY:(n % 2 + 1) * NKEY], start=True, stop=True)
                m.then_inc(ks_ready, 1)

            with pe.Fori(PQ0, PQ0 + NP // 2) as pair:
                panel("cols", 0, pair, x2T)
                half("cols", 2, pair, x2T, 1, 1)
                key_products(pair, 0)
                half("cols", 3, pair, x2T, 1, 1)
                key_products(pair, 1)

            pe.wait_ge(ks_copied, NP + CREDIT)
            pe.wait_ge(top_ready, 1)
            pe.wait_ge(consts_ready, 2)
            for b in range(8):
                m = nc.tensor.matmul(ps[:, b, :], diag[:, 0, :], x2[:, 0, 0:BANK], start=True, stop=True)
            m.then_inc(v_used, RING_CREDIT)

            def mix_body(h):
                for t in range(NT):
                    for j in range(TOPK):
                        n = (h * NT + t) * TOPK + j
                        pe.wait_ge(v_landed[j % NV], ((h * NT + t) * 2 + j // NV) * 16 + 16)
                        pe.wait_ge(diag_ready, n + 1)
                        for q in range(NP):
                            m = nc.tensor.matmul(ps[:, 4 * t + q, :], diag[:, j, :],
                                                 v_ring[j % NV][:, q * BANK:(q + 1) * BANK],
                                                 start=False, stop=False, skip_group_check=True)
                        m.then_inc(v_used, 1)

            with pe.Fori(0, PH) as h:
                mix_body(h)

        @block.scalar
        def _(act):
            steps = Steps(act, act_step)
            act.dma_start(rope_cs[:, :].rearrange("p (t c) -> p t c", t=NT),
                          rope.rearrange("(t p) c -> p t c", p=P)).then_inc(small_landed, 16)
            act.dma_start(lam_in, df_lambda[0].rearrange("a d -> (a d)").partition_broadcast(P)).then_inc(small_landed, 16)
            act.dma_start(sbg[:, :], sb_gain[0].rearrange("h d -> (h d)").partition_broadcast(P)).then_inc(small_landed, 16)
            act.dma_start(dfg[:, :], df_gain[0].partition_broadcast(P)).then_inc(small_landed, 16)
            act.sem_inc(proj_taken, CREDIT)
            act.sem_inc(ks_copied, CREDIT)
            act.sem_inc(oT_copied, CREDIT)
            act.sem_inc(pT_copied, CREDIT)

            def copy_turned(dst, nth):
                for g in range(8):
                    act.wait_ge(turned, nth + g + 1)
                    nc.scalar.activation(dst[:, g * 2 * T:(g + 1) * 2 * T], ps[:, 4 + (nth + g) % 4, :],
                                         ACT.Copy).then_inc(turned_taken, 1)

            def take(kind, dst, col, pair, s, b0):
                act.wait_ge(w_used[2 * s + 1], pair + 1)
                if kind == "rows":
                    nc.scalar.activation(dst[:, :, bass.ds(col, BANK)], ps[:, b0:b0 + 2, :],
                                         ACT.Copy).then_inc(proj_taken, 1)
                else:
                    nc.scalar.activation(dst[:, bass.ds(col, 2 * BANK)], bank(b0, 2), ACT.Copy).then_inc(proj_taken, 1)

            def section(kind, dst, first_pair, pairs, width=BANK):
                with act.Fori(0, pairs) as i:
                    for s in range(2):
                        take(kind, dst, (i * 2 + s) * width, i + first_pair, s, 2 * s)

            copy_turned(r0, 0)
            act.wait_ge(roped, 1)
            nc.scalar.activation(lam_e, lam_s, ACT.Exp).then_inc(roped, 1)
            section("cols", r1, 0, 2, 2 * BANK)
            section("rows", sb_v, 2, 1)
            section("rows", df_qk, 3, 2)
            section("rows", df_v, 5, 1)
            copy_turned(r4, 8)

            def attention_body(b, kind):
                for hh in range(2):
                    act.wait_ge(dfT_ready, b * 2 + hh + 1)
                    nc.scalar.activation(dfT[hh], ps[:, 4 + hh, :], ACT.Copy).then_inc(dfT_copied, 1)
                for hh in range(2):
                    act.wait_ge(z_ready, b * 2 + hh + 1)
                    for dst, src, func, scale in ((e_z[hh], ps[:, 2 + hh, 0:ZC], ACT.Copy, SB_SCALE),
                                                  (sp_z[hh], e_z[hh], ACT.Abs, 1.0), (sp_z[hh], sp_z[hh], ACT.Exp, -1.0)):
                        steps.did(nc.scalar.activation(dst, src, func, scale=scale))
                        steps.wait()
                    nc.scalar.activation(sp_z[hh], sp_z[hh], ACT.Ln, bias=1.0).then_inc(e_ready, 1)
                act.wait_ge(smax_ready, b + 1)
                for hh in range(2):
                    for st in range(2):
                        n = 2 * hh + st
                        nc.scalar.activation(s_t0[:, n, :], s_t0[:, n, :], ACT.Exp, bias=nmx[:, n:n + 1],
                                             scale=DF_SCALE, accum_out=dsum[:, n:n + 1])
                        m = nc.scalar.activation(s_t1[hh][:, st, :], s_t1[hh][:, st, :], ACT.Exp,
                                                 bias=nmx[:, 4 + n:5 + n], scale=DF_SCALE,
                                                 accum_out=dsum[:, 4 + n:5 + n])
                m.then_inc(p_ready, 1)
                for hh in range(2):
                    act.wait_ge(wexp_in, b * 2 + hh + 1)
                    nc.scalar.activation(sp_z[hh], e_z[hh], ACT.Exp).then_inc(wexp_out, 1)
                dst, width = (r5, 2 * BANK) if kind == "cols" else (mv, BANK)
                i = b if kind == "cols" else b - BODIES // 2
                take(kind, dst, i * 2 * width, b + MKV0, 0, 0)
                act.wait_ge(o_ready, b + 1)
                for c in range(4):
                    m = nc.scalar.activation(sb_n[:, c, :], ps[:, 7, c * P:(c + 1) * P], ACT.Square,
                                             accum_out=ss[:, c:c + 1])
                m.then_inc(ss_ready, 1)
                for hh in range(2):
                    act.wait_ge(pT_ready, b * 2 + hh + 1)
                    nc.scalar.activation(pT[hh], ps[:, 4 + hh, 0:ZC], ACT.Copy).then_inc(pT_copied, 1)
                act.wait_ge(do_ready, b + 1)
                for c in range(4):
                    m = nc.scalar.activation(s_t1[c // 2][:, 1, (c % 2) * P:(c % 2 + 1) * P], ps[:, 6, c * P:(c + 1) * P], ACT.Square,
                                             accum_out=dss[:, c:c + 1])
                m.then_inc(ss_ready, 1)
                act.wait_ge(oT_ready, b * 2 + 1)
                nc.scalar.activation(r0[:, bass.ds(b * 2 * T, 2 * T)], ps[:, 2, :], ACT.Copy).then_inc(oT_copied, 1)
                take(kind, dst, i * 2 * width + width, b + MKV0, 1, 0)
                act.wait_ge(oT_ready, b * 2 + 2)
                nc.scalar.activation(r0[:, bass.ds(b * 2 * T + SBH * T, 2 * T)], ps[:, 7, :],
                                     ACT.Copy).then_inc(oT_copied, 1)

            act.preload_act_table_set("natural_log_exp_and_others")
            for first, kind in ((0, "cols"), (BODIES // 2, "rows")):
                with act.Fori(first, first + BODIES // 2) as b:
                    steps.enter(b - first if first else b, 6)
                    attention_body(b, kind)
                steps.leave(BODIES // 2)

            copy_turned(r4, 16)
            section("cols", r0, MQ0, NP // 2, 2 * BANK)
            for h in range(MH):
                act.wait_ge(cmax_ready, h + 1)
                for t in range(NT):
                    n = 2 * h + t
                    m = nc.scalar.activation(c_p[:, h, t, :], ps[:, 4 + h, t * T:(t + 1) * T], ACT.Exp,
                                             bias=nmx[:, n:n + 1], scale=M_SCALE, accum_out=dsum[:, n:n + 1])
                m.then_inc(cp_ready, 1)
            for h in range(MH):
                act.wait_ge(cT_ready, h + 1)
                nc.scalar.activation(c_pT[:, h, :, :], ps[:, h, :].rearrange("p (m q) -> p m q", m=NT),
                                     ACT.Copy).then_inc(cT_copied, 1)
            for g in range(KB // 2):
                act.wait_ge(co_ready, g + 1)
                nc.scalar.activation(r1[:, g * 2 * T:(g + 1) * 2 * T], ps[:, 4 + g % 4, :], ACT.Copy)\
                    .then_inc(co_copied, 1)
            act.wait_ge(keysT_ready, 1)
            nc.scalar.activation(keysT[:, :], ps[:, 7, 0:2 * NKEY], ACT.Copy).then_inc(keysT_copied, 1)
            copy_turned(r4, 24)
            with act.Fori(0, NP // 2) as i:
                def take_scores(s):
                    act.wait_ge(ks_ready, i * 2 + s + 1)
                    nc.scalar.activation(key_scores[:, :, bass.ds((i * 2 + s) * BANK, BANK)],
                                         ps[:, 4 + 2 * s:6 + 2 * s, :], ACT.Copy).then_inc(ks_copied, 1)

                def take_queries(s):
                    act.wait_ge(w_used[2 * s + 1], i + (PQ0 + 1))
                    if s == 0:
                        act.wait_ge(ks_copied, i * 2 + CREDIT)
                    nc.scalar.activation(pq_st[s].rearrange("p b t -> p (b t)"), bank(2 * s, 2),
                                         ACT.Copy).then_inc(proj_taken, 1)
                take_queries(0)
                take_scores(0)
                take_queries(1)
                take_scores(1)

            def gates(n):
                act.wait_ge(top_ready, n + 1)
                t = 0
                nc.scalar.activation(top, top, ACT.Exp, bias=ntop, accum_out=gsum).then_inc(gexp_ready, 1)

            for t in range(NT):
                gates(t)

            def peer_body(h, last):
                for t in range(NT):
                    unit = h * NT + t
                    act.wait_ge(h_ready, unit + 1)
                    nc.scalar.activation(act_h[t], hdot[t], ACT.Gelu).then_inc(gelu_ready, 1)
                    if not last:
                        gates(unit + NT)
                    act.wait_ge(a_ready, unit + 1)
                    for j in range(TOPK):
                        act.wait_ge(v_used, unit * TOPK + (j + 1 + RING_CREDIT - TOPK))
                        nc.scalar.activation(diag[:, j, :], ident[:, :], ACT.Copy,
                                             scale=weight[t][:, j:j + 1]).then_inc(diag_ready, 1)

            with act.Fori(0, PH - 1) as h:
                peer_body(h, False)
            peer_body(PH - 1, True)

        @block.gpsimd
        def _(pool):
            steps = Steps(pool, pool_step)
            pool.sem_inc(o_normed, CREDIT)
            for dst, v in ((ident, 0.0), (before, 1.0), (neg_after, -1.0), (neg_ones, -1.0), (causal, 0.0)):
                steps.did(pool.memset(dst[:, :], v))
            steps.did(pool.memset(nhalf, -0.5))
            steps.wait()
            steps.did(pool.affine_select(out=ident[:, :], in_=ident[:, :], compare_op=ALU.not_equal, fill=1.0,
                                         base=0, pattern=[[-1, P]], channel_multiplier=1))
            steps.did(pool.affine_select(out=before[:, :], in_=before[:, :], compare_op=ALU.is_gt, fill=0.0,
                                         base=0, pattern=[[1, P]], channel_multiplier=-1))
            steps.did(pool.affine_select(out=neg_after[:, :], in_=neg_after[:, :], compare_op=ALU.is_gt, fill=0.0,
                                         base=0, pattern=[[-1, P]], channel_multiplier=1))
            steps.did(pool.affine_select(out=causal[:, P:T], in_=causal[:, P:T], compare_op=ALU.is_ge,
                                         fill=NEG_BIG, base=0, pattern=[[-1, P]], channel_multiplier=1))
            steps.did(pool.iota(iota[:, :], pattern=[[1, TOPK]], base=0, channel_multiplier=0,
                                allow_small_or_imprecise_dtypes=True))
            steps.wait()
            pool.sem_inc(consts_ready, 1)

            def power(src, dst, nth):
                pool.wait_ge(ms_ready, nth)
                nc.gpsimd.tensor_tensor(dst, src, nhalf, ALU.pow).then_inc(rms_ready, 1)

            def attention_body(b):
                pool.wait_ge(z_ready, b * 2 + 2)
                pool.wait_ge(dfT_ready, b * 2 + 2)
                stage(b + 1)
                powers(b)

            def stage(b):
                nc.gpsimd.tensor_copy(k_st, r1[:, bass.ds(b * 2 * T + SBH * T, 2 * T)]).then_inc(k_staged, 1)
                src = df_qk.rearrange("p t (q c) -> p t q c", q=2)[:, :, :, bass.ds(b * 2 * P, 2 * P)]
                for t in range(NT):
                    m = nc.gpsimd.tensor_copy(df_st[:, t], src[:, t])
                m.then_inc(df_staged, 1)

            def powers(b):
                power(ss, rs, b * 2 + 1)
                power(dss, drs, b * 2 + 2)

            pool.wait_ge(proj_taken, 2 * MKV0 + CREDIT)
            pool.wait_ge(roped, 3)
            stage(0)
            with pool.Fori(0, BODIES - 1) as b:
                attention_body(b)
            powers(BODIES - 1)
            pool.wait_ge(z_ready, 2 * BODIES)
            pool.dma_start(z1, x_rows).then_inc(z_landed, 16)
            pool.wait_ge(dfT_ready, 2 * BODIES)
            for n, (g, b) in enumerate(((ln1_g, ln1_b), (ln2_g, ln2_b), (ln3_g, ln3_b))):
                if n:
                    pool.wait_ge(x_ready, 4 * n)
                pool.dma_start(gain_b, g[0].partition_broadcast(P)).then_inc(gb_landed, 16)
                pool.dma_start(bias_b, b[0].partition_broadcast(P)).then_inc(gb_landed, 16)
                if n == 2:
                    break
                pool.wait_ge(var_ready, n + 1)
                nc.gpsimd.tensor_tensor(rstd, veps, nhalf[:, 0:NT], ALU.pow).then_inc(rstd_ready, 1)
                if n == 0:
                    pool.wait_ge(cT_ready, MH)
                    pool.dma_start(keys_in.rearrange("p (s d) -> p s d", s=2),
                                   sub_keys[0].rearrange("s n d -> n s d")).then_inc(keys_landed, 16)
            pool.wait_ge(keysT_copied, 1)
            pool.wait_ge(ks_copied, CREDIT + 1)
            pool.memset(diag[:, 0, :], 0.0).then_inc(consts_ready, 1)

            def gather(table, ring_slots, landed, t, j, **kw):
                pool.indirect_dma_start(ring_slots[j % len(ring_slots)], None, table,
                                        bass.IndirectOffsetOnAxis(ap=idx[t][:, j:j + 1], axis=0), **kw).then_inc(landed[j % len(ring_slots)], 16)

            def gather_u(unit, t, j, waits=True):
                if waits:
                    pool.wait_ge(u_used, unit * TOPK + (j + 1 - NU))
                    pool.sem_inc(slots_freed, 1)
                gather(peer_u[0], u_ring, u_landed, t, j)

            def gather_v(unit, t, j):
                pool.wait_ge(v_used, unit * TOPK + (j + 1 - NV + RING_CREDIT))
                pool.sem_inc(slots_freed, 1)
                gather(peer_v[0], v_ring, v_landed, t, j, **({"engine_sem": v_issued} if j == TOPK - 1 else {}))

            def peer_body(h, last):
                for t in range(NT):
                    unit = h * NT + t
                    follow = not (last and t == NT - 1)
                    for j in range(TOPK + 2):
                        if j < TOPK:
                            gather_v(unit, t, j)
                        if j >= 2 and follow:
                            if j == 2:
                                pool.wait_ge(idx_ready, unit + 2)
                                pool.sem_inc(slots_freed, 1)
                            gather_u(unit + 1, (t + 1) % NT, j - 2)

            pool.wait_ge(idx_ready, 1)
            for j in range(TOPK):
                gather_u(0, 0, j, waits=j >= NU)
            with pool.Fori(0, PH - 1) as h:
                peer_body(h, False)
            peer_body(PH - 1, True)
            pool.wait_ge(var_ready, 3)
            nc.gpsimd.tensor_tensor(rstd, veps, nhalf[:, 0:NT], ALU.pow).then_inc(rstd_ready, 1)

        @block.vector
        def _(dve):
            steps = Steps(dve, dve_step)

            def chain(ins):
                steps.did(ins)
                steps.wait()

            dve.wait_ge(small_landed, 64)
            for n in range(2):
                steps.did(nc.vector.tensor_tensor(lam_pr, lam_in[:, 2 * n * QD:(2 * n + 1) * QD],
                                                  lam_in[:, (2 * n + 1) * QD:(2 * n + 2) * QD], ALU.mult))
                steps.wait()
                steps.did(nc.vector.tensor_reduce(lam_s[:, n:n + 1], lam_pr, AX_X, ALU.add))
                steps.wait()
            dve.sem_inc(roped, 1)
            steps.did(nc.vector.tensor_scalar(dfg[:, :], dfg[:, :], 1.0 - LAMBDA_INIT, None, ALU.mult))
            dve.wait_ge(roped, 2)
            chain(nc.vector.tensor_tensor(neg_lam, lam_e[:, 1:2], lam_e[:, 0:1], ALU.subtract))
            steps.did(nc.vector.tensor_scalar(neg_lam, neg_lam, -LAMBDA_INIT, None, ALU.add))

            dve.wait_ge(proj_taken, 10 + CREDIT)
            heads = 2 * SBW // QD
            both = ta[:, 0:heads * ROT].rearrange("p (h c) -> p h c", h=heads)
            cross = ta[:, heads * ROT:2 * heads * ROT].rearrange("p (h c) -> p h c", h=heads)
            for t in range(NT):
                part = df_qk[:, t].rearrange("p (h c) -> p h c", c=QD)[:, :, 0:ROT]
                cos_t = cos2[:, t:t + 1, :].to_broadcast([P, heads, ROT])
                sin_t = sin2[:, t:t + 1, :].to_broadcast([P, heads, ROT])
                steps.did(nc.vector.tensor_tensor(both, part, cos_t, ALU.mult))
                steps.did(nc.vector.tensor_tensor(cross[:, :, 0:HR], part[:, :, HR:ROT], sin_t[:, :, 0:HR], ALU.mult))
                steps.did(nc.vector.tensor_tensor(cross[:, :, HR:ROT], part[:, :, 0:HR], sin_t[:, :, HR:ROT], ALU.mult))
                steps.wait()
                steps.did(nc.vector.tensor_tensor(part, both, cross, ALU.add))
                steps.wait()
            dve.sem_inc(roped, 1)

            diag_of = lambda a: a.rearrange("p (b c) -> p b c", b=3)[:, 0:3:2, :]
            before2 = before[:, :].unsqueeze(1).to_broadcast([P, 2, P])
            def rms_norm(b, nth, src_bank, sums, root, gain_of, dst):
                dve.wait_ge(ss_ready, nth)
                nc.vector.tensor_scalar(sums, sums, 1.0 / DH, RMS_EPS, ALU.mult, ALU.add).then_inc(ms_ready, 1)
                dve.wait_ge(rms_ready, nth)
                for c in range(4):
                    m = nc.vector.scalar_tensor_tensor(out=dst[:, c, :], in0=ps[:, src_bank, c * P:(c + 1) * P],
                                                       scalar=root[:, c:c + 1], in1=gain_of(c // 2),
                                                       op0=ALU.mult, op1=ALU.mult)
                m.then_inc(o_normed, 1)

            def attention_body(b):
                for hh in range(2):
                    dve.wait_ge(e_ready, b * 2 + hh + 1)
                    chain(nc.vector.scalar_tensor_tensor(out=sp_z[hh], in0=e_z[hh], scalar=0.0, in1=sp_z[hh],
                                                         op0=ALU.max, op1=ALU.add))
                    chain(nc.vector.tensor_tensor(e_z[hh], e_z[hh], sp_z[hh], ALU.subtract))
                    nc.vector.tensor_tensor(diag_of(sp_z[hh]), diag_of(sp_z[hh]), before2, ALU.mult)\
                        .then_inc(sp_ready, 1)
                dve.wait_ge(s_ready, b + 1)
                for st in range(2):
                    steps.did(nc.vector.tensor_tensor(s_t0[:, st:4:2, :], ps[:, 6 + st, 0:T].rearrange("p (h c) -> p h c", h=2),
                                                      causal[:, P:T].unsqueeze(1).to_broadcast([P, 2, P]), ALU.add))
                for hh in range(2):
                    steps.did(nc.vector.tensor_tensor(s_t1[hh], ps[:, 4:6, hh * T:(hh + 1) * T],
                                                      causal[:, :].unsqueeze(1).to_broadcast([P, 2, T]), ALU.add))
                steps.wait()
                steps.did(nc.vector.tensor_reduce(mx[:, 0:4], s_t0, AX_X, ALU.max))
                for hh in range(2):
                    steps.did(nc.vector.tensor_reduce(mx[:, 4 + 2 * hh:6 + 2 * hh], s_t1[hh], AX_X, ALU.max))
                steps.wait()
                nc.vector.tensor_scalar(nmx, mx, -DF_SCALE, None, ALU.mult).then_inc(smax_ready, 1)
                for hh in range(2):
                    dve.wait_ge(stick_ready, b * 2 + hh + 1)
                    nc.vector.tensor_tensor(e_z[hh], e_z[hh], ps[:, 2 + hh, 0:ZC], ALU.add).then_inc(wexp_in, 1)
                for hh in range(2):
                    dve.wait_ge(wexp_out, b * 2 + hh + 1)
                    nc.vector.tensor_tensor(diag_of(sp_z[hh]), diag_of(sp_z[hh]), before2, ALU.mult)\
                        .then_inc(w_ready, 1)
                dve.wait_ge(p_ready, b + 1)
                chain(nc.vector.reciprocal(rsum, dsum))
                chain(nc.vector.tensor_scalar(c2, rsum, neg_lam, None, ALU.mult))
                for hh in range(2):
                    p2 = (s_t0[:, 2 * hh + 1, :], s_t1[hh][:, 1, :])
                    p1 = (s_t0[:, 2 * hh, :], s_t1[hh][:, 0, :])
                    for n in range(2):
                        c = 4 * n + 2 * hh
                        steps.did(nc.vector.tensor_scalar(p2[n], p2[n], c2[:, c + 1:c + 2], None, ALU.mult))
                    steps.wait()
                    for n in range(2):
                        c = 4 * n + 2 * hh
                        m = nc.vector.scalar_tensor_tensor(out=p1[n], in0=p1[n], scalar=rsum[:, c:c + 1], in1=p2[n],
                                                           op0=ALU.mult, op1=ALU.add)
                    m.then_inc(pw_ready, 1)
                rms_norm(b, b * 2 + 1, 7, ss, rs, lambda hh: sbg[:, bass.ds((b * 2 + hh) * DH, DH)], sb_n)
                rms_norm(b, b * 2 + 2, 6, dss, drs, lambda hh: dfg[:, :], df_n)

            with dve.Fori(0, BODIES) as b:
                steps.enter(b, 17)
                attention_body(b)
            steps.leave(BODIES)

            def residual(z, x_old, first_pair):
                with dve.Fori(0, NP // 2) as i:
                    steps.enter(i, 2)
                    for s in range(2):
                        q = i * 2 + s
                        cols = bass.ds(q * BANK, BANK)
                        dve.wait_ge(w_used[2 * s + 1], i + (first_pair + 1))
                        nc.vector.scalar_tensor_tensor(out=z[:, :, cols], in0=x_old[:, :, cols], scalar=ALPHA,
                                                       in1=ps[:, 2 * s:2 * s + 2, :], op0=ALU.mult,
                                                       op1=ALU.add).then_inc(proj_taken, 1)
                        dve.wait_ge(proj_taken, i * 2 + (2 * first_pair + s + 1 + CREDIT))
                        for t in range(NT):
                            m = nc.vector.bn_stats(small[:, bass.ds(q * 6 + (65 + t * NP * 6), 6)], z[:, t, cols])
                        steps.did(m)
                steps.leave(NP // 2)

            def norm(z, dst, nth, done):
                steps.wait()
                for t in range(NT):
                    steps.did(nc.vector.bn_aggr(mvar[:, t, :], stats[:, t].rearrange("p q c -> p (q c)")))
                steps.wait()
                nc.vector.tensor_scalar(veps, mvar[:, :, 1], LN_EPS, None, ALU.add).then_inc(var_ready, 1)
                dve.wait_ge(gb_landed, 32 * nth + 32)
                dve.wait_ge(rstd_ready, nth + 1)
                done(z, dst)

            def by_chunks(z, dst):
                for q in range(NP):
                    cols = slice(q * BANK, (q + 1) * BANK)
                    for t in range(NT):
                        steps.did(nc.vector.scalar_tensor_tensor(out=dst[:, t, cols], in0=z[:, t, cols],
                                                                 scalar=mvar[:, t, 0:1], in1=gain_b[:, cols],
                                                                 op0=ALU.subtract, op1=ALU.mult))
                    steps.wait()
                    for t in range(NT):
                        m = nc.vector.scalar_tensor_tensor(out=dst[:, t, cols], in0=dst[:, t, cols],
                                                           scalar=rstd[:, t:t + 1], in1=bias_b[:, cols],
                                                           op0=ALU.mult, op1=ALU.add)
                    m.then_inc(x_ready, 1)

            dve.wait_ge(z_landed, 16)
            residual(z1, z1, WO0)
            norm(z1, x1, 0, by_chunks)

            for h in range(MH):
                dve.wait_ge(cs_ready, h + 1)
                chain(nc.vector.tensor_reduce(mx[:, 2 * h:2 * h + 2], ps[:, 4 + h, :].rearrange("p (t m) -> p t m", t=NT),
                                              AX_X, ALU.max))
                nc.vector.tensor_scalar(nmx[:, 2 * h:2 * h + 2], mx[:, 2 * h:2 * h + 2], -M_SCALE, None,
                                        ALU.mult).then_inc(cmax_ready, 1)
            for h in range(MH):
                dve.wait_ge(cp_ready, h + 1)
                chain(nc.vector.reciprocal(rsum[:, 2 * h:2 * h + 2], dsum[:, 2 * h:2 * h + 2]))
                for t in range(NT):
                    m = nc.vector.tensor_scalar(c_p[:, h, t, :], c_p[:, h, t, :], rsum[:, 2 * h + t:2 * h + t + 1], None,
                                                ALU.mult)
                m.then_inc(cn_ready, 1)
            residual(x1, x1, MO0)
            norm(x1, x2, 1, by_chunks)

            def ordered(ins):
                dve.drain()

            def copy_scores(t, h):
                ordered(nc.vector.tensor_copy(sc, key_scores[:, t, bass.ds(h * 2 * NKEY, 2 * NKEY)]))

            def top16(values, left, best, where):
                ordered(nc.vector.max(best[:, 0:8], values))
                (nc.vector.max_index(where[:, 0:8], best[:, 0:8], values))
                ordered(nc.vector.match_replace(left, best[:, 0:8], values, NEG_MAX))
                ordered(nc.vector.max(best[:, 8:16], left))
                ordered(nc.vector.max_index(where[:, 8:16], best[:, 8:16], left))

            def retrieve(unit, t, h):
                copy_scores(t, h)
                for n in range(2):
                    c = slice(n * NKEY, (n + 1) * NKEY)
                    top16(sc[:, c], sc_left[:, c], val[:, 16 * n:16 * n + 16], ix[:, 16 * n:16 * n + 16])
                (nc.vector.tensor_copy(ixf, ix))
                grid = lambda a: a.rearrange("p (i j) -> p i j", i=TOPK)
                ordered(nc.vector.tensor_tensor(grid(cand), val[:, 0:16].unsqueeze(2).to_broadcast([P, TOPK, TOPK]),
                                              val[:, 16:32].unsqueeze(1).to_broadcast([P, TOPK, TOPK]), ALU.add))
                top16(cand, cand_left, top, pos)
                nc.vector.tensor_scalar(ntop, top[:, 0:1], -1.0, None, ALU.mult).then_inc(top_ready, 1)
                (nc.vector.tensor_scalar(ij[:, 0:16], pos, 4, None, ALU.logical_shift_right))
                ordered(nc.vector.tensor_scalar(ij[:, 16:32], pos, 15, None, ALU.bitwise_and))
                ordered(nc.vector.tensor_copy(ijf, ij))
                for n in range(2):
                    ordered(nc.vector.tensor_tensor(grid(hot), ijf[:, 16 * n:16 * n + 16].unsqueeze(2).to_broadcast([P, TOPK, TOPK]),
                                                  iota[:, :].unsqueeze(1).to_broadcast([P, TOPK, TOPK]), ALU.is_equal))
                    ordered(nc.vector.tensor_tensor(grid(hot_v), grid(hot),
                                                  ixf[:, 16 * n:16 * n + 16].unsqueeze(1).to_broadcast([P, TOPK, TOPK]),
                                                  ALU.mult))
                    ordered(nc.vector.tensor_reduce(picked[:, 16 * n:16 * n + 16], grid(hot_v), AX_X, ALU.add))
                (nc.vector.scalar_tensor_tensor(out=next_idx[t], in0=picked[:, 0:16], scalar=float(NKEY),
                                                         in1=picked[:, 16:32], op0=ALU.mult, op1=ALU.add))
                dve.wait_ge(gexp_ready, unit + 1)
                ordered(nc.vector.reciprocal(gsum, gsum))
                ordered(nc.vector.tensor_scalar(gate[t], top, gsum, None, ALU.mult))

            def hand_over(t):
                nc.vector.tensor_copy(idx[t], next_idx[t]).then_inc(idx_ready, 1)

            def peer_body(h, last):
                for t in range(NT):
                    unit = h * NT + t
                    for j in range(TOPK):
                        dve.wait_ge(u_landed[j % NU], (unit * 2 + j // NU) * 16 + 16)
                        m = nc.vector.tensor_tensor_reduce(u_ring[j % NU], u_ring[j % NU], x2[:, t, :], 1.0, 0.0,
                                                           ALU.mult, ALU.add, hdot[t][:, j:j + 1])
                        m.then_inc(u_used, 1)
                    dve.wait_ge(u_used, unit * TOPK + TOPK)
                    dve.sem_inc(h_ready, 1)
                    if not (last and t == NT - 1):
                        if not isinstance(unit, int) or unit > 0:
                            dve.wait_ge(v_issued, unit)
                        hand_over(NT - 1 - t)
                    dve.wait_ge(gelu_ready, unit + 1)
                    nc.vector.tensor_tensor(weight[t], act_h[t], gate[t], ALU.mult).then_inc(a_ready, 1)
                    if not last:
                        dve.wait_ge(a_ready, unit + 1)
                        retrieve(unit + NT, t, h + 1)

            dve.wait_ge(ks_copied, NP + CREDIT)
            for t in range(NT):
                retrieve(t, t, 0)
                if t == 0:
                    hand_over(0)
            peer_body(0, False)
            with dve.Fori(1, PH - 1) as h:
                peer_body(h, False)
            peer_body(PH - 1, True)
            dve.wait_ge(v_used, PH * NT * TOPK + RING_CREDIT)
            for t in range(NT):
                chain(nc.vector.scalar_tensor_tensor(out=x2[:, t, :], in0=x2[:, t, :], scalar=ALPHA,
                                                     in1=bank(4 * t, 4), op0=ALU.mult, op1=ALU.add))
                for q in range(NP):
                    steps.did(nc.vector.bn_stats(stats[:, t, q, :], x2[:, t, q * BANK:(q + 1) * BANK]))

            def by_tiles(z, dst):
                for t in range(NT):
                    chain(nc.vector.scalar_tensor_tensor(out=dst[:, t, :], in0=z[:, t, :], scalar=mvar[:, t, 0:1],
                                                         in1=gain_b, op0=ALU.subtract, op1=ALU.mult))
                    nc.vector.scalar_tensor_tensor(out=dst[:, t, :], in0=dst[:, t, :], scalar=rstd[:, t:t + 1],
                                                   in1=bias_b, op0=ALU.mult, op1=ALU.add).then_inc(y_ready, 1)

            norm(x2, y_out, 2, by_tiles)


_INS = ["x", "mem", "w_in", "sb_norm_gain", "df_lambda", "df_subln_gain", "w_o", "ln1_gain", "ln1_bias",
        "w_mq", "w_mkv", "w_mo", "ln2_gain", "ln2_bias", "w_pq", "peer_sub_keys", "peer_u", "peer_v",
        "ln3_gain", "ln3_bias"]


def rope_table(tokens, rot):
    import numpy as np

    half = rot // 2
    freq = np.power(np.float32(ROPE_THETA), -np.arange(half, dtype=np.float32) * np.float32(2.0) / np.float32(rot))
    ang = np.arange(tokens, dtype=np.float32)[:, None] * freq.astype(np.float32)[None, :]
    cos, sin = np.cos(ang), np.sin(ang)
    return np.concatenate([cos, cos, -sin, sin], axis=1).astype(np.float32)


def kernel(**inputs):
    import numpy as np
    import concourse.bacc as bacc
    from concourse.bass_utils import run_bass_kernel_spmd as run

    nc = bacc.Bacc("TRN2", target_bir_lowering=False, num_devices=1)
    arrays = {f"in_{n}_dram": np.ascontiguousarray(inputs[n]) for n in _INS}
    _, tokens, width = inputs["x"].shape
    arrays["rope_dram"] = rope_table(tokens, inputs["df_lambda"].shape[2] // 4)
    args = [nc.dram_tensor(n, a.shape, mybir.dt.from_np(a.dtype), kind="ExternalInput").ap()
            for n, a in arrays.items()]
    out = nc.dram_tensor("out_dram", (1, tokens, width), F32, kind="ExternalOutput").ap()
    layer_program(nc, *args, out)
    return run(nc, [arrays], core_ids=[0]).results[0]["out_dram"]
```

```python
import math
from contextlib import ExitStack

import concourse.bass as bass
from concourse import mybir

F32 = mybir.dt.float32
F32R = mybir.dt.float32r
U32 = mybir.dt.uint32
ALU = mybir.AluOpType
ACT = mybir.ActivationFunctionType
AX_X = mybir.AxisListType.X

P = 128
BANK = 512
NEG_BIG = -1.0e30
NEG_MAX = -3.0e38
ROPE_THETA = 500000.0
LAMBDA_INIT = 0.8 - 0.6 * math.exp(-0.3 * 0)
LN_EPS, RMS_EPS = 1e-5, 1e-6
ALPHA = 2.0 ** 0.25


class Steps:

    def __init__(self, eng, sem):
        self.eng, self.sem, self.base, self.n = eng, sem, 0, 0

    def did(self, ins):
        ins.then_inc(self.sem, 1)
        self.n += 1

    def wait(self, but=0):
        self.eng.wait_ge(self.sem, self.base + self.n - but)

    def enter(self, i, per):
        self.start, self.per = self.base + self.n, per
        self.base, self.n = self.start + i * per, 0

    def leave(self, times):
        assert self.n == self.per, (self.n, self.per)
        self.base, self.n = self.start + times * self.per, 0


def layer_program(nc, x, mem, w_in, sb_gain, df_lambda, df_gain, w_o, ln1_g, ln1_b, w_mq, w_mkv,
                  w_mo, ln2_g, ln2_b, w_pq, sub_keys, peer_u, peer_v, ln3_g, ln3_b, rope, out):
    D = x.shape[2]
    NT = x.shape[1] // P
    T = NT * P
    KB = D // P
    SK = 2
    NS = KB // SK
    NP = D // BANK
    SBH, DH = sb_gain.shape[1], sb_gain.shape[2]
    SBW = SBH * DH
    QD = df_lambda.shape[2]
    ROT = rope.shape[1] // 2
    PH = w_pq.shape[2] // (2 * P)
    NKEY = sub_keys.shape[2]
    TOPK = 16
    MH = 4
    MB = KB // MH
    SB_SCALE, DF_SCALE, M_SCALE = DH ** -0.5, QD ** -0.5, (D // MH) ** -0.5
    assert (P, T, KB, NP) == (DH, 2 * P, 16, 4) and NKEY == P and PH == SBH == 8

    x_rows = x[0].rearrange("(t p) n -> p t n", p=P)
    mem_rows = mem[0].rearrange("(t p) n -> p t n", p=P)
    out_rows = out[0].rearrange("(t p) n -> p t n", p=P)

    with ExitStack() as ctx:
        def sb(name, cols, dt=F32):
            return ctx.enter_context(nc.sbuf_tensor(name, [P, cols], dt))

        def sem(name):
            return ctx.enter_context(nc.semaphore(name))

        RC = NT * D
        RAW, SPLIT = 8, 4
        SC = SK * BANK
        base = -(-nc.sbuf_base // 32) * 32
        arena = sb("arena", 7 * RC + (RAW + 2 * SPLIT) * SC)

        def at(name, col, cols, dt=F32):
            return nc.alloc_sbuf_tensor_at(name, [P, cols], dt, offset=base + 4 * col)

        r0, r1, r2, r3, r4, r5, r6 = [at(f"region{n}", n * RC, RC) for n in range(7)]
        p0, p1, p3, p4 = [at(f"parts{n}", n * RC, RC, F32R) for n in (0, 1, 3, 4)]
        ring = at("weight_ring", 7 * RC, (RAW + 2 * SPLIT) * SC)
        split_ring = at("split_ring", 7 * RC + RAW * SC, 2 * SPLIT * SC, F32R)

        def blocks(r):
            return r[:, :].rearrange("p (k t) -> p k t", k=KB)

        def rows(r):
            return r[:, :].rearrange("p (t n) -> p t n", t=NT)

        def parts(hi, lo):
            return [[r[:, k * T:(k + 1) * T] for k in range(KB)] for r in (hi, lo)]

        def mixed_rest(k):
            kind, b, hh = k // SBH, k % SBH // 2, k % 2
            c = kind * D + hh * SBW + b * T
            return p3[:, c:c + T]

        xT = memT = parts(p0, p4)
        mixedT = [parts(p1, p3)[0], [mixed_rest(k) for k in range(KB)]]
        x1T = coT = x2T = parts(p1, p3)
        mixed_lo = p3[:, :].rearrange("p (m h n) -> p m h n", m=2, h=2)
        cqT = blocks(r0)
        sb_v, df_v = rows(r2)[:, :, 0:SBW], rows(r2)[:, :, SBW:D]
        z1 = rows(r0)
        x1 = rows(r2)
        df_qk = rows(r3)
        gain_b, bias_b = r4[:, 0:D], r4[:, D:2 * D]
        x_in, mkT, x2 = rows(r5), blocks(r5), rows(r5)
        mem_in, mv, key_scores = rows(r6), rows(r6), rows(r6)

        def slots(r, n, first=0):
            return [r[:, (first + s) * SC:(first + s + 1) * SC] for s in range(n)]

        raw, w_hi, w_lo = slots(ring, RAW), slots(split_ring, SPLIT), slots(split_ring, SPLIT, SPLIT)
        halves = lambda r: [r[:, 0:D], r[:, D:2 * D]]
        in_ring = [ring[:, s * D:(s + 1) * D] for s in range(8)]
        u_ring = halves(r0) + halves(r2) + halves(r4) + in_ring[0:2]
        gain3_b, bias3_b = in_ring[2:4]
        v_ring = halves(r1) + halves(r3) + in_ring[4:8]
        NU = NV = 8
        EARLY = 6
        u_extra = [len(range(s, TOPK, EARLY)) * (s < EARLY) - TOPK // NU for s in range(NU)]
        y_out = rows(r0)

        ident = sb("ident", P)
        before = sb("before", P)
        neg_after = sb("neg_after", P)
        neg_ones = sb("neg_ones", P)
        causal = sb("causal", T)
        rope_cs = sb("rope_cs", NT * 2 * ROT)
        sbg = sb("sbg", SBW)
        dfg = sb("dfg", DH)
        keysT = sb("keysT", 2 * NKEY)
        iota = sb("iota", TOPK)
        small = sb("small", 128)
        ta = sb("temps", 5632)

        cos2 = rope_cs[:, :].rearrange("p (t c) -> p t c", t=NT)[:, :, 0:ROT]
        sin2 = rope_cs[:, :].rearrange("p (t c) -> p t c", t=NT)[:, :, ROT:2 * ROT]
        HR = ROT // 2
        k_st = ta[:, 0:512]
        df_st = ta[:, 512:1536].rearrange("p (t q c) -> p t q c", t=NT, q=2)
        ZC = 3 * P
        e_z = [ta[:, 1536 + n * ZC:1536 + (n + 1) * ZC] for n in range(2)]
        sp_z = [ta[:, 2304 + n * ZC:2304 + (n + 1) * ZC] for n in range(2)]
        sb_n = ta[:, 1536:2048].rearrange("p (b c) -> p b c", b=4)
        dfT = [ta[:, 3072 + n * 512:3584 + n * 512] for n in range(2)]
        pT = [ta[:, 3072 + n * 512:3072 + n * 512 + ZC] for n in range(2)]
        s_t0 = ta[:, 4096:4608].rearrange("p (b c) -> p b c", b=4)
        df_n = ta[:, 4096:4608].rearrange("p (b c) -> p b c", b=4)
        s_t1 = [ta[:, 4608 + n * 512:5120 + n * 512].rearrange("p (s c) -> p s c", s=2) for n in range(2)]
        c_p = ta[:, 0:MH * NT * T].rearrange("p (h t m) -> p h t m", h=MH, t=NT)
        c_pT = ta[:, 2048:4096].rearrange("p (h m q) -> p h m q", h=MH, m=NT)
        pq_st = [ta[:, s * 1024:1024 + s * 1024].rearrange("p (b t) -> p b t", b=4) for s in range(2)]
        keys_in = ta[:, 0:2 * NKEY]
        diag = ta[:, 0:TOPK * P].rearrange("p (j c) -> p j c", j=TOPK)
        tk = ta[:, 2048:5632]
        sc, sc_left = tk[:, 0:256], tk[:, 256:512]
        cand, cand_left = tk[:, 512:768], tk[:, 768:1024]
        hot, hot_v = tk[:, 1024:1280], tk[:, 1280:1536]
        val = tk[:, 1536:1568]
        ixf = tk[:, 1568:1600]
        top = tk[:, 1600:1616]
        ijf = tk[:, 1616:1648]
        picked = tk[:, 1648:1680]
        gate = [tk[:, 1680 + 16 * t:1696 + 16 * t] for t in range(NT)]
        hdot = [tk[:, 1712 + 16 * t:1728 + 16 * t] for t in range(NT)]
        act_h = [tk[:, 1744 + 16 * t:1760 + 16 * t] for t in range(NT)]
        weight = [tk[:, 1776 + 16 * t:1792 + 16 * t] for t in range(NT)]
        gsum, ntop = tk[:, 1808:1809], tk[:, 1809:1810]
        ints = tk[:, 1856:2048].bitcast(U32)
        ix, pos, ij = ints[:, 0:32], ints[:, 32:48], ints[:, 48:80]
        next_idx = [ints[:, 80 + 16 * t:96 + 16 * t] for t in range(NT)]
        idx_all = ints[:, 112:144]
        idx = [idx_all[:, 16 * t:16 * t + 16] for t in range(NT)]

        lam_in = ta[:, 0:4 * QD]
        lam_pr = ta[:, 4 * QD:5 * QD]
        neg_lam = small[:, 0:1]
        lam_s = small[:, 1:3]
        lam_e = small[:, 3:5]
        nhalf = small[:, 5:9]
        ss, rs = small[:, 9:13], small[:, 13:17]
        dss, drs = small[:, 17:21], small[:, 21:25]
        mx, nmx, dsum, rsum, c2 = [small[:, 25 + 8 * n:33 + 8 * n] for n in range(5)]
        stats = small[:, 65:113].rearrange("p (t q c) -> p t q c", t=NT, c=6)
        mvar = small[:, 113:117].rearrange("p (t c) -> p t c", t=NT)
        veps, rstd = small[:, 117:119], small[:, 119:121]

        ps = ctx.enter_context(nc.psum_tensor("ps", [P, 8, BANK], F32))

        def bank(b, n=1):
            return ps[:, b:b + n, :].rearrange("p b c -> p (b c)")

        x_landed = [sem(f"x_landed{q}") for q in range(NP)]
        mem_landed, small_landed = sem("mem_landed"), sem("small_landed")
        w_landed = [sem(f"w_landed{s}") for s in range(RAW)]
        hi_ready, lo_ready, w_used = sem("hi_ready"), sem("lo_ready"), sem("w_used")
        pool_step, dve_step, act_step = sem("pool_step"), sem("dve_step"), sem("act_step")
        consts_ready = sem("consts_ready")
        turned, turned_hi, turned_taken = sem("turned"), sem("turned_hi"), sem("turned_taken")
        proj_taken = sem("proj_taken")
        roped = sem("roped")
        k_staged, df_staged = sem("k_staged"), sem("df_staged")
        z_ready, dfT_ready, dfT_copied = sem("z_ready"), sem("dfT_ready"), sem("dfT_copied")
        e_ready, sp_ready = sem("e_ready"), sem("sp_ready")
        s_ready, stick_ready = sem("s_ready"), sem("stick_ready")
        smax_ready, p_ready, wexp_in, wexp_out = sem("smax_ready"), sem("p_ready"), sem("wexp_in"), sem("wexp_out")
        w_ready, pw_ready = sem("w_ready"), sem("pw_ready")
        o_ready, pT_ready, pT_copied = sem("o_ready"), sem("pT_ready"), sem("pT_copied")
        ss_ready, ms_ready, rms_ready, o_normed = sem("ss_ready"), sem("ms_ready"), sem("rms_ready"), sem("o_normed")
        do_ready, oT_ready, oT_hi, oT_copied = sem("do_ready"), sem("oT_ready"), sem("oT_hi"), sem("oT_copied")
        z_landed, gb_landed = sem("z_landed"), sem("gb_landed")
        var_ready, rstd_ready, x_ready = sem("var_ready"), sem("rstd_ready"), sem("x_ready")
        cs_ready, cmax_ready, cp_ready, cn_ready = sem("cs_ready"), sem("cmax_ready"), sem("cp_ready"), sem("cn_ready")
        cT_ready, cT_copied = sem("cT_ready"), sem("cT_copied")
        co_ready, co_hi, co_copied = sem("co_ready"), sem("co_hi"), sem("co_copied")
        keys_landed, keysT_ready, keysT_copied = sem("keys_landed"), sem("keysT_ready"), sem("keysT_copied")
        ks_ready, ks_copied = sem("ks_ready"), sem("ks_copied")
        top_ready, gexp_ready, idx_ready = sem("top_ready"), sem("gexp_ready"), sem("idx_ready")
        u_landed = [sem(f"u_landed{s}") for s in range(NU)]
        v_landed = [sem(f"v_landed{s}") for s in range(NV)]
        u_used, v_used, v_issued = sem("u_used"), sem("v_used"), sem("v_issued")
        slots_freed = sem("slots_freed")
        h_ready, gelu_ready, a_ready, diag_ready = sem("h_ready"), sem("gelu_ready"), sem("a_ready"), sem("diag_ready")
        acc_done, y_ready, y_stored = sem("acc_done"), sem("y_ready"), sem("y_stored")

        PS = 2 * NS
        SEG = SPLIT
        IN_PAIRS = w_in.shape[2] // (2 * BANK)
        MKV0 = IN_PAIRS
        WO0 = MKV0 + w_mkv.shape[2] // (2 * BANK)
        MQ0 = WO0 + NP // 2
        MO0 = MQ0 + NP // 2
        PQ0 = MO0 + NP // 2
        BODIES = SBH // 2
        CREDIT = 2
        RING_CREDIT = 16

        block = ctx.enter_context(nc.Block())

        @block.sync
        def _(sp):
            for q in range(NP):
                cols = slice(q * BANK, (q + 1) * BANK)
                sp.dma_start(x_in[:, :, cols], x_rows[:, :, cols]).then_inc(x_landed[q], 16)

            def load_pair(w, i, pair, first=False):
                for j in range(PS):
                    if not (first and j < RAW):
                        sp.wait_ge(lo_ready, pair * PS + (j + 1 - RAW))
                    cols = w[0][:, bass.ds(i * 2 * BANK + (j // NS) * BANK, BANK)]
                    src = cols.rearrange("(s k p) n -> s p k n", s=NS, p=P)[j % NS]
                    dst = raw[j % RAW].rearrange("p (k n) -> p k n", k=SK)
                    sp.dma_start(dst, src).then_inc(w_landed[j % RAW], 16)

            load_pair(w_in, 0, 0, first=True)
            sp.dma_start(mem_in, mem_rows).then_inc(mem_landed, 16)
            with sp.Fori(1, IN_PAIRS) as i:
                load_pair(w_in, i, i)
            for w, first_pair in ((w_mkv, MKV0), (w_o, WO0), (w_mq, MQ0), (w_mo, MO0), (w_pq, PQ0)):
                with sp.Fori(0, w.shape[2] // (2 * BANK)) as i:
                    load_pair(w, i, i + first_pair)
            for n in range(2 * NT):
                t, cols = n // 2, slice(n % 2 * D // 2, (n % 2 + 1) * D // 2)
                sp.wait_ge(y_ready, n + 1)
                sp.dma_start(out_rows[:, t, cols], y_out[:, t, cols]).then_inc(y_stored, 16)
            sp.wait_ge(y_stored, 16 * 2 * NT)

        @block.tensor
        def _(pe):
            def turn(src, group, nth):
                if nth >= 4:
                    pe.wait_ge(turned_taken, nth - 3)
                for k in (2 * group, 2 * group + 1):
                    for t in range(NT):
                        c = (k % 2) * T + t * P
                        m = nc.tensor.transpose(ps[:, 4 + nth % 4, c:c + P], src[:, t, k * P:(k + 1) * P], ident[:, :])
                m.then_inc(turned, 1)

            def slices(kind, js, pair, acts, par, spare):
                b0 = 2 * par
                for j in js:
                    if j % NS == 0:
                        pe.wait_ge(proj_taken, pair * 2 + j // NS + CREDIT - spare)
                    pe.wait_ge(lo_ready, pair * PS + j + 1)
                    hi, lo = w_hi[j % SPLIT], w_lo[j % SPLIT]
                    for k in range(SK):
                        kk = j % NS * SK + k
                        a_hi, a_lo = acts[0][kk], acts[1][kk]
                        first, last = kk == 0, kk == KB - 1
                        if kind == "rows":
                            for t in range(NT):
                                for n, (a, w) in enumerate(((a_hi, hi), (a_hi, lo), (a_lo, hi))):
                                    m = nc.tensor.matmul(ps[:, b0 + t, :], a[:, t * P:(t + 1) * P],
                                                         w[:, k * BANK:(k + 1) * BANK],
                                                         start=first and n == 0, stop=last and n == 2)
                        else:
                            for nb in range(4):
                                for n, (a, w) in enumerate(((a_hi, hi), (a_lo, hi), (a_hi, lo))):
                                    m = nc.tensor.matmul(ps[:, b0 + nb // 2, (nb % 2) * T:(nb % 2 + 1) * T],
                                                         w[:, k * BANK + nb * P:k * BANK + (nb + 1) * P], a,
                                                         start=first and nb % 2 == 0 and n == 0,
                                                         stop=last and nb % 2 == 1 and n == 2,
                                                         skip_group_check=True)
                    m.then_inc(w_used, 1)

            def panel(kind, s, pair, acts):
                slices(kind, range(s * NS, (s + 1) * NS), pair, acts, s, 1)

            def section(kind, first_pair, pairs, acts):
                with pe.Fori(first_pair, first_pair + pairs) as pair:
                    for s in range(2):
                        panel(kind, s, pair, acts)

            pe.wait_ge(consts_ready, 1)
            for g in range(8):
                if g % 2 == 0:
                    pe.wait_ge(x_landed[g // 2], 16)
                turn(x_in, g, g)
            pe.wait_ge(turned_taken, 8)
            section("cols", 0, 2, xT)
            section("rows", 2, 4, xT)
            pe.wait_ge(mem_landed, 16)
            for g in range(8):
                turn(mem_in, g, 8 + g)
            pe.wait_ge(turned_taken, 16)

            def attention_body(b, kind):
                pair = b + MKV0
                pe.wait_ge(k_staged, b + 1)
                pe.wait_ge(oT_copied, b * 2 - 1 + CREDIT)
                for hh in range(2):
                    q0 = (b * 2 + hh) * T
                    nc.tensor.matmul(ps[:, 2 + hh, 0:T], k_st[:, hh * T:hh * T + P], r1[:, bass.ds(q0, T)],
                                     start=True, stop=True)
                    nc.tensor.matmul(ps[:, 2 + hh, T:ZC], k_st[:, hh * T + P:(hh + 1) * T], r1[:, bass.ds(q0 + P, P)],
                                     start=True, stop=True).then_inc(z_ready, 1)
                pe.wait_ge(df_staged, b + 1)
                pe.wait_ge(pT_copied, b * 2 + CREDIT)
                for hh in range(2):
                    for q in range(2):
                        for t in range(NT):
                            m = nc.tensor.transpose(ps[:, 4 + hh, (q * NT + t) * P:(q * NT + t + 1) * P],
                                                    df_st[:, t, q, hh * P:(hh + 1) * P], ident[:, :])
                    m.then_inc(dfT_ready, 1)
                slices(kind, range(0, 4), pair, memT, 0, 0)
                pe.wait_ge(dfT_copied, b * 2 + 2)
                pe.wait_ge(o_normed, b * 2 + CREDIT)
                pe.wait_ge(oT_copied, b * 2 + CREDIT)
                for hh in range(2):
                    for st in range(2):
                        q = dfT[hh][st * QD:(st + 1) * QD, :]
                        nc.tensor.matmul(ps[:, 4 + st, hh * T:(hh + 1) * T], q[:, P:2 * P], q[:, T:2 * T],
                                         start=True, stop=True)
                        m = nc.tensor.matmul(ps[:, 6 + st, hh * P:(hh + 1) * P], q[:, 0:P], q[:, T:T + P],
                                             start=True, stop=True)
                m.then_inc(s_ready, 1)
                for hh in range(2):
                    pe.wait_ge(sp_ready, b * 2 + hh + 1)
                    nc.tensor.matmul(ps[:, 2 + hh, 0:ZC], neg_after[:, :], sp_z[hh], start=True, stop=False,
                                     skip_group_check=True)
                    nc.tensor.matmul(ps[:, 2 + hh, P:T], neg_ones[:, :], sp_z[hh][:, T:ZC], start=False, stop=True,
                                     skip_group_check=True).then_inc(stick_ready, 1)
                slices(kind, range(4, 8), pair, memT, 0, 0)
                for hh in range(2):
                    pe.wait_ge(w_ready, b * 2 + hh + 1)
                    v0 = (b * 2 + hh) * DH
                    w = sp_z[hh]
                    nc.tensor.matmul(ps[:, 7, hh * T:hh * T + P], w[:, 0:P], r2[:, bass.ds(v0, DH)], start=True, stop=True)
                    nc.tensor.matmul(ps[:, 7, hh * T + P:(hh + 1) * T], w[:, P:T], r2[:, bass.ds(v0, DH)],
                                     start=True, stop=False)
                    m = nc.tensor.matmul(ps[:, 7, hh * T + P:(hh + 1) * T], w[:, T:ZC], r2[:, bass.ds(v0 + D, DH)],
                                         start=False, stop=True)
                m.then_inc(o_ready, 1)
                for hh in range(2):
                    pe.wait_ge(pw_ready, b * 2 + hh + 1)
                    for c, src in enumerate((s_t0[:, 2 * hh, :], s_t1[hh][:, 0, 0:P], s_t1[hh][:, 0, P:T])):
                        m = nc.tensor.transpose(ps[:, 4 + hh, c * P:(c + 1) * P], src, ident[:, :])
                    m.then_inc(pT_ready, 1)
                slices(kind, range(8, 12), pair, memT, 0, 0)
                for hh in range(2):
                    pe.wait_ge(pT_copied, b * 2 + hh + 1 + CREDIT)
                    v0 = (b * 2 + hh) * DH + SBW
                    nc.tensor.matmul(ps[:, 6, hh * T:hh * T + P], pT[hh][:, 0:P], r2[:, bass.ds(v0, DH)],
                                     start=True, stop=True)
                    nc.tensor.matmul(ps[:, 6, hh * T + P:(hh + 1) * T], pT[hh][:, P:T], r2[:, bass.ds(v0, DH)],
                                     start=True, stop=False)
                    m = nc.tensor.matmul(ps[:, 6, hh * T + P:(hh + 1) * T], pT[hh][:, T:ZC],
                                         r2[:, bass.ds(v0 + D, DH)], start=False, stop=True)
                m.then_inc(do_ready, 1)
                pe.wait_ge(o_normed, b * 2 + 1 + CREDIT)
                for c in range(4):
                    m = nc.tensor.transpose(ps[:, 2, c * P:(c + 1) * P], sb_n[:, c, :], ident[:, :])
                m.then_inc(oT_ready, 1)
                slices(kind, range(12, 16), pair, memT, 0, 0)
                pe.wait_ge(o_normed, b * 2 + 2 + CREDIT)
                for c in range(4):
                    m = nc.tensor.transpose(ps[:, 7, c * P:(c + 1) * P], df_n[:, c, :], ident[:, :])
                m.then_inc(oT_ready, 1)

            with pe.Fori(0, BODIES // 2) as b:
                attention_body(b, "cols")
            with pe.Fori(BODIES // 2, BODIES) as b:
                attention_body(b, "rows")
            pe.wait_ge(oT_copied, 2 * BODIES + CREDIT)
            pe.wait_ge(proj_taken, 2 * WO0 + CREDIT)
            section("rows", WO0, NP // 2, mixedT)

            def turn_norm(src, nth, first_chunk):
                for g in range(8):
                    if g % 2 == 0:
                        pe.wait_ge(x_ready, first_chunk + g // 2 + 1)
                    turn(src, g, nth + g)
                pe.wait_ge(turned_taken, nth + 8)

            turn_norm(x1, 16, 0)
            section("cols", MQ0, NP // 2, x1T)
            pe.wait_ge(proj_taken, 2 * MO0 + CREDIT)
            for h in range(MH):
                for t in range(NT):
                    for kb in range(MB):
                        m = nc.tensor.matmul(ps[:, 4 + h, t * T:(t + 1) * T], cqT[:, h * MB + kb, t * P:(t + 1) * P],
                                             mkT[:, h * MB + kb, :], start=kb == 0, stop=kb == MB - 1)
                m.then_inc(cs_ready, 1)
            for h in range(MH):
                pe.wait_ge(cn_ready, h + 1)
                for m_t in range(NT):
                    for t in range(NT):
                        m = nc.tensor.transpose(ps[:, h, m_t * T + t * P:m_t * T + (t + 1) * P],
                                                c_p[:, h, t, m_t * P:(m_t + 1) * P], ident[:, :])
                m.then_inc(cT_ready, 1)
            for g in range(KB // 2):
                if g % (MB // 2) == 0:
                    pe.wait_ge(cT_copied, g // (MB // 2) + 1)
                if g >= 4:
                    pe.wait_ge(co_copied, g - 3)
                for n in range(2):
                    blk = 2 * g + n
                    for m_t in range(NT):
                        m = nc.tensor.matmul(ps[:, 4 + g % 4, n * T:(n + 1) * T], mv[:, m_t, blk * P:(blk + 1) * P],
                                             c_pT[:, blk // MB, m_t, :], start=m_t == 0, stop=m_t == NT - 1)
                m.then_inc(co_ready, 1)
            pe.wait_ge(co_copied, KB // 2)
            section("rows", MO0, NP // 2, coT)
            pe.wait_ge(keys_landed, 16)
            for n in range(2):
                m = nc.tensor.transpose(ps[:, 7, n * P:(n + 1) * P], keys_in[:, n * NKEY:(n + 1) * NKEY], ident[:, :])
            m.then_inc(keysT_ready, 1)
            pe.wait_ge(keysT_copied, 1)
            turn_norm(x2, 24, 4)

            def key_products(pair, s):
                pe.wait_ge(proj_taken, pair * 2 + s + 1 + CREDIT)
                pe.wait_ge(ks_copied, pair * 2 + s - 2 * PQ0 + CREDIT - 1)
                for t in range(NT):
                    for n in range(4):
                        m = nc.tensor.matmul(ps[:, 4 + 2 * s + t, n * P:(n + 1) * P], pq_st[s][:, n, t * P:(t + 1) * P],
                                             keysT[:, (n % 2) * NKEY:(n % 2 + 1) * NKEY], start=True, stop=True)
                m.then_inc(ks_ready, 1)

            with pe.Fori(PQ0, PQ0 + NP // 2) as pair:
                panel("cols", 0, pair, x2T)
                slices("cols", range(8, 10), pair, x2T, 1, 1)
                key_products(pair, 0)
                slices("cols", range(10, 16), pair, x2T, 1, 1)
                key_products(pair, 1)

            pe.wait_ge(ks_copied, NP + CREDIT)
            pe.wait_ge(consts_ready, 2)
            for b in range(8):
                m = nc.tensor.matmul(ps[:, b, :], diag[:, 0, :], x2[:, 0, 0:BANK], start=True, stop=True)
            m.then_inc(v_used, RING_CREDIT)

            def mix_body(h):
                for t in range(NT):
                    for j in range(TOPK):
                        n = (h * NT + t) * TOPK + j
                        pe.wait_ge(v_landed[j % NV], ((h * NT + t) * 2 + j // NV) * 16 + 16)
                        pe.wait_ge(diag_ready, n + 1)
                        for q in range(NP):
                            m = nc.tensor.matmul(ps[:, 4 * t + q, :], diag[:, j, :],
                                                 v_ring[j % NV][:, q * BANK:(q + 1) * BANK],
                                                 start=False, stop=False, skip_group_check=True)
                        m.then_inc(v_used, 1)

            with pe.Fori(0, PH) as h:
                mix_body(h)

        @block.scalar
        def _(act):
            steps = Steps(act, act_step)
            act.dma_start(rope_cs[:, :].rearrange("p (t c) -> p t c", t=NT),
                          rope.rearrange("(t p) c -> p t c", p=P)).then_inc(small_landed, 16)
            act.dma_start(lam_in, df_lambda[0].rearrange("a d -> (a d)").partition_broadcast(P)).then_inc(small_landed, 16)
            act.dma_start(sbg[:, :], sb_gain[0].rearrange("h d -> (h d)").partition_broadcast(P)).then_inc(small_landed, 16)
            act.dma_start(dfg[:, :], df_gain[0].partition_broadcast(P)).then_inc(small_landed, 16)
            act.sem_inc(proj_taken, CREDIT)
            act.sem_inc(ks_copied, CREDIT)
            act.sem_inc(oT_copied, CREDIT)
            act.sem_inc(pT_copied, CREDIT)

            def copy_turned(dst, nth):
                for g in range(8):
                    act.wait_ge(turned, nth + g + 1)
                    nc.scalar.activation(dst[:, g * 2 * T:(g + 1) * 2 * T], ps[:, 4 + (nth + g) % 4, :],
                                         ACT.Copy).then_inc(turned_hi, 1)

            def split_hi(pair, js, start=False):
                for j in js:
                    act.wait_ge(w_landed[j % RAW], (pair * (PS // RAW) + j // RAW) * 16 + 16)
                    if not start:
                        act.wait_ge(w_used, pair * PS + (j + 1 - SPLIT))
                    nc.scalar.activation(w_hi[j % SPLIT], raw[j % RAW], ACT.Copy).then_inc(hi_ready, 1)

            def take(kind, dst, col, pair, s, b0):
                act.wait_ge(w_used, pair * PS + (s + 1) * NS)
                if kind == "rows":
                    nc.scalar.activation(dst[:, :, bass.ds(col, BANK)], ps[:, b0:b0 + 2, :],
                                         ACT.Copy).then_inc(proj_taken, 1)
                else:
                    nc.scalar.activation(dst[:, bass.ds(col, 2 * BANK)], bank(b0, 2), ACT.Copy).then_inc(proj_taken, 1)

            def split_pair(pair, take_panel=lambda s: None):
                for s in range(2):
                    split_hi(pair, range(4 + 8 * s, 11 + 8 * s))
                    take_panel(s)
                    split_hi(pair, [11 + 8 * s])

            def section(kind, dst, first_pair, pairs, width=BANK):
                with act.Fori(0, pairs) as i:
                    split_pair(i + first_pair,
                               lambda s: take(kind, dst, (i * 2 + s) * width, i + first_pair, s, 2 * s))

            act.wait_ge(roped, 1)
            nc.scalar.activation(lam_e, lam_s, ACT.Exp).then_inc(roped, 1)
            copy_turned(p0, 0)
            split_hi(0, range(SEG), start=True)
            section("cols", r1, 0, 2, 2 * BANK)
            section("rows", sb_v, 2, 1)
            section("rows", df_qk, 3, 2)
            section("rows", df_v, 5, 1)
            copy_turned(p0, 8)

            def attention_body(b, kind):
                for hh in range(2):
                    act.wait_ge(dfT_ready, b * 2 + hh + 1)
                    nc.scalar.activation(dfT[hh], ps[:, 4 + hh, :], ACT.Copy).then_inc(dfT_copied, 1)
                pair = b + MKV0
                for hh in range(2):
                    act.wait_ge(z_ready, b * 2 + hh + 1)
                    for dst, src, func, scale in ((e_z[hh], ps[:, 2 + hh, 0:ZC], ACT.Copy, SB_SCALE),
                                                  (sp_z[hh], e_z[hh], ACT.Abs, 1.0), (sp_z[hh], sp_z[hh], ACT.Exp, -1.0)):
                        steps.did(nc.scalar.activation(dst, src, func, scale=scale))
                        steps.wait()
                    nc.scalar.activation(sp_z[hh], sp_z[hh], ACT.Ln, bias=1.0).then_inc(e_ready, 1)
                    split_hi(pair, (4 + 2 * hh, 5 + 2 * hh))
                act.wait_ge(smax_ready, b + 1)
                for hh in range(2):
                    for st in range(2):
                        n = 2 * hh + st
                        nc.scalar.activation(s_t0[:, n, :], s_t0[:, n, :], ACT.Exp, bias=nmx[:, n:n + 1],
                                             scale=DF_SCALE, accum_out=dsum[:, n:n + 1])
                        m = nc.scalar.activation(s_t1[hh][:, st, :], s_t1[hh][:, st, :], ACT.Exp,
                                                 bias=nmx[:, 4 + n:5 + n], scale=DF_SCALE,
                                                 accum_out=dsum[:, 4 + n:5 + n])
                m.then_inc(p_ready, 1)
                for hh in range(2):
                    act.wait_ge(wexp_in, b * 2 + hh + 1)
                    nc.scalar.activation(sp_z[hh], e_z[hh], ACT.Exp).then_inc(wexp_out, 1)
                dst, width = (r5, 2 * BANK) if kind == "cols" else (mv, BANK)
                i = b if kind == "cols" else b - BODIES // 2
                split_hi(pair, range(8, 11))
                take(kind, dst, i * 2 * width, pair, 0, 0)
                split_hi(pair, [11])
                act.wait_ge(o_ready, b + 1)
                for c in range(4):
                    m = nc.scalar.activation(sb_n[:, c, :], ps[:, 7, c * P:(c + 1) * P], ACT.Square,
                                             accum_out=ss[:, c:c + 1])
                m.then_inc(ss_ready, 1)
                for hh in range(2):
                    act.wait_ge(pT_ready, b * 2 + hh + 1)
                    nc.scalar.activation(pT[hh], ps[:, 4 + hh, 0:ZC], ACT.Copy).then_inc(pT_copied, 1)
                split_hi(pair, range(12, 16))
                act.wait_ge(do_ready, b + 1)
                for c in range(4):
                    m = nc.scalar.activation(s_t1[c // 2][:, 1, (c % 2) * P:(c % 2 + 1) * P], ps[:, 6, c * P:(c + 1) * P], ACT.Square,
                                             accum_out=dss[:, c:c + 1])
                m.then_inc(ss_ready, 1)
                act.wait_ge(oT_ready, b * 2 + 1)
                nc.scalar.activation(p1[:, bass.ds(b * 2 * T, 2 * T)], ps[:, 2, :], ACT.Copy).then_inc(oT_hi, 1)
                split_hi(pair, range(16, 19))
                take(kind, dst, i * 2 * width + width, pair, 1, 0)
                split_hi(pair, [19])
                act.wait_ge(oT_ready, b * 2 + 2)
                nc.scalar.activation(p1[:, bass.ds(b * 2 * T + SBH * T, 2 * T)], ps[:, 7, :],
                                     ACT.Copy).then_inc(oT_hi, 1)

            act.preload_act_table_set("natural_log_exp_and_others")
            for first, kind in ((0, "cols"), (BODIES // 2, "rows")):
                with act.Fori(first, first + BODIES // 2) as b:
                    steps.enter(b - first if first else b, 6)
                    attention_body(b, kind)
                steps.leave(BODIES // 2)

            with act.Fori(WO0, WO0 + NP // 2) as pair:
                split_pair(pair)
            copy_turned(p1, 16)
            section("cols", r0, MQ0, NP // 2, 2 * BANK)
            for h in range(MH):
                act.wait_ge(cmax_ready, h + 1)
                for t in range(NT):
                    n = 2 * h + t
                    m = nc.scalar.activation(c_p[:, h, t, :], ps[:, 4 + h, t * T:(t + 1) * T], ACT.Exp,
                                             bias=nmx[:, n:n + 1], scale=M_SCALE, accum_out=dsum[:, n:n + 1])
                m.then_inc(cp_ready, 1)
            for h in range(MH):
                act.wait_ge(cT_ready, h + 1)
                nc.scalar.activation(c_pT[:, h, :, :], ps[:, h, :].rearrange("p (m q) -> p m q", m=NT),
                                     ACT.Copy).then_inc(cT_copied, 1)
            for g in range(KB // 2):
                act.wait_ge(co_ready, g + 1)
                nc.scalar.activation(p1[:, g * 2 * T:(g + 1) * 2 * T], ps[:, 4 + g % 4, :], ACT.Copy)\
                    .then_inc(co_hi, 1)
            with act.Fori(MO0, MO0 + NP // 2) as pair:
                split_pair(pair)
            act.wait_ge(keysT_ready, 1)
            nc.scalar.activation(keysT[:, :], ps[:, 7, 0:2 * NKEY], ACT.Copy).then_inc(keysT_copied, 1)
            copy_turned(p1, 24)
            def gates(n):
                act.wait_ge(top_ready, n + 1)
                t = 0
                nc.scalar.activation(top, top, ACT.Exp, bias=ntop, accum_out=gsum).then_inc(gexp_ready, 1)

            for i in range(NP // 2):
                def take_scores(s):
                    act.wait_ge(ks_ready, i * 2 + s + 1)
                    nc.scalar.activation(key_scores[:, :, bass.ds((i * 2 + s) * BANK, BANK)],
                                         ps[:, 4 + 2 * s:6 + 2 * s, :], ACT.Copy).then_inc(ks_copied, 1)

                def take_queries(s):
                    act.wait_ge(w_used, (PQ0 + i) * PS + (s + 1) * NS)
                    if s == 0:
                        act.wait_ge(ks_copied, i * 2 + CREDIT)
                    nc.scalar.activation(pq_st[s].rearrange("p b t -> p (b t)"), bank(2 * s, 2),
                                         ACT.Copy).then_inc(proj_taken, 1)
                if i == 0:
                    split_hi(PQ0, range(4, 11))
                    take_queries(0)
                    split_hi(PQ0, [11])
                    take_scores(0)
                    split_hi(PQ0, range(12, 16))
                    gates(0)
                    split_hi(PQ0, range(16, 19))
                    take_queries(1)
                    split_hi(PQ0, [19])
                    take_scores(1)
                    split_hi(PQ0, range(20, 24))
                    gates(1)
                else:
                    split_hi(PQ0 + i, range(8, 11))
                    take_queries(0)
                    split_hi(PQ0 + i, [11])
                    take_scores(0)
                    split_hi(PQ0 + i, range(12, 16))
                    take_queries(1)
                    take_scores(1)

            def peer_body(h, last):
                for t in range(NT):
                    unit = h * NT + t
                    act.wait_ge(h_ready, unit + 1)
                    nc.scalar.activation(act_h[t], hdot[t], ACT.Gelu).then_inc(gelu_ready, 1)
                    if not last:
                        gates(unit + NT)
                    act.wait_ge(a_ready, unit + 1)
                    for j in range(TOPK):
                        act.wait_ge(v_used, unit * TOPK + (j + 1 + RING_CREDIT - TOPK))
                        nc.scalar.activation(diag[:, j, :], ident[:, :], ACT.Copy,
                                             scale=weight[t][:, j:j + 1]).then_inc(diag_ready, 1)

            with act.Fori(0, PH - 1) as h:
                peer_body(h, False)
            peer_body(PH - 1, True)

        @block.gpsimd
        def _(pool):
            steps = Steps(pool, pool_step)
            pool.sem_inc(o_normed, CREDIT)
            for dst, v in ((ident, 0.0), (before, 1.0), (neg_after, -1.0), (neg_ones, -1.0), (causal, 0.0)):
                steps.did(pool.memset(dst[:, :], v))
            steps.did(pool.memset(nhalf, -0.5))
            steps.wait()
            steps.did(pool.affine_select(out=ident[:, :], in_=ident[:, :], compare_op=ALU.not_equal, fill=1.0,
                                         base=0, pattern=[[-1, P]], channel_multiplier=1))
            steps.did(pool.affine_select(out=before[:, :], in_=before[:, :], compare_op=ALU.is_gt, fill=0.0,
                                         base=0, pattern=[[1, P]], channel_multiplier=-1))
            steps.did(pool.affine_select(out=neg_after[:, :], in_=neg_after[:, :], compare_op=ALU.is_gt, fill=0.0,
                                         base=0, pattern=[[-1, P]], channel_multiplier=1))
            steps.did(pool.affine_select(out=causal[:, P:T], in_=causal[:, P:T], compare_op=ALU.is_ge,
                                         fill=NEG_BIG, base=0, pattern=[[-1, P]], channel_multiplier=1))
            steps.did(pool.iota(iota[:, :], pattern=[[1, TOPK]], base=0, channel_multiplier=0,
                                allow_small_or_imprecise_dtypes=True))
            steps.wait()
            pool.sem_inc(consts_ready, 1)

            def power(src, dst, nth):
                pool.wait_ge(ms_ready, nth)
                nc.gpsimd.tensor_tensor(dst, src, nhalf, ALU.pow).then_inc(rms_ready, 1)

            def attention_body(b):
                pool.wait_ge(z_ready, b * 2 + 2)
                pool.wait_ge(dfT_ready, b * 2 + 2)
                stage(b + 1)
                powers(b)

            def stage(b):
                nc.gpsimd.tensor_copy(k_st, r1[:, bass.ds(b * 2 * T + SBH * T, 2 * T)]).then_inc(k_staged, 1)
                src = df_qk.rearrange("p t (q c) -> p t q c", q=2)[:, :, :, bass.ds(b * 2 * P, 2 * P)]
                for t in range(NT):
                    m = nc.gpsimd.tensor_copy(df_st[:, t], src[:, t])
                m.then_inc(df_staged, 1)

            def powers(b):
                power(ss, rs, b * 2 + 1)
                power(dss, drs, b * 2 + 2)

            pool.wait_ge(proj_taken, 2 * MKV0 + CREDIT)
            pool.wait_ge(roped, 3)
            stage(0)
            with pool.Fori(0, BODIES - 1) as b:
                attention_body(b)
            powers(BODIES - 1)
            pool.wait_ge(w_used, WO0 * PS)
            pool.dma_start(z1, x_rows).then_inc(z_landed, 16)
            for n, (g, b) in enumerate(((ln1_g, ln1_b), (ln2_g, ln2_b))):
                if n:
                    pool.wait_ge(x_ready, 4 * n)
                pool.dma_start(gain_b, g[0].partition_broadcast(P)).then_inc(gb_landed, 16)
                pool.dma_start(bias_b, b[0].partition_broadcast(P)).then_inc(gb_landed, 16)
                pool.wait_ge(var_ready, n + 1)
                nc.gpsimd.tensor_tensor(rstd, veps, nhalf[:, 0:NT], ALU.pow).then_inc(rstd_ready, 1)
                if n == 0:
                    pool.wait_ge(cT_ready, MH)
                    pool.dma_start(keys_in.rearrange("p (s d) -> p s d", s=2),
                                   sub_keys[0].rearrange("s n d -> n s d")).then_inc(keys_landed, 16)
            def gather(table, ring_slots, landed, t, j, **kw):
                pool.indirect_dma_start(ring_slots[j % len(ring_slots)], None, table,
                                        bass.IndirectOffsetOnAxis(ap=idx[t][:, j:j + 1], axis=0), **kw).then_inc(landed[j % len(ring_slots)], 16)

            def gather_u(unit, t, j):
                if isinstance(unit, int) and unit == 1 and j < NU:
                    if j == EARLY:
                        pool.wait_ge(lo_ready, (PQ0 + NP // 2) * PS)
                    used = max(range(j, TOPK, EARLY)) + 1 if j < EARLY else TOPK
                else:
                    used = unit * TOPK + (j + 1 - NU)
                pool.wait_ge(u_used, used)
                pool.sem_inc(slots_freed, 1)
                gather(peer_u[0], u_ring, u_landed, t, j)

            def gather_v(unit, t, j):
                pool.wait_ge(v_used, unit * TOPK + (j + 1 - NV + RING_CREDIT))
                pool.sem_inc(slots_freed, 1)
                gather(peer_v[0], v_ring, v_landed, t, j, **({"engine_sem": v_issued} if j == TOPK - 1 else {}))

            def split_lo(j):
                pool.wait_ge(hi_ready, PQ0 * PS + j + 1)
                nc.gpsimd.tensor_tensor(w_lo[j % SPLIT], raw[j % RAW], w_hi[j % SPLIT].bitcast(F32),
                                        ALU.subtract).then_inc(lo_ready, 1)

            def first_u(j):
                if j >= EARLY:
                    pool.wait_ge(u_used, j + 1 - EARLY)
                    pool.sem_inc(slots_freed, 1)
                pool.indirect_dma_start(u_ring[j % EARLY], None, peer_u[0],
                                        bass.IndirectOffsetOnAxis(ap=idx[0][:, j:j + 1], axis=0))\
                    .then_inc(u_landed[j % EARLY], 16)

            for j in range(4, 2 * PS):
                split_lo(j)
                if j == 18:
                    pool.wait_ge(idx_ready, 1)
                    pool.sem_inc(slots_freed, 1)
                if 18 <= j < 21:
                    first_u(2 * (j - 18))
                    first_u(2 * (j - 18) + 1)
                if 26 <= j < 31:
                    first_u(EARLY + 2 * (j - 26))
                    first_u(EARLY + 2 * (j - 26) + 1)
            pool.wait_ge(lo_ready, (PQ0 + NP // 2) * PS)
            pool.dma_start(gain3_b, ln3_g[0].partition_broadcast(P)).then_inc(gb_landed, 16)
            pool.dma_start(bias3_b, ln3_b[0].partition_broadcast(P)).then_inc(gb_landed, 16)
            pool.wait_ge(ks_copied, NP + CREDIT)
            pool.memset(diag[:, 0, :], 0.0).then_inc(consts_ready, 1)

            def next_indices(unit):
                pool.wait_ge(idx_ready, unit + 1)
                pool.sem_inc(slots_freed, 1)

            def unit_rows(unit, t):
                for j in range(TOPK + 2):
                    if j < TOPK:
                        gather_v(unit, t, j)
                    if j == 2:
                        next_indices(unit + 1)
                    if j >= 2:
                        gather_u(unit + 1, (t + 1) % NT, j - 2)

            next_indices(1)
            for j in range(NU):
                gather_u(1, 1, j)
            for j in range(NU):
                gather_v(0, 0, 2 * j)
                gather_v(0, 0, 2 * j + 1)
                gather_u(1, 1, NU + j)
            unit_rows(1, 1)
            with pool.Fori(1, PH - 1) as h:
                for t in range(NT):
                    unit_rows(h * NT + t, t)
            unit_rows((PH - 1) * NT, 0)
            for j in range(TOPK):
                gather_v((PH - 1) * NT + 1, 1, j)
            for t in range(NT):
                pool.wait_ge(var_ready, 3 + t)
                nc.gpsimd.tensor_tensor(rstd[:, t:t + 1], veps[:, t:t + 1], nhalf[:, 0:1], ALU.pow).then_inc(rstd_ready, 1)

        @block.vector
        def _(dve):
            steps = Steps(dve, dve_step)

            def chain(ins):
                steps.did(ins)
                steps.wait()

            dve.wait_ge(small_landed, 64)
            for n in range(2):
                steps.did(nc.vector.tensor_tensor(lam_pr, lam_in[:, 2 * n * QD:(2 * n + 1) * QD],
                                                  lam_in[:, (2 * n + 1) * QD:(2 * n + 2) * QD], ALU.mult))
                steps.wait()
                steps.did(nc.vector.tensor_reduce(lam_s[:, n:n + 1], lam_pr, AX_X, ALU.add))
                steps.wait()
            dve.sem_inc(roped, 1)
            steps.did(nc.vector.tensor_scalar(dfg[:, :], dfg[:, :], 1.0 - LAMBDA_INIT, None, ALU.mult))
            dve.wait_ge(roped, 2)
            chain(nc.vector.tensor_tensor(neg_lam, lam_e[:, 1:2], lam_e[:, 0:1], ALU.subtract))
            steps.did(nc.vector.tensor_scalar(neg_lam, neg_lam, -LAMBDA_INIT, None, ALU.add))

            def turned_lo(dst, nth, groups):
                for g in groups:
                    hi, lo = [r[:, g * 2 * T:(g + 1) * 2 * T] for r in dst]
                    dve.wait_ge(turned_hi, nth + g + 1)
                    nc.vector.tensor_tensor(lo, ps[:, 4 + (nth + g) % 4, :], hi.bitcast(F32),
                                            ALU.subtract).then_inc(turned_taken, 1)

            def split_lo(pair, js):
                for j in js:
                    dve.wait_ge(hi_ready, pair * PS + j + 1)
                    nc.vector.tensor_tensor(w_lo[j % SPLIT], raw[j % RAW], w_hi[j % SPLIT].bitcast(F32),
                                            ALU.subtract).then_inc(lo_ready, 1)

            turned_lo((p0, p4), 0, range(8))
            split_lo(0, range(SEG))
            with dve.Fori(0, IN_PAIRS - 1) as pair:
                split_lo(pair, range(4, 20))
            split_lo(IN_PAIRS - 1, range(4, 8))

            dve.wait_ge(proj_taken, 10 + CREDIT)
            heads = 2 * SBW // QD
            both = ta[:, 0:heads * ROT].rearrange("p (h c) -> p h c", h=heads)
            cross = ta[:, heads * ROT:2 * heads * ROT].rearrange("p (h c) -> p h c", h=heads)
            for t in range(NT):
                part = df_qk[:, t].rearrange("p (h c) -> p h c", c=QD)[:, :, 0:ROT]
                cos_t = cos2[:, t:t + 1, :].to_broadcast([P, heads, ROT])
                sin_t = sin2[:, t:t + 1, :].to_broadcast([P, heads, ROT])
                steps.did(nc.vector.tensor_tensor(both, part, cos_t, ALU.mult))
                steps.did(nc.vector.tensor_tensor(cross[:, :, 0:HR], part[:, :, HR:ROT], sin_t[:, :, 0:HR], ALU.mult))
                steps.did(nc.vector.tensor_tensor(cross[:, :, HR:ROT], part[:, :, 0:HR], sin_t[:, :, HR:ROT], ALU.mult))
                steps.wait()
                steps.did(nc.vector.tensor_tensor(part, both, cross, ALU.add))
                steps.wait()
            dve.sem_inc(roped, 1)

            split_lo(IN_PAIRS - 1, range(8, 20))
            turned_lo((p0, p4), 8, range(8))

            diag_of = lambda a: a.rearrange("p (b c) -> p b c", b=3)[:, 0:3:2, :]
            before2 = before[:, :].unsqueeze(1).to_broadcast([P, 2, P])
            def rms_norm(b, nth, src_bank, sums, root, gain_of, dst):
                dve.wait_ge(ss_ready, nth)
                nc.vector.tensor_scalar(sums, sums, 1.0 / DH, RMS_EPS, ALU.mult, ALU.add).then_inc(ms_ready, 1)
                dve.wait_ge(rms_ready, nth)
                for c in range(4):
                    m = nc.vector.scalar_tensor_tensor(out=dst[:, c, :], in0=ps[:, src_bank, c * P:(c + 1) * P],
                                                       scalar=root[:, c:c + 1], in1=gain_of(c // 2),
                                                       op0=ALU.mult, op1=ALU.mult)
                m.then_inc(o_normed, 1)

            def attention_body(b):
                pair = b + MKV0
                for hh in range(2):
                    dve.wait_ge(e_ready, b * 2 + hh + 1)
                    chain(nc.vector.scalar_tensor_tensor(out=sp_z[hh], in0=e_z[hh], scalar=0.0, in1=sp_z[hh],
                                                         op0=ALU.max, op1=ALU.add))
                    chain(nc.vector.tensor_tensor(e_z[hh], e_z[hh], sp_z[hh], ALU.subtract))
                    nc.vector.tensor_tensor(diag_of(sp_z[hh]), diag_of(sp_z[hh]), before2, ALU.mult)\
                        .then_inc(sp_ready, 1)
                    split_lo(pair, (4 + 2 * hh, 5 + 2 * hh))
                dve.wait_ge(s_ready, b + 1)
                for st in range(2):
                    steps.did(nc.vector.tensor_tensor(s_t0[:, st:4:2, :], ps[:, 6 + st, 0:T].rearrange("p (h c) -> p h c", h=2),
                                                      causal[:, P:T].unsqueeze(1).to_broadcast([P, 2, P]), ALU.add))
                for hh in range(2):
                    steps.did(nc.vector.tensor_tensor(s_t1[hh], ps[:, 4:6, hh * T:(hh + 1) * T],
                                                      causal[:, :].unsqueeze(1).to_broadcast([P, 2, T]), ALU.add))
                steps.wait()
                steps.did(nc.vector.tensor_reduce(mx[:, 0:4], s_t0, AX_X, ALU.max))
                for hh in range(2):
                    steps.did(nc.vector.tensor_reduce(mx[:, 4 + 2 * hh:6 + 2 * hh], s_t1[hh], AX_X, ALU.max))
                steps.wait()
                nc.vector.tensor_scalar(nmx, mx, -DF_SCALE, None, ALU.mult).then_inc(smax_ready, 1)
                for hh in range(2):
                    dve.wait_ge(stick_ready, b * 2 + hh + 1)
                    nc.vector.tensor_tensor(e_z[hh], e_z[hh], ps[:, 2 + hh, 0:ZC], ALU.add).then_inc(wexp_in, 1)
                for hh in range(2):
                    dve.wait_ge(wexp_out, b * 2 + hh + 1)
                    nc.vector.tensor_tensor(diag_of(sp_z[hh]), diag_of(sp_z[hh]), before2, ALU.mult)\
                        .then_inc(w_ready, 1)
                dve.wait_ge(p_ready, b + 1)
                chain(nc.vector.reciprocal(rsum, dsum))
                chain(nc.vector.tensor_scalar(c2, rsum, neg_lam, None, ALU.mult))
                for hh in range(2):
                    p2 = (s_t0[:, 2 * hh + 1, :], s_t1[hh][:, 1, :])
                    p1 = (s_t0[:, 2 * hh, :], s_t1[hh][:, 0, :])
                    for n in range(2):
                        c = 4 * n + 2 * hh
                        steps.did(nc.vector.tensor_scalar(p2[n], p2[n], c2[:, c + 1:c + 2], None, ALU.mult))
                    steps.wait()
                    for n in range(2):
                        c = 4 * n + 2 * hh
                        m = nc.vector.scalar_tensor_tensor(out=p1[n], in0=p1[n], scalar=rsum[:, c:c + 1], in1=p2[n],
                                                           op0=ALU.mult, op1=ALU.add)
                    m.then_inc(pw_ready, 1)
                split_lo(pair, range(8, 12))
                rms_norm(b, b * 2 + 1, 7, ss, rs, lambda hh: sbg[:, bass.ds((b * 2 + hh) * DH, DH)], sb_n)
                split_lo(pair, range(12, 16))
                rms_norm(b, b * 2 + 2, 6, dss, drs, lambda hh: dfg[:, :], df_n)
                mixed_rests(b, 0, 2)
                split_lo(pair, range(16, 20))
                mixed_rests(b, 1, 7)

            def mixed_rests(b, kind, src_bank):
                dve.wait_ge(oT_hi, b * 2 + kind + 1)
                nc.vector.tensor_tensor(mixed_lo[:, kind, :, bass.ds(b * T, T)],
                                        ps[:, src_bank, :].rearrange("p (h t) -> p h t", h=2),
                                        p1[:, bass.ds(b * 2 * T + kind * SBH * T, 2 * T)].bitcast(F32)
                                        .rearrange("p (h t) -> p h t", h=2), ALU.subtract).then_inc(oT_copied, 1)

            with dve.Fori(0, BODIES) as b:
                steps.enter(b, 17)
                attention_body(b)
            steps.leave(BODIES)

            def residual(z, x_old, first_pair):
                with dve.Fori(0, NP // 2) as i:
                    steps.enter(i, 2)
                    for s in range(2):
                        q = i * 2 + s
                        cols = bass.ds(q * BANK, BANK)
                        split_lo(i + first_pair, range(4 + 8 * s, 11 + 8 * s))
                        dve.wait_ge(w_used, (i + first_pair) * PS + (s + 1) * NS)
                        nc.vector.scalar_tensor_tensor(out=z[:, :, cols], in0=x_old[:, :, cols], scalar=ALPHA,
                                                       in1=ps[:, 2 * s:2 * s + 2, :], op0=ALU.mult,
                                                       op1=ALU.add).then_inc(proj_taken, 1)
                        split_lo(i + first_pair, [11 + 8 * s])
                        dve.wait_ge(proj_taken, i * 2 + (2 * first_pair + s + 1 + CREDIT))
                        for t in range(NT):
                            m = nc.vector.bn_stats(small[:, bass.ds(q * 6 + (65 + t * NP * 6), 6)], z[:, t, cols])
                        steps.did(m)
                steps.leave(NP // 2)

            def norm(z, dst, nth, done, *turned):
                steps.wait()
                for t in range(NT):
                    steps.did(nc.vector.bn_aggr(mvar[:, t, :], stats[:, t].rearrange("p q c -> p (q c)")))
                steps.wait()
                nc.vector.tensor_scalar(veps, mvar[:, :, 1], LN_EPS, None, ALU.add).then_inc(var_ready, 1)
                dve.wait_ge(gb_landed, 32 * nth + 32)
                dve.wait_ge(rstd_ready, nth + 1)
                done(z, dst, *turned)

            def by_chunks(z, dst, nth):
                for q in range(NP):
                    cols = slice(q * BANK, (q + 1) * BANK)
                    for t in range(NT):
                        steps.did(nc.vector.scalar_tensor_tensor(out=dst[:, t, cols], in0=z[:, t, cols],
                                                                 scalar=mvar[:, t, 0:1], in1=gain_b[:, cols],
                                                                 op0=ALU.subtract, op1=ALU.mult))
                    steps.wait()
                    for t in range(NT):
                        m = nc.vector.scalar_tensor_tensor(out=dst[:, t, cols], in0=dst[:, t, cols],
                                                           scalar=rstd[:, t:t + 1], in1=bias_b[:, cols],
                                                           op0=ALU.mult, op1=ALU.add)
                    m.then_inc(x_ready, 1)
                    if q:
                        turned_lo((p1, p3), nth, (2 * q - 2, 2 * q - 1))
                turned_lo((p1, p3), nth, (2 * NP - 2, 2 * NP - 1))

            dve.wait_ge(z_landed, 16)
            residual(z1, z1, WO0)
            norm(z1, x1, 0, by_chunks, 16)
            with dve.Fori(MQ0, MQ0 + NP // 2) as pair:
                split_lo(pair, range(4, 20))

            for h in range(MH):
                dve.wait_ge(cs_ready, h + 1)
                chain(nc.vector.tensor_reduce(mx[:, 2 * h:2 * h + 2], ps[:, 4 + h, :].rearrange("p (t m) -> p t m", t=NT),
                                              AX_X, ALU.max))
                nc.vector.tensor_scalar(nmx[:, 2 * h:2 * h + 2], mx[:, 2 * h:2 * h + 2], -M_SCALE, None,
                                        ALU.mult).then_inc(cmax_ready, 1)
            for h in range(MH):
                dve.wait_ge(cp_ready, h + 1)
                chain(nc.vector.reciprocal(rsum[:, 2 * h:2 * h + 2], dsum[:, 2 * h:2 * h + 2]))
                for t in range(NT):
                    m = nc.vector.tensor_scalar(c_p[:, h, t, :], c_p[:, h, t, :], rsum[:, 2 * h + t:2 * h + t + 1], None,
                                                ALU.mult)
                m.then_inc(cn_ready, 1)
            for g in range(KB // 2):
                hi, lo = [r[:, g * 2 * T:(g + 1) * 2 * T] for r in (p1, p3)]
                dve.wait_ge(co_hi, g + 1)
                nc.vector.tensor_tensor(lo, ps[:, 4 + g % 4, :], hi.bitcast(F32), ALU.subtract).then_inc(co_copied, 1)
            residual(x1, x1, MO0)
            norm(x1, x2, 1, by_chunks, 24)

            def ordered(ins):
                dve.drain()

            def copy_scores(t, h):
                ordered(nc.vector.tensor_copy(sc, key_scores[:, t, bass.ds(h * 2 * NKEY, 2 * NKEY)]))

            def top16(values, left, best, where):
                ordered(nc.vector.max(best[:, 0:8], values))
                (nc.vector.max_index(where[:, 0:8], best[:, 0:8], values))
                ordered(nc.vector.match_replace(left, best[:, 0:8], values, NEG_MAX))
                ordered(nc.vector.max(best[:, 8:16], left))
                ordered(nc.vector.max_index(where[:, 8:16], best[:, 8:16], left))

            def retrieve(unit, t, h):
                copy_scores(t, h)
                for n in range(2):
                    c = slice(n * NKEY, (n + 1) * NKEY)
                    top16(sc[:, c], sc_left[:, c], val[:, 16 * n:16 * n + 16], ix[:, 16 * n:16 * n + 16])
                (nc.vector.tensor_copy(ixf, ix))
                grid = lambda a: a.rearrange("p (i j) -> p i j", i=TOPK)
                ordered(nc.vector.tensor_tensor(grid(cand), val[:, 0:16].unsqueeze(2).to_broadcast([P, TOPK, TOPK]),
                                              val[:, 16:32].unsqueeze(1).to_broadcast([P, TOPK, TOPK]), ALU.add))
                top16(cand, cand_left, top, pos)
                nc.vector.tensor_scalar(ntop, top[:, 0:1], -1.0, None, ALU.mult).then_inc(top_ready, 1)
                (nc.vector.tensor_scalar(ij[:, 0:16], pos, 4, None, ALU.logical_shift_right))
                ordered(nc.vector.tensor_scalar(ij[:, 16:32], pos, 15, None, ALU.bitwise_and))
                ordered(nc.vector.tensor_copy(ijf, ij))
                for n in range(2):
                    ordered(nc.vector.tensor_tensor(grid(hot), ijf[:, 16 * n:16 * n + 16].unsqueeze(2).to_broadcast([P, TOPK, TOPK]),
                                                  iota[:, :].unsqueeze(1).to_broadcast([P, TOPK, TOPK]), ALU.is_equal))
                    ordered(nc.vector.tensor_tensor(grid(hot_v), grid(hot),
                                                  ixf[:, 16 * n:16 * n + 16].unsqueeze(1).to_broadcast([P, TOPK, TOPK]),
                                                  ALU.mult))
                    ordered(nc.vector.tensor_reduce(picked[:, 16 * n:16 * n + 16], grid(hot_v), AX_X, ALU.add))
                (nc.vector.scalar_tensor_tensor(out=next_idx[t], in0=picked[:, 0:16], scalar=float(NKEY),
                                                         in1=picked[:, 16:32], op0=ALU.mult, op1=ALU.add))
                if isinstance(unit, int) and unit == 0:
                    dve.drain()
                    hand_over(0)
                dve.wait_ge(gexp_ready, unit + 1)
                ordered(nc.vector.reciprocal(gsum, gsum))
                ordered(nc.vector.tensor_scalar(gate[t], top, gsum, None, ALU.mult))

            def hand_over(t):
                nc.vector.tensor_copy(idx[t], next_idx[t]).then_inc(idx_ready, 1)

            def peer_body(h, last):
                for t in range(NT):
                    unit = h * NT + t
                    for j in range(TOPK):
                        slot = j % NU
                        count = unit * 2 + (j // NU + 1 + u_extra[slot])
                        if isinstance(unit, int) and unit == 0:
                            slot, count = j % EARLY, j // EARLY + 1
                        dve.wait_ge(u_landed[slot], count * 16)
                        m = nc.vector.tensor_tensor_reduce(u_ring[slot], u_ring[slot], x2[:, t, :], 1.0, 0.0,
                                                           ALU.mult, ALU.add, hdot[t][:, j:j + 1])
                        m.then_inc(u_used, 1)
                    dve.wait_ge(u_used, unit * TOPK + TOPK)
                    dve.sem_inc(h_ready, 1)
                    if not (last and t == NT - 1):
                        if not isinstance(unit, int) or unit > 0:
                            dve.wait_ge(v_issued, unit)
                        hand_over(NT - 1 - t)
                    dve.wait_ge(gelu_ready, unit + 1)
                    nc.vector.tensor_tensor(weight[t], act_h[t], gate[t], ALU.mult).then_inc(a_ready, 1)
                    if not last:
                        dve.wait_ge(a_ready, unit + 1)
                        retrieve(unit + NT, t, h + 1)

            dve.wait_ge(ks_copied, 1 + CREDIT)
            for t in range(NT):
                retrieve(t, t, 0)
            peer_body(0, False)
            dve.wait_ge(ks_copied, NP + CREDIT)
            with dve.Fori(1, PH - 1) as h:
                peer_body(h, False)
            peer_body(PH - 1, True)

            for t in range(NT):
                dve.wait_ge(v_used, ((PH - 1) * NT + t + 1) * TOPK + RING_CREDIT)
                chunk = [slice(q * BANK, (q + 1) * BANK) for q in range(NP)]
                for q in range(NP + 1):
                    if q < NP:
                        steps.did(nc.vector.scalar_tensor_tensor(out=x2[:, t, chunk[q]], in0=x2[:, t, chunk[q]], scalar=ALPHA,
                                                                 in1=ps[:, 4 * t + q, :], op0=ALU.mult, op1=ALU.add))
                    if q > 0:
                        steps.wait(but=int(q < NP))
                        steps.did(nc.vector.bn_stats(stats[:, t, q - 1, :], x2[:, t, chunk[q - 1]]))
                steps.wait()
                chain(nc.vector.bn_aggr(mvar[:, t, :], stats[:, t].rearrange("p q c -> p (q c)")))
                nc.vector.tensor_scalar(veps[:, t:t + 1], mvar[:, t, 1:2], LN_EPS, None, ALU.add).then_inc(var_ready, 1)
                dve.wait_ge(gb_landed, 96)
                halves_of = [slice(n * D // 2, (n + 1) * D // 2) for n in range(2)]
                for c in halves_of:
                    steps.did(nc.vector.scalar_tensor_tensor(out=y_out[:, t, c], in0=x2[:, t, c], scalar=mvar[:, t, 0:1],
                                                             in1=gain3_b[:, c], op0=ALU.subtract, op1=ALU.mult))
                dve.wait_ge(rstd_ready, 3 + t)
                for n, c in enumerate(halves_of):
                    steps.wait(but=1 - n)
                    nc.vector.scalar_tensor_tensor(out=y_out[:, t, c], in0=y_out[:, t, c], scalar=rstd[:, t:t + 1],
                                                   in1=bias3_b[:, c], op0=ALU.mult, op1=ALU.add).then_inc(y_ready, 1)


_INS = ["x", "mem", "w_in", "sb_norm_gain", "df_lambda", "df_subln_gain", "w_o", "ln1_gain", "ln1_bias",
        "w_mq", "w_mkv", "w_mo", "ln2_gain", "ln2_bias", "w_pq", "peer_sub_keys", "peer_u", "peer_v",
        "ln3_gain", "ln3_bias"]


def rope_table(tokens, rot):
    import numpy as np

    half = rot // 2
    freq = np.power(np.float32(ROPE_THETA), -np.arange(half, dtype=np.float32) * np.float32(2.0) / np.float32(rot))
    ang = np.arange(tokens, dtype=np.float32)[:, None] * freq.astype(np.float32)[None, :]
    cos, sin = np.cos(ang), np.sin(ang)
    return np.concatenate([cos, cos, -sin, sin], axis=1).astype(np.float32)


def kernel(**inputs):
    import numpy as np
    import concourse.bacc as bacc
    from concourse.bass_utils import run_bass_kernel_spmd as run

    nc = bacc.Bacc("TRN2", target_bir_lowering=False, num_devices=1)
    arrays = {f"in_{n}_dram": np.ascontiguousarray(inputs[n]) for n in _INS}
    _, tokens, width = inputs["x"].shape
    arrays["rope_dram"] = rope_table(tokens, inputs["df_lambda"].shape[2] // 4)
    args = [nc.dram_tensor(n, a.shape, mybir.dt.from_np(a.dtype), kind="ExternalInput").ap()
            for n, a in arrays.items()]
    out = nc.dram_tensor("out_dram", (1, tokens, width), F32, kind="ExternalOutput").ap()
    layer_program(nc, *args, out)
    return run(nc, [arrays], core_ids=[0]).results[0]["out_dram"]
```

```python
import math
from contextlib import ExitStack

import concourse.bass as bass
from concourse import mybir

F32 = mybir.dt.float32
F32R = mybir.dt.float32r
U32 = mybir.dt.uint32
ALU = mybir.AluOpType
ACT = mybir.ActivationFunctionType
AX_X = mybir.AxisListType.X

P = 128
BANK = 512
NEG_BIG = -1.0e30
NEG_MAX = -3.0e38
ROPE_THETA = 500000.0
LAMBDA_INIT = 0.8 - 0.6 * math.exp(-0.3 * 0)
LN_EPS, RMS_EPS = 1e-5, 1e-6
ALPHA = 2.0 ** 0.25


class Steps:

    def __init__(self, eng, sem):
        self.eng, self.sem, self.base, self.n = eng, sem, 0, 0

    def did(self, ins):
        ins.then_inc(self.sem, 1)
        self.n += 1

    def wait(self, but=0):
        self.eng.wait_ge(self.sem, self.base + self.n - but)

    def enter(self, i, per):
        self.start, self.per = self.base + self.n, per
        self.base, self.n = self.start + i * per, 0

    def leave(self, times):
        assert self.n == self.per, (self.n, self.per)
        self.base, self.n = self.start + times * self.per, 0


def layer_program(nc, x, mem, w_in, sb_gain, df_lambda, df_gain, w_o, ln1_g, ln1_b, w_mq, w_mkv,
                  w_mo, ln2_g, ln2_b, w_pq, sub_keys, peer_u, peer_v, ln3_g, ln3_b, rope, out):
    D = x.shape[2]
    NT = x.shape[1] // P
    T = NT * P
    KB = D // P
    SK = 2
    NS = KB // SK
    NP = D // BANK
    SBH, DH = sb_gain.shape[1], sb_gain.shape[2]
    SBW = SBH * DH
    QD = df_lambda.shape[2]
    ROT = rope.shape[1] // 2
    PH = w_pq.shape[2] // (2 * P)
    NKEY = sub_keys.shape[2]
    TOPK = 16
    MH = 4
    MB = KB // MH
    SB_SCALE, DF_SCALE, M_SCALE = DH ** -0.5, QD ** -0.5, (D // MH) ** -0.5
    assert (P, T, KB, NP) == (DH, 2 * P, 16, 4) and NKEY == P and PH == SBH == 8

    x_rows = x[0].rearrange("(t p) n -> p t n", p=P)
    mem_rows = mem[0].rearrange("(t p) n -> p t n", p=P)
    out_rows = out[0].rearrange("(t p) n -> p t n", p=P)

    with ExitStack() as ctx:
        def sb(name, cols, dt=F32):
            return ctx.enter_context(nc.sbuf_tensor(name, [P, cols], dt))

        def sem(name):
            return ctx.enter_context(nc.semaphore(name))

        RC = NT * D
        RAW, SPLIT = 8, 4
        SC = SK * BANK
        base = -(-nc.sbuf_base // 32) * 32
        TEMPS = 5632
        arena = sb("arena", 7 * RC + (RAW + 2 * SPLIT) * SC + TEMPS)

        def at(name, col, cols, dt=F32):
            return nc.alloc_sbuf_tensor_at(name, [P, cols], dt, offset=base + 4 * col)

        r0, r1, r2, r3, r4, r5, r6 = [at(f"region{n}", n * RC, RC) for n in range(7)]
        p0, p1, p3, p4, p6 = [at(f"parts{n}", n * RC, RC, F32R) for n in (0, 1, 3, 4, 6)]
        ring = at("weight_ring", 7 * RC, (RAW + 2 * SPLIT) * SC)
        ta = at("temps", 7 * RC + (RAW + 2 * SPLIT) * SC, TEMPS)
        ta_parts = at("temp_parts", 7 * RC + (RAW + 2 * SPLIT) * SC, TEMPS, F32R)
        split_ring = at("split_ring", 7 * RC + RAW * SC, 2 * SPLIT * SC, F32R)

        def blocks(r):
            return r[:, :].rearrange("p (k t) -> p k t", k=KB)

        def rows(r):
            return r[:, :].rearrange("p (t n) -> p t n", t=NT)

        def parts(hi, lo):
            return [[r[:, k * T:(k + 1) * T] for k in range(KB)] for r in (hi, lo)]

        def mixed_rest(k):
            kind, b, hh = k // SBH, k % SBH // 2, k % 2
            c = kind * D + hh * SBW + b * T
            return p3[:, c:c + T]

        xT = memT = parts(p0, p4)
        mixedT = [parts(p1, p3)[0], [mixed_rest(k) for k in range(KB)]]
        x1T = coT = x2T = parts(p1, p3)
        mixed_lo = p3[:, :].rearrange("p (m h n) -> p m h n", m=2, h=2)
        cqT = blocks(r0)
        sb_v, df_v = rows(r2)[:, :, 0:SBW], rows(r2)[:, :, SBW:D]
        z1 = rows(r0)
        x1 = rows(r2)
        df_qk = rows(r3)
        gain_b, bias_b = r4[:, 0:D], r4[:, D:2 * D]
        x_in, mkT, x2 = rows(r5), blocks(r5), rows(r5)
        mem_in, mv, key_scores = rows(r6), rows(r6), rows(r6)

        def slots(r, n, first=0):
            return [r[:, (first + s) * SC:(first + s + 1) * SC] for s in range(n)]

        raw, w_hi, w_lo = slots(ring, RAW), slots(split_ring, SPLIT), slots(split_ring, SPLIT, SPLIT)
        halves = lambda r: [r[:, 0:D], r[:, D:2 * D]]
        in_ring = [ring[:, s * D:(s + 1) * D] for s in range(8)]
        u_ring = [halves(r0) + halves(r2) + halves(r4) + in_ring[0:2], in_ring[2:8] + in_ring[0:2]]
        experts = [at("experts_of_tile0", RC, 4 * RC), at("experts_of_tile1", 7 * RC, 4 * RC)]
        HALF, QTR = D // 2, D // 4
        v_raw = [r0[:, s * HALF:(s + 1) * HALF] for s in range(4)]
        v_hi, v_lo = [[p6[:, (4 * n + s) * QTR:(4 * n + s + 1) * QTR] for s in range(4)] for n in range(2)]
        e_hi, e_lo = [[ta_parts[:, 2048 + (2 * n + s) * T:2048 + (2 * n + s + 1) * T] for s in range(2)]
                      for n in range(2)]
        gain3_b, bias3_b = ta[:, 0:D], ta[:, 3072:3072 + D]
        NU = 8
        POOLS = 5
        EARLY = 6
        u_extra = [len(range(s, TOPK, EARLY)) * (s < EARLY) - TOPK // NU for s in range(NU)]
        y_out = rows(r0)

        ident = sb("ident", P)
        before = sb("before", P)
        neg_after = sb("neg_after", P)
        neg_ones = sb("neg_ones", P)
        causal = sb("causal", T)
        rope_cs = sb("rope_cs", NT * 2 * ROT)
        sbg = sb("sbg", SBW)
        dfg = sb("dfg", DH)
        keysT = sb("keysT", 2 * NKEY)
        iota = sb("iota", TOPK)
        small = sb("small", 128)

        cos2 = rope_cs[:, :].rearrange("p (t c) -> p t c", t=NT)[:, :, 0:ROT]
        sin2 = rope_cs[:, :].rearrange("p (t c) -> p t c", t=NT)[:, :, ROT:2 * ROT]
        HR = ROT // 2
        k_st = ta[:, 0:512]
        df_st = ta[:, 512:1536].rearrange("p (t q c) -> p t q c", t=NT, q=2)
        ZC = 3 * P
        e_z = [ta[:, 1536 + n * ZC:1536 + (n + 1) * ZC] for n in range(2)]
        sp_z = [ta[:, 2304 + n * ZC:2304 + (n + 1) * ZC] for n in range(2)]
        sb_n = ta[:, 1536:2048].rearrange("p (b c) -> p b c", b=4)
        dfT = [ta[:, 3072 + n * 512:3584 + n * 512] for n in range(2)]
        pT = [ta[:, 3072 + n * 512:3072 + n * 512 + ZC] for n in range(2)]
        s_t0 = ta[:, 4096:4608].rearrange("p (b c) -> p b c", b=4)
        df_n = ta[:, 4096:4608].rearrange("p (b c) -> p b c", b=4)
        s_t1 = [ta[:, 4608 + n * 512:5120 + n * 512].rearrange("p (s c) -> p s c", s=2) for n in range(2)]
        whole = [ta[:, 2048 + n * 512:2560 + n * 512] for n in range(4)]
        c_p = ta[:, 0:MH * NT * T].rearrange("p (h t m) -> p h t m", h=MH, t=NT)
        c_pT = ta[:, 2048:4096].rearrange("p (h m q) -> p h m q", h=MH, m=NT)
        pq_st = [ta[:, s * 1024:1024 + s * 1024].rearrange("p (b t) -> p b t", b=4) for s in range(2)]
        keys_in = ta[:, 0:2 * NKEY]
        OH = 8
        POOL_IW, ACT_J = (0, 3, 6, 9, 13), range(12, 16)
        hot_j = [ta[:, s * P:(s + 1) * P] for s in range(OH)]
        hot_iw = [ta[:, (OH + s) * P:(OH + s + 1) * P] for s in range(OH)]
        WIJ = 3
        wij = [[ta[:, 4096 + (WIJ * t + n) * P:4096 + (WIJ * t + n + 1) * P] for n in range(WIJ)] for t in range(NT)]
        wijT = [ta[:, 4864 + WIJ * t * P:4864 + WIJ * (t + 1) * P].rearrange("p (n c) -> p n c", n=WIJ)
                for t in range(NT)]
        wijT_now = [keysT[:, n * 48:(n + 1) * 48].rearrange("p (n c) -> p n c", n=WIJ) for n in range(2)]
        count = neg_ones
        tk = ta[:, 2048:5632]
        sc, sc_left = tk[:, 0:256], tk[:, 256:512]
        cand, cand_left = tk[:, 512:768], tk[:, 768:1024]
        hot, hot_v = tk[:, 1024:1280], tk[:, 1280:1536]
        val = tk[:, 1536:1568]
        ixf = tk[:, 1568:1600]
        top = tk[:, 1600:1616]
        ijf = tk[:, 1616:1648]
        picked = tk[:, 1648:1680]
        gate = [tk[:, 1680 + 16 * t:1696 + 16 * t] for t in range(NT)]
        hdot = [tk[:, 1712 + 16 * t:1728 + 16 * t] for t in range(NT)]
        act_h = [tk[:, 1744 + 16 * t:1760 + 16 * t] for t in range(NT)]
        gsum, ntop = tk[:, 1808:1809], tk[:, 1809:1810]
        ints = tk[:, 1856:2048].bitcast(U32)
        ix, pos, ij = ints[:, 0:32], ints[:, 32:48], ints[:, 48:80]
        idx_all = ints[:, 112:144]
        idx = [idx_all[:, 16 * t:16 * t + 16] for t in range(NT)]

        lam_in = ta[:, 0:4 * QD]
        lam_pr = ta[:, 4 * QD:5 * QD]
        neg_lam = small[:, 0:1]
        lam_s = small[:, 1:3]
        lam_e = small[:, 3:5]
        nhalf = small[:, 5:9]
        ss, rs = small[:, 9:13], small[:, 13:17]
        dss, drs = small[:, 17:21], small[:, 21:25]
        mx, nmx, dsum, rsum, c2 = [small[:, 25 + 8 * n:33 + 8 * n] for n in range(5)]
        stats = small[:, 65:113].rearrange("p (t q c) -> p t q c", t=NT, c=6)
        mvar = small[:, 113:117].rearrange("p (t c) -> p t c", t=NT)
        veps, rstd = small[:, 117:119], small[:, 119:121]

        ps = ctx.enter_context(nc.psum_tensor("ps", [P, 8, BANK], F32))

        def bank(b, n=1):
            return ps[:, b:b + n, :].rearrange("p b c -> p (b c)")

        x_landed = [sem(f"x_landed{q}") for q in range(NP)]
        mem_landed, small_landed = sem("mem_landed"), sem("small_landed")
        w_landed = [sem(f"w_landed{s}") for s in range(RAW)]
        hi_ready, lo_ready, w_used = sem("hi_ready"), sem("lo_ready"), sem("w_used")
        pool_step, dve_step, act_step = sem("pool_step"), sem("dve_step"), sem("act_step")
        consts_ready = sem("consts_ready")
        turned, turned_hi, turned_taken = sem("turned"), sem("turned_hi"), sem("turned_taken")
        turned_lo_ready = sem("turned_lo_ready")
        proj_taken = sem("proj_taken")
        roped = sem("roped")
        k_staged, df_staged = sem("k_staged"), sem("df_staged")
        z_ready, dfT_ready, dfT_copied = sem("z_ready"), sem("dfT_ready"), sem("dfT_copied")
        e_ready, sp_ready = sem("e_ready"), sem("sp_ready")
        s_ready, stick_ready = sem("s_ready"), sem("stick_ready")
        smax_ready, p_ready, wexp_in, wexp_out = sem("smax_ready"), sem("p_ready"), sem("wexp_in"), sem("wexp_out")
        w_ready, pw_ready = sem("w_ready"), sem("pw_ready")
        o_ready, pT_ready, pT_copied = sem("o_ready"), sem("pT_ready"), sem("pT_copied")
        ss_ready, ms_ready, rms_ready, o_normed = sem("ss_ready"), sem("ms_ready"), sem("rms_ready"), sem("o_normed")
        do_ready, oT_ready, oT_hi, oT_copied = sem("do_ready"), sem("oT_ready"), sem("oT_hi"), sem("oT_copied")
        z_landed, gb_landed = sem("z_landed"), sem("gb_landed")
        var_ready, rstd_ready, x_ready = sem("var_ready"), sem("rstd_ready"), sem("x_ready")
        cs_ready, cmax_ready, cp_ready, cn_ready = sem("cs_ready"), sem("cmax_ready"), sem("cp_ready"), sem("cn_ready")
        cT_ready, cT_copied = sem("cT_ready"), sem("cT_copied")
        co_ready, co_hi, co_copied = sem("co_ready"), sem("co_hi"), sem("co_copied")
        keys_landed, keysT_ready, keysT_copied = sem("keys_landed"), sem("keysT_ready"), sem("keysT_copied")
        ks_ready, ks_copied = sem("ks_ready"), sem("ks_copied")
        top_ready, gexp_ready, idx_ready = sem("top_ready"), sem("gexp_ready"), sem("idx_ready")
        u_landed = [sem(f"u_landed{s}") for s in range(NU)]
        u_used, prod_ready, u_summed = sem("u_used"), sem("prod_ready"), sem("u_summed")
        wij_turned, wijT_ready, now_ready = sem("wij_turned"), sem("wijT_ready"), sem("now_ready")
        j_act, j_dve, iw_pool, iw_dve = sem("j_act"), sem("j_dve"), sem("iw_pool"), sem("iw_dve")
        e_placed, e_copied = sem("e_placed"), sem("e_copied")
        v_landed = [sem(f"v_landed{s}") for s in range(4)]
        e_hi_ready, e_lo_ready, v_hi_ready, v_lo_ready = sem("e_hi_ready"), sem("e_lo_ready"), sem("v_hi_ready"), sem("v_lo_ready")
        v_used = sem("v_used")
        waited = sem("waited")
        h_ready, gelu_ready, a_ready = sem("h_ready"), sem("gelu_ready"), sem("a_ready")
        y_ready, y_stored = sem("y_ready"), sem("y_stored")

        PS = 2 * NS
        IN_PAIRS = w_in.shape[2] // (2 * BANK)
        MKV0 = IN_PAIRS
        WO0 = MKV0 + w_mkv.shape[2] // (2 * BANK)
        MQ0 = WO0 + NP // 2
        MO0 = MQ0 + NP // 2
        PQ0 = MO0 + NP // 2
        BODIES = SBH // 2
        CREDIT = 2
        UNITS = NT * PH

        def dots(unit, j):
            if isinstance(unit, int) and unit == 0:
                return j + 1
            mine = [i for i in range(TOPK) if i % NU != POOLS]
            return (unit - 1) * len(mine) + (TOPK + sum(i <= j for i in mine))

        def sums(unit, j):
            return (unit - 1) * (TOPK // NU) + (j // NU + 1)


        block = ctx.enter_context(nc.Block())

        @block.sync
        def _(sp):
            def load_x(qs):
                for q in qs:
                    cols = slice(q * BANK, (q + 1) * BANK)
                    sp.dma_start(x_in[:, :, cols], x_rows[:, :, cols]).then_inc(x_landed[q], 16)

            def load_pair(w, i, pair, first=False):
                for j in range(PS):
                    if not (first and j < RAW):
                        sp.wait_ge(lo_ready, pair * PS + (j + 1 - RAW))
                    cols = w[0][:, bass.ds(i * 2 * BANK + (j // NS) * BANK, BANK)]
                    src = cols.rearrange("(s k p) n -> s p k n", s=NS, p=P)[j % NS]
                    dst = raw[j % RAW].rearrange("p (k n) -> p k n", k=SK)
                    sp.dma_start(dst, src).then_inc(w_landed[j % RAW], 16)
                    if first and j == 1:
                        load_x(range(2, NP))

            load_x(range(2))
            load_pair(w_in, 0, 0, first=True)
            sp.dma_start(mem_in, mem_rows).then_inc(mem_landed, 16)
            with sp.Fori(1, IN_PAIRS) as i:
                load_pair(w_in, i, i)
            for w, first_pair in ((w_mkv, MKV0), (w_o, WO0), (w_mq, MQ0), (w_mo, MO0), (w_pq, PQ0)):
                with sp.Fori(0, w.shape[2] // (2 * BANK)) as i:
                    load_pair(w, i, i + first_pair)
            def load_v(i, b, first=False):
                for n in range(2):
                    if not first:
                        sp.wait_ge(v_lo_ready, i * 4 + (2 * n + 2 - 8))
                    sp.dma_start(v_raw[2 * b + n], peer_v[0][bass.ds(i * NKEY, NKEY), n * HALF:(n + 1) * HALF])\
                        .then_inc(v_landed[2 * b + n], 16)

            sp.wait_ge(u_used, dots(PH, 0))
            for b in range(2):
                load_v(b, b, first=True)
            with sp.Fori(1, NKEY // 2) as i:
                for b in range(2):
                    load_v(i * 2 + b, b)
            for n in range(2 * NT):
                t, cols = n // 2, slice(n % 2 * D // 2, (n % 2 + 1) * D // 2)
                sp.wait_ge(y_ready, n + 1)
                sp.dma_start(out_rows[:, t, cols], y_out[:, t, cols]).then_inc(y_stored, 16)
            sp.wait_ge(y_stored, 16 * 2 * NT)

        @block.tensor
        def _(pe):
            def turn(src, group, nth):
                if nth >= 4:
                    pe.wait_ge(turned_taken, nth - 3)
                for k in (2 * group, 2 * group + 1):
                    for t in range(NT):
                        c = (k % 2) * T + t * P
                        m = nc.tensor.transpose(ps[:, 4 + nth % 4, c:c + P], src[:, t, k * P:(k + 1) * P], ident[:, :])
                m.then_inc(turned, 1)

            def slices(kind, js, pair, acts, par, spare):
                b0 = 2 * par
                for j in js:
                    if j % NS == 0:
                        pe.wait_ge(proj_taken, pair * 2 + j // NS + CREDIT - spare)
                    pe.wait_ge(lo_ready, pair * PS + j + 1)
                    hi, lo = w_hi[j % SPLIT], w_lo[j % SPLIT]
                    for k in range(SK):
                        kk = j % NS * SK + k
                        a_hi, a_lo = acts[0][kk], acts[1][kk]
                        first, last = kk == 0, kk == KB - 1
                        if kind == "rows":
                            for t in range(NT):
                                for n, (a, w) in enumerate(((a_hi, hi), (a_hi, lo), (a_lo, hi))):
                                    m = nc.tensor.matmul(ps[:, b0 + t, :], a[:, t * P:(t + 1) * P],
                                                         w[:, k * BANK:(k + 1) * BANK],
                                                         start=first and n == 0, stop=last and n == 2)
                        else:
                            for nb in range(4):
                                for n, (a, w) in enumerate(((a_hi, hi), (a_lo, hi), (a_hi, lo))):
                                    m = nc.tensor.matmul(ps[:, b0 + nb // 2, (nb % 2) * T:(nb % 2 + 1) * T],
                                                         w[:, k * BANK + nb * P:k * BANK + (nb + 1) * P], a,
                                                         start=first and nb % 2 == 0 and n == 0,
                                                         stop=last and nb % 2 == 1 and n == 2,
                                                         skip_group_check=True)
                    m.then_inc(w_used, 1)

            def panel(kind, s, pair, acts):
                slices(kind, range(s * NS, (s + 1) * NS), pair, acts, s, 1)

            def section(kind, first_pair, pairs, acts):
                with pe.Fori(first_pair, first_pair + pairs) as pair:
                    for s in range(2):
                        panel(kind, s, pair, acts)

            def rest_of_pair(pair, acts):
                slices("cols", range(4, NS), pair, acts, 0, 1)
                panel("cols", 1, pair, acts)

            pe.wait_ge(consts_ready, 1)
            for g in range(8):
                if g % 2 == 0:
                    pe.wait_ge(x_landed[g // 2], 16)
                turn(x_in, g, g)
                if g == 3:
                    pe.wait_ge(turned_taken, 4)
                    slices("cols", range(2), 0, xT, 0, 1)
            slices("cols", range(2, 4), 0, xT, 0, 1)
            pe.wait_ge(turned_taken, 8)
            rest_of_pair(0, xT)
            section("cols", 1, 1, xT)
            section("rows", 2, 4, xT)
            pe.wait_ge(mem_landed, 16)
            for g in range(8):
                turn(mem_in, g, 8 + g)
            pe.wait_ge(turned_taken, 16)

            def attention_body(b, kind):
                pair = b + MKV0
                pe.wait_ge(k_staged, b + 1)
                pe.wait_ge(oT_copied, b * 2 - 1 + CREDIT)
                for hh in range(2):
                    q0 = (b * 2 + hh) * T
                    nc.tensor.matmul(ps[:, 2 + hh, 0:T], k_st[:, hh * T:hh * T + P], r1[:, bass.ds(q0, T)],
                                     start=True, stop=True)
                    nc.tensor.matmul(ps[:, 2 + hh, T:ZC], k_st[:, hh * T + P:(hh + 1) * T], r1[:, bass.ds(q0 + P, P)],
                                     start=True, stop=True).then_inc(z_ready, 1)
                pe.wait_ge(df_staged, b + 1)
                pe.wait_ge(pT_copied, b * 2 + CREDIT)
                for hh in range(2):
                    for q in range(2):
                        for t in range(NT):
                            m = nc.tensor.transpose(ps[:, 4 + hh, (q * NT + t) * P:(q * NT + t + 1) * P],
                                                    df_st[:, t, q, hh * P:(hh + 1) * P], ident[:, :])
                    m.then_inc(dfT_ready, 1)
                slices(kind, range(0, 4), pair, memT, 0, 0)
                pe.wait_ge(dfT_copied, b * 2 + 2)
                pe.wait_ge(o_normed, b * 2 + CREDIT)
                pe.wait_ge(oT_copied, b * 2 + CREDIT)
                for hh in range(2):
                    for st in range(2):
                        q = dfT[hh][st * QD:(st + 1) * QD, :]
                        nc.tensor.matmul(ps[:, 4 + st, hh * T:(hh + 1) * T], q[:, P:2 * P], q[:, T:2 * T],
                                         start=True, stop=True)
                        m = nc.tensor.matmul(ps[:, 6 + st, hh * P:(hh + 1) * P], q[:, 0:P], q[:, T:T + P],
                                             start=True, stop=True)
                m.then_inc(s_ready, 1)
                for hh in range(2):
                    pe.wait_ge(sp_ready, b * 2 + hh + 1)
                    nc.tensor.matmul(ps[:, 2 + hh, 0:ZC], neg_after[:, :], sp_z[hh], start=True, stop=False,
                                     skip_group_check=True)
                    nc.tensor.matmul(ps[:, 2 + hh, P:T], neg_ones[:, :], sp_z[hh][:, T:ZC], start=False, stop=True,
                                     skip_group_check=True).then_inc(stick_ready, 1)
                slices(kind, range(4, 8), pair, memT, 0, 0)
                for hh in range(2):
                    pe.wait_ge(w_ready, b * 2 + hh + 1)
                    v0 = (b * 2 + hh) * DH
                    w = sp_z[hh]
                    nc.tensor.matmul(ps[:, 7, hh * T:hh * T + P], w[:, 0:P], r2[:, bass.ds(v0, DH)], start=True, stop=True)
                    nc.tensor.matmul(ps[:, 7, hh * T + P:(hh + 1) * T], w[:, P:T], r2[:, bass.ds(v0, DH)],
                                     start=True, stop=False)
                    m = nc.tensor.matmul(ps[:, 7, hh * T + P:(hh + 1) * T], w[:, T:ZC], r2[:, bass.ds(v0 + D, DH)],
                                         start=False, stop=True)
                m.then_inc(o_ready, 1)
                for hh in range(2):
                    pe.wait_ge(pw_ready, b * 2 + hh + 1)
                    for c, src in enumerate((s_t0[:, 2 * hh, :], s_t1[hh][:, 0, 0:P], s_t1[hh][:, 0, P:T])):
                        m = nc.tensor.transpose(ps[:, 4 + hh, c * P:(c + 1) * P], src, ident[:, :])
                    m.then_inc(pT_ready, 1)
                slices(kind, range(8, 12), pair, memT, 0, 0)
                for hh in range(2):
                    pe.wait_ge(pT_copied, b * 2 + hh + 1 + CREDIT)
                    v0 = (b * 2 + hh) * DH + SBW
                    nc.tensor.matmul(ps[:, 6, hh * T:hh * T + P], pT[hh][:, 0:P], r2[:, bass.ds(v0, DH)],
                                     start=True, stop=True)
                    nc.tensor.matmul(ps[:, 6, hh * T + P:(hh + 1) * T], pT[hh][:, P:T], r2[:, bass.ds(v0, DH)],
                                     start=True, stop=False)
                    m = nc.tensor.matmul(ps[:, 6, hh * T + P:(hh + 1) * T], pT[hh][:, T:ZC],
                                         r2[:, bass.ds(v0 + D, DH)], start=False, stop=True)
                m.then_inc(do_ready, 1)
                pe.wait_ge(o_normed, b * 2 + 1 + CREDIT)
                for c in range(4):
                    m = nc.tensor.transpose(ps[:, 2, c * P:(c + 1) * P], sb_n[:, c, :], ident[:, :])
                m.then_inc(oT_ready, 1)
                slices(kind, range(12, 16), pair, memT, 0, 0)
                pe.wait_ge(o_normed, b * 2 + 2 + CREDIT)
                for c in range(4):
                    m = nc.tensor.transpose(ps[:, 7, c * P:(c + 1) * P], df_n[:, c, :], ident[:, :])
                m.then_inc(oT_ready, 1)

            with pe.Fori(0, BODIES // 2) as b:
                attention_body(b, "cols")
            with pe.Fori(BODIES // 2, BODIES) as b:
                attention_body(b, "rows")
            pe.wait_ge(oT_copied, 2 * BODIES + CREDIT)
            pe.wait_ge(proj_taken, 2 * WO0 + CREDIT)
            section("rows", WO0, NP // 2, mixedT)

            def turn_norm(src, nth, first_chunk, pair, acts):
                for g in range(8):
                    if g % 2 == 0:
                        pe.wait_ge(x_ready, first_chunk + g // 2 + 1)
                    turn(src, g, nth + g)
                    if g in (3, 7):
                        pe.wait_ge(turned_lo_ready, nth - 16 + g // 2 + 1)
                        slices("cols", range(g // 2 - 1, g // 2 + 1), pair, acts, 0, 1)
                pe.wait_ge(turned_taken, nth + 8)
                pe.wait_ge(turned_lo_ready, nth - 8)

            turn_norm(x1, 16, 0, MQ0, x1T)
            rest_of_pair(MQ0, x1T)
            section("cols", MQ0 + 1, NP // 2 - 1, x1T)
            pe.wait_ge(proj_taken, 2 * MO0 + CREDIT)
            for h in range(MH):
                for t in range(NT):
                    for kb in range(MB):
                        m = nc.tensor.matmul(ps[:, 4 + h, t * T:(t + 1) * T], cqT[:, h * MB + kb, t * P:(t + 1) * P],
                                             mkT[:, h * MB + kb, :], start=kb == 0, stop=kb == MB - 1)
                m.then_inc(cs_ready, 1)
            for h in range(MH):
                pe.wait_ge(cn_ready, h + 1)
                for m_t in range(NT):
                    for t in range(NT):
                        m = nc.tensor.transpose(ps[:, h, m_t * T + t * P:m_t * T + (t + 1) * P],
                                                c_p[:, h, t, m_t * P:(m_t + 1) * P], ident[:, :])
                m.then_inc(cT_ready, 1)
            for g in range(KB // 2):
                if g % (MB // 2) == 0:
                    pe.wait_ge(cT_copied, g // (MB // 2) + 1)
                if g >= 4:
                    pe.wait_ge(co_copied, g - 3)
                for n in range(2):
                    blk = 2 * g + n
                    for m_t in range(NT):
                        m = nc.tensor.matmul(ps[:, 4 + g % 4, n * T:(n + 1) * T], mv[:, m_t, blk * P:(blk + 1) * P],
                                             c_pT[:, blk // MB, m_t, :], start=m_t == 0, stop=m_t == NT - 1)
                m.then_inc(co_ready, 1)
            pe.wait_ge(co_copied, KB // 2)
            section("rows", MO0, NP // 2, coT)
            pe.wait_ge(keys_landed, 16)
            for n in range(2):
                m = nc.tensor.transpose(ps[:, 7, n * P:(n + 1) * P], keys_in[:, n * NKEY:(n + 1) * NKEY], ident[:, :])
            m.then_inc(keysT_ready, 1)
            pe.wait_ge(keysT_copied, 1)
            turn_norm(x2, 24, 4, PQ0, x2T)

            def key_products(pair, s):
                pe.wait_ge(proj_taken, pair * 2 + s + 1 + CREDIT)
                pe.wait_ge(ks_copied, pair * 2 + s - 2 * PQ0 + CREDIT - 1)
                for t in range(NT):
                    for n in range(4):
                        m = nc.tensor.matmul(ps[:, 4 + 2 * s + t, n * P:(n + 1) * P], pq_st[s][:, n, t * P:(t + 1) * P],
                                             keysT[:, (n % 2) * NKEY:(n % 2 + 1) * NKEY], start=True, stop=True)
                m.then_inc(ks_ready, 1)

            for pair in range(PQ0, PQ0 + NP // 2):
                slices("cols", range(4 if pair == PQ0 else 0, NS), pair, x2T, 0, 1)
                slices("cols", range(8, 10), pair, x2T, 1, 1)
                key_products(pair, 0)
                slices("cols", range(10, 16), pair, x2T, 1, 1)
                key_products(pair, 1)

            def turn_wij(t):
                pe.wait_ge(a_ready, (t + 1) * PH)
                for n in range(WIJ):
                    m = nc.tensor.transpose(ps[:, 4, n * P:(n + 1) * P], wij[t][n], ident[:, :])
                m.then_inc(wij_turned, 1)

            def products(t, q, b, first=False):
                c = slice(t * P, (t + 1) * P)
                for n, (e, v) in enumerate(((e_hi[b], v_hi[q]), (e_hi[b], v_lo[q]), (e_lo[b], v_hi[q]))):
                    m = nc.tensor.matmul(ps[:, 4 * t + q, :], e[:, c], v, start=first and n == 0, stop=False,
                                         skip_group_check=True)
                return m

            def last_block(i, b):
                pe.wait_ge(e_lo_ready, i + 1)
                for t in range(NT):
                    for q in range(4):
                        if t == 0:
                            pe.wait_ge(v_lo_ready, i * 4 + (q + 1))
                        m = products(t, q, b)
                    m.then_inc(v_used, 2)

            def mix_block(i, b, first=False):
                for q in range(4):
                    if q == 0:
                        pe.wait_ge(e_lo_ready, i + 1)
                    pe.wait_ge(v_lo_ready, i * 4 + (q + 1))
                    for t in range(NT):
                        m = products(t, q, b, first)
                    m.then_inc(v_used, 1)

            turn_wij(0)
            def place(t, n, hot_wait):
                for m in range(TOPK):
                    if m % 4 == 0:
                        pe.wait_ge(e_copied, n * 4 + (t * P // 4 + m // 4 + 1))
                    hot_wait(n, m)
                    nc.tensor.matmul(ps[:, m // 4, m % 4 * P:(m % 4 + 1) * P], hot_j[m % OH], hot_iw[m % OH],
                                     start=True, stop=True).then_inc(e_placed, 1)

            def tile0_hot(n, m):
                pe.wait_ge(j_act, n * TOPK + (m + 1))
                pe.wait_ge(iw_pool, n * TOPK + (m + 1))

            def tile1_hot(n, m):
                if m in ACT_J:
                    pe.wait_ge(j_act, n * len(ACT_J) + (P + m - ACT_J[0] + 1))
                elif m % 4 == 0:
                    pe.wait_ge(j_dve, n * 3 + (m // 4 + 1))
                upto = sum(i <= m for i in POOL_IW)
                if m in POOL_IW:
                    pe.wait_ge(iw_pool, n * len(POOL_IW) + (P + upto))
                else:
                    pe.wait_ge(iw_dve, n * (TOPK - len(POOL_IW)) + (m + 1 - upto))

            with pe.Fori(0, PH) as n:
                place(0, n, tile0_hot)
            turn_wij(1)
            with pe.Fori(0, PH) as n:
                place(1, n, tile1_hot)
            pe.wait_ge(e_copied, 2 * P // 4 + 4)
            for b in range(2):
                mix_block(b, b, first=b == 0)
            with pe.Fori(1, NKEY // 2 - 1) as i:
                for b in range(2):
                    mix_block(i * 2 + b, b)
            mix_block(NKEY - 2, 0)
            last_block(NKEY - 1, 1)

        @block.scalar
        def _(act):
            steps = Steps(act, act_step)
            act.dma_start(rope_cs[:, :].rearrange("p (t c) -> p t c", t=NT),
                          rope.rearrange("(t p) c -> p t c", p=P)).then_inc(small_landed, 16)
            act.dma_start(lam_in, df_lambda[0].rearrange("a d -> (a d)").partition_broadcast(P)).then_inc(small_landed, 16)
            act.dma_start(sbg[:, :], sb_gain[0].rearrange("h d -> (h d)").partition_broadcast(P)).then_inc(small_landed, 16)
            act.dma_start(dfg[:, :], df_gain[0].partition_broadcast(P)).then_inc(small_landed, 16)
            act.sem_inc(proj_taken, CREDIT)
            act.sem_inc(ks_copied, CREDIT)
            act.sem_inc(oT_copied, CREDIT)
            act.sem_inc(e_copied, 4)
            act.sem_inc(e_placed, OH)
            act.sem_inc(pT_copied, CREDIT)

            def copy_turned(dst, nth, groups):
                for g in groups:
                    act.wait_ge(turned, nth + g + 1)
                    nc.scalar.activation(dst[:, g * 2 * T:(g + 1) * 2 * T], ps[:, 4 + (nth + g) % 4, :],
                                         ACT.Copy).then_inc(turned_hi, 1)

            def copy_turned_whole(dst, nth):
                for g in range(8):
                    act.wait_ge(turned, nth + g + 1)
                    nc.scalar.activation(dst[:, g * 2 * T:(g + 1) * 2 * T], ps[:, 4 + g % 4, :], ACT.Copy)\
                        .then_inc(turned_hi, 1)
                    if nth + g - 16 >= 4:
                        act.wait_ge(turned_lo_ready, nth + g - 16 - 3)
                    nc.scalar.activation(whole[g % 4], ps[:, 4 + g % 4, :], ACT.Copy).then_inc(turned_taken, 1)

            def split_hi(pair, js, start=False):
                for j in js:
                    act.wait_ge(w_landed[j % RAW], (pair * (PS // RAW) + j // RAW) * 16 + 16)
                    if not start:
                        act.wait_ge(w_used, pair * PS + (j + 1 - SPLIT))
                    nc.scalar.activation(w_hi[j % SPLIT], raw[j % RAW], ACT.Copy).then_inc(hi_ready, 1)

            def take(kind, dst, col, pair, s, b0):
                act.wait_ge(w_used, pair * PS + (s + 1) * NS)
                if kind == "rows":
                    nc.scalar.activation(dst[:, :, bass.ds(col, BANK)], ps[:, b0:b0 + 2, :],
                                         ACT.Copy).then_inc(proj_taken, 1)
                else:
                    nc.scalar.activation(dst[:, bass.ds(col, 2 * BANK)], bank(b0, 2), ACT.Copy).then_inc(proj_taken, 1)

            def split_pair(pair, take_panel=lambda s: None):
                for s in range(2):
                    split_hi(pair, range(4 + 8 * s, 11 + 8 * s))
                    take_panel(s)
                    split_hi(pair, [11 + 8 * s])

            def section(kind, dst, first_pair, pairs, width=BANK):
                with act.Fori(0, pairs) as i:
                    split_pair(i + first_pair,
                               lambda s: take(kind, dst, (i * 2 + s) * width, i + first_pair, s, 2 * s))

            for n in range(2):
                copy_turned(p0, 0, range(4 * n, 4 * n + 4))
                split_hi(0, range(2 * n, 2 * n + 2), start=True)
            act.wait_ge(roped, 1)
            nc.scalar.activation(lam_e, lam_s, ACT.Exp).then_inc(roped, 1)
            section("cols", r1, 0, 2, 2 * BANK)
            section("rows", sb_v, 2, 1)
            section("rows", df_qk, 3, 2)
            section("rows", df_v, 5, 1)
            copy_turned(p0, 8, range(8))

            def attention_body(b, kind):
                for hh in range(2):
                    act.wait_ge(dfT_ready, b * 2 + hh + 1)
                    nc.scalar.activation(dfT[hh], ps[:, 4 + hh, :], ACT.Copy).then_inc(dfT_copied, 1)
                pair = b + MKV0
                for hh in range(2):
                    act.wait_ge(z_ready, b * 2 + hh + 1)
                    for dst, src, func, scale in ((e_z[hh], ps[:, 2 + hh, 0:ZC], ACT.Copy, SB_SCALE),
                                                  (sp_z[hh], e_z[hh], ACT.Abs, 1.0), (sp_z[hh], sp_z[hh], ACT.Exp, -1.0)):
                        steps.did(nc.scalar.activation(dst, src, func, scale=scale))
                        steps.wait()
                    nc.scalar.activation(sp_z[hh], sp_z[hh], ACT.Ln, bias=1.0).then_inc(e_ready, 1)
                    split_hi(pair, (4 + 2 * hh, 5 + 2 * hh))
                act.wait_ge(smax_ready, b + 1)
                for hh in range(2):
                    for st in range(2):
                        n = 2 * hh + st
                        nc.scalar.activation(s_t0[:, n, :], s_t0[:, n, :], ACT.Exp, bias=nmx[:, n:n + 1],
                                             scale=DF_SCALE, accum_out=dsum[:, n:n + 1])
                        m = nc.scalar.activation(s_t1[hh][:, st, :], s_t1[hh][:, st, :], ACT.Exp,
                                                 bias=nmx[:, 4 + n:5 + n], scale=DF_SCALE,
                                                 accum_out=dsum[:, 4 + n:5 + n])
                m.then_inc(p_ready, 1)
                for hh in range(2):
                    act.wait_ge(wexp_in, b * 2 + hh + 1)
                    nc.scalar.activation(sp_z[hh], e_z[hh], ACT.Exp).then_inc(wexp_out, 1)
                dst, width = (r5, 2 * BANK) if kind == "cols" else (mv, BANK)
                i = b if kind == "cols" else b - BODIES // 2
                split_hi(pair, range(8, 11))
                take(kind, dst, i * 2 * width, pair, 0, 0)
                split_hi(pair, [11])
                act.wait_ge(o_ready, b + 1)
                for c in range(4):
                    m = nc.scalar.activation(sb_n[:, c, :], ps[:, 7, c * P:(c + 1) * P], ACT.Square,
                                             accum_out=ss[:, c:c + 1])
                m.then_inc(ss_ready, 1)
                for hh in range(2):
                    act.wait_ge(pT_ready, b * 2 + hh + 1)
                    nc.scalar.activation(pT[hh], ps[:, 4 + hh, 0:ZC], ACT.Copy).then_inc(pT_copied, 1)
                split_hi(pair, range(12, 16))
                act.wait_ge(do_ready, b + 1)
                for c in range(4):
                    m = nc.scalar.activation(s_t1[c // 2][:, 1, (c % 2) * P:(c % 2 + 1) * P], ps[:, 6, c * P:(c + 1) * P], ACT.Square,
                                             accum_out=dss[:, c:c + 1])
                m.then_inc(ss_ready, 1)
                act.wait_ge(oT_ready, b * 2 + 1)
                nc.scalar.activation(p1[:, bass.ds(b * 2 * T, 2 * T)], ps[:, 2, :], ACT.Copy).then_inc(oT_hi, 1)
                split_hi(pair, range(16, 19))
                take(kind, dst, i * 2 * width + width, pair, 1, 0)
                split_hi(pair, [19])
                act.wait_ge(oT_ready, b * 2 + 2)
                nc.scalar.activation(p1[:, bass.ds(b * 2 * T + SBH * T, 2 * T)], ps[:, 7, :],
                                     ACT.Copy).then_inc(oT_hi, 1)

            act.preload_act_table_set("natural_log_exp_and_others")
            for first, kind in ((0, "cols"), (BODIES // 2, "rows")):
                with act.Fori(first, first + BODIES // 2) as b:
                    steps.enter(b - first if first else b, 6)
                    attention_body(b, kind)
                steps.leave(BODIES // 2)

            with act.Fori(WO0, WO0 + NP // 2) as pair:
                split_pair(pair)
            copy_turned_whole(p1, 16)
            section("cols", r0, MQ0, NP // 2, 2 * BANK)
            for h in range(MH):
                act.wait_ge(cmax_ready, h + 1)
                for t in range(NT):
                    n = 2 * h + t
                    m = nc.scalar.activation(c_p[:, h, t, :], ps[:, 4 + h, t * T:(t + 1) * T], ACT.Exp,
                                             bias=nmx[:, n:n + 1], scale=M_SCALE, accum_out=dsum[:, n:n + 1])
                m.then_inc(cp_ready, 1)
            for h in range(MH):
                act.wait_ge(cT_ready, h + 1)
                nc.scalar.activation(c_pT[:, h, :, :], ps[:, h, :].rearrange("p (m q) -> p m q", m=NT),
                                     ACT.Copy).then_inc(cT_copied, 1)
            for g in range(KB // 2):
                act.wait_ge(co_ready, g + 1)
                nc.scalar.activation(p1[:, g * 2 * T:(g + 1) * 2 * T], ps[:, 4 + g % 4, :], ACT.Copy)\
                    .then_inc(co_hi, 1)
            with act.Fori(MO0, MO0 + NP // 2) as pair:
                split_pair(pair)
            act.wait_ge(keysT_ready, 1)
            nc.scalar.activation(keysT[:, :], ps[:, 7, 0:2 * NKEY], ACT.Copy).then_inc(keysT_copied, 1)
            copy_turned_whole(p1, 24)
            def gates(n):
                act.wait_ge(top_ready, n + 1)
                t = 0
                nc.scalar.activation(top, top, ACT.Exp, bias=ntop, accum_out=gsum).then_inc(gexp_ready, 1)

            for i in range(NP // 2):
                def take_scores(s):
                    act.wait_ge(ks_ready, i * 2 + s + 1)
                    nc.scalar.activation(key_scores[:, :, bass.ds((i * 2 + s) * BANK, BANK)],
                                         ps[:, 4 + 2 * s:6 + 2 * s, :], ACT.Copy).then_inc(ks_copied, 1)

                def take_queries(s):
                    act.wait_ge(w_used, (PQ0 + i) * PS + (s + 1) * NS)
                    if s == 0:
                        act.wait_ge(ks_copied, i * 2 + CREDIT)
                    nc.scalar.activation(pq_st[s].rearrange("p b t -> p (b t)"), bank(2 * s, 2),
                                         ACT.Copy).then_inc(proj_taken, 1)

                if i == 0:
                    split_hi(PQ0, range(4, 11))
                    take_queries(0)
                    split_hi(PQ0, [11])
                    take_scores(0)
                    split_hi(PQ0, range(12, 16))
                    gates(0)
                    split_hi(PQ0, range(16, 19))
                    take_queries(1)
                    split_hi(PQ0, [19])
                    take_scores(1)
                    split_hi(PQ0, range(20, 24))
                    gates(1)
                else:
                    split_hi(PQ0 + i, range(8, 11))
                    take_queries(0)
                    split_hi(PQ0 + i, [11])
                    take_scores(0)
                    split_hi(PQ0 + i, range(12, 16))
                    take_queries(1)
                    take_scores(1)

            def copy_placed(t, n, g):
                act.wait_ge(e_placed, n * TOPK + (t * P + 4 * g + 4 + OH))
                dst = experts[t][:, :].rearrange("p (i c) -> p i c", i=NKEY)[:, :, bass.ds(n * TOPK + 4 * g, 4)]
                nc.scalar.activation(dst, ps[:, g, :].rearrange("p (c i) -> p i c", c=4), ACT.Copy).then_inc(e_copied, 1)

            def hot_second(n, par, ms, t=0):
                for m in ms:
                    act.wait_ge(e_placed, n * TOPK + (t * P + m + 1))
                    steps.did(nc.scalar.activation(hot_j[m % OH], count[:, :], ACT.Abs, bias=wijT_now[par][:, 2, m:m + 1],
                                                    scale=-1.0))
                    steps.wait()
                    nc.scalar.activation(hot_j[m % OH], hot_j[m % OH], ACT.Relu, bias=1.0, scale=-1.0)\
                        .then_inc(j_act, 1)

            def peer_unit(t, unit, par, n=None, gates_of=True, final=False):
                own = not (isinstance(unit, int) and unit == 0)

                def sum_row(j):
                    act.wait_ge(prod_ready, sums(unit, j))
                    nc.scalar.activation(u_ring[t][POOLS], u_ring[t][POOLS], ACT.Copy,
                                         accum_out=hdot[par][:, j:j + 1]).then_inc(u_summed, 1)
                if own:
                    sum_row(POOLS)
                if t == 1:
                    act.wait_ge(now_ready, n + 1)
                    hot_second(n, par, range(OH))
                    for g in range(2):
                        copy_placed(0, n, g)
                if final:
                    hot_second(n, par, range(OH, TOPK))
                    for g in range(2, 4):
                        copy_placed(0, n, g)
                if own:
                    sum_row(POOLS + NU)
                if t == 1 and not final:
                    hot_second(n, par, range(OH, TOPK))
                act.wait_ge(h_ready, unit + 1)
                if own:
                    act.wait_ge(u_summed, sums(unit, POOLS + NU))
                nc.scalar.activation(act_h[par], hdot[par], ACT.Gelu).then_inc(gelu_ready, 1)
                if gates_of:
                    gates(unit + 2)
                if t == 1 and not final:
                    for g in range(2, 4):
                        copy_placed(0, n, g)

            def take_turned_wij(t):
                act.wait_ge(wij_turned, t + 1)
                for n in range(WIJ):
                    m = nc.scalar.activation(wijT[t][:, n, :], ps[:, 4, n * P:(n + 1) * P], ACT.Copy)
                m.then_inc(wijT_ready, 1)

            for par in range(2):
                peer_unit(0, par, par)
            with act.Fori(1, PH // 2) as hp:
                for par in range(2):
                    peer_unit(0, hp * 2 + par, par)
            take_turned_wij(0)

            def tile1_units(hp, last=False):
                for par in range(2):
                    peer_unit(1, hp * 2 + (PH + par), par, hp * 2 + par, not last, last and par == 1)
            with act.Fori(0, PH // 2 - 1) as hp:
                steps.enter(hp, 2 * TOPK)
                tile1_units(hp)
            steps.leave(PH // 2 - 1)
            tile1_units(PH // 2 - 1, last=True)
            take_turned_wij(1)
            with act.Fori(0, PH // 2) as hp:
                steps.enter(hp, 2 * len(ACT_J))
                for par in range(2):
                    n = hp * 2 + par
                    copy_placed(1, n, 0)
                    act.wait_ge(now_ready, n + (PH + 1))
                    hot_second(n, par, ACT_J, 1)
                    for g in range(1, 4):
                        copy_placed(1, n, g)
            steps.leave(PH // 2)

            def expert_parts(i, b, first=False):
                if not first:
                    act.wait_ge(v_used, i * 4 - 4)
                for t in range(NT):
                    m = nc.scalar.activation(e_hi[b][:, t * P:(t + 1) * P], experts[t][:, bass.ds(i * P, P)], ACT.Copy)
                m.then_inc(e_hi_ready, 1)

            def v_parts(pair, b, first=False, last=False):
                i = pair * 2 + b
                for q in range(4):
                    if q % 2 == 0:
                        act.wait_ge(v_landed[2 * b + q // 2], pair * 16 + 16)
                    if not first:
                        act.wait_ge(v_used, i * 4 + (q - 3))
                    nc.scalar.activation(v_hi[q], v_raw[2 * b + q // 2][:, q % 2 * QTR:(q % 2 + 1) * QTR],
                                         ACT.Copy).then_inc(v_hi_ready, 1)
                    if q == 1 and not last:
                        expert_parts(i + 1, 1 - b, first)

            act.wait_ge(e_copied, 2 * P // 4 + 4)
            expert_parts(0, 0, True)
            v_parts(0, 0, first=True)
            v_parts(0, 1)
            with act.Fori(1, NKEY // 2 - 1) as pair:
                for b in range(2):
                    v_parts(pair, b)
            v_parts(NKEY // 2 - 1, 0)
            v_parts(NKEY // 2 - 1, 1, last=True)

        @block.gpsimd
        def _(pool):
            steps = Steps(pool, pool_step)
            pool.sem_inc(o_normed, CREDIT)
            for dst, v in ((ident, 0.0), (before, 1.0), (neg_after, -1.0), (neg_ones, -1.0), (causal, 0.0)):
                steps.did(pool.memset(dst[:, :], v))
            steps.did(pool.memset(nhalf, -0.5))
            steps.wait()
            steps.did(pool.affine_select(out=ident[:, :], in_=ident[:, :], compare_op=ALU.not_equal, fill=1.0,
                                         base=0, pattern=[[-1, P]], channel_multiplier=1))
            steps.did(pool.affine_select(out=before[:, :], in_=before[:, :], compare_op=ALU.is_gt, fill=0.0,
                                         base=0, pattern=[[1, P]], channel_multiplier=-1))
            steps.did(pool.affine_select(out=neg_after[:, :], in_=neg_after[:, :], compare_op=ALU.is_gt, fill=0.0,
                                         base=0, pattern=[[-1, P]], channel_multiplier=1))
            steps.did(pool.affine_select(out=causal[:, P:T], in_=causal[:, P:T], compare_op=ALU.is_ge,
                                         fill=NEG_BIG, base=0, pattern=[[-1, P]], channel_multiplier=1))
            steps.did(pool.iota(iota[:, :], pattern=[[1, TOPK]], base=0, channel_multiplier=0,
                                allow_small_or_imprecise_dtypes=True))
            steps.wait()
            pool.sem_inc(consts_ready, 1)

            def power(src, dst, nth):
                pool.wait_ge(ms_ready, nth)
                nc.gpsimd.tensor_tensor(dst, src, nhalf, ALU.pow).then_inc(rms_ready, 1)

            def attention_body(b):
                pool.wait_ge(z_ready, b * 2 + 2)
                pool.wait_ge(dfT_ready, b * 2 + 2)
                stage(b + 1)
                powers(b)

            def stage(b):
                nc.gpsimd.tensor_copy(k_st, r1[:, bass.ds(b * 2 * T + SBH * T, 2 * T)]).then_inc(k_staged, 1)
                src = df_qk.rearrange("p t (q c) -> p t q c", q=2)[:, :, :, bass.ds(b * 2 * P, 2 * P)]
                for t in range(NT):
                    m = nc.gpsimd.tensor_copy(df_st[:, t], src[:, t])
                m.then_inc(df_staged, 1)

            def powers(b):
                power(ss, rs, b * 2 + 1)
                power(dss, drs, b * 2 + 2)

            pool.wait_ge(proj_taken, 2 * MKV0 + CREDIT)
            pool.wait_ge(roped, 3)
            stage(0)
            with pool.Fori(0, BODIES - 1) as b:
                attention_body(b)
            powers(BODIES - 1)
            pool.wait_ge(w_used, WO0 * PS)
            pool.dma_start(z1, x_rows).then_inc(z_landed, 16)
            for n, (g, b) in enumerate(((ln1_g, ln1_b), (ln2_g, ln2_b))):
                if n:
                    pool.wait_ge(x_ready, 4 * n)
                pool.dma_start(gain_b, g[0].partition_broadcast(P)).then_inc(gb_landed, 16)
                pool.dma_start(bias_b, b[0].partition_broadcast(P)).then_inc(gb_landed, 16)
                pool.wait_ge(var_ready, n + 1)
                nc.gpsimd.tensor_tensor(rstd, veps, nhalf[:, 0:NT], ALU.pow).then_inc(rstd_ready, 1)
                for g in range(8):
                    hi, lo = [r[:, g * 2 * T:(g + 1) * 2 * T] for r in (p1, p3)]
                    pool.wait_ge(turned_hi, (n + 2) * 8 + g + 1)
                    pool.wait_ge(turned_taken, (n + 2) * 8 + g + 1)
                    nc.gpsimd.tensor_tensor(lo, whole[g % 4], hi.bitcast(F32), ALU.subtract).then_inc(turned_lo_ready, 1)
                if n == 0:
                    pool.wait_ge(cT_ready, MH)
                    pool.dma_start(keys_in.rearrange("p (s d) -> p s d", s=2),
                                   sub_keys[0].rearrange("s n d -> n s d")).then_inc(keys_landed, 16)
            def carry_wait():
                pool.sem_inc(waited, 1)

            def gather(t, par, slot, j):
                pool.indirect_dma_start(u_ring[t][slot], None, peer_u[0],
                                        bass.IndirectOffsetOnAxis(ap=idx[par][:, j:j + 1], axis=0))\
                    .then_inc(u_landed[slot], 16)

            def gather_u(t, unit, par, j):
                if j % NU == POOLS and not (isinstance(unit, int) and unit == 1 and j < NU):
                    pool.wait_ge(u_summed, sums(unit, j) - 1)
                elif isinstance(unit, int) and unit == 1 and j < NU:
                    if j == EARLY:
                        pool.wait_ge(lo_ready, (PQ0 + NP // 2) * PS)
                    pool.wait_ge(u_used, max(range(j, TOPK, EARLY)) + 1 if j < EARLY else TOPK)
                elif j < NU:
                    pool.wait_ge(u_used, dots(unit - 1, j + NU))
                else:
                    pool.wait_ge(u_used, dots(unit, j - NU))
                carry_wait()
                gather(t, par, j % NU, j)

            def split_lo(j):
                pool.wait_ge(hi_ready, PQ0 * PS + j + 1)
                nc.gpsimd.tensor_tensor(w_lo[j % SPLIT], raw[j % RAW], w_hi[j % SPLIT].bitcast(F32),
                                        ALU.subtract).then_inc(lo_ready, 1)

            def first_u(j):
                if j >= EARLY:
                    pool.wait_ge(u_used, j + 1 - EARLY)
                    carry_wait()
                gather(0, 0, j % EARLY, j)

            for j in range(4, 2 * PS):
                split_lo(j)
                if j == 18:
                    pool.wait_ge(idx_ready, 1)
                    carry_wait()
                if 18 <= j < 21:
                    first_u(2 * (j - 18))
                    first_u(2 * (j - 18) + 1)
                if 26 <= j < 31:
                    first_u(EARLY + 2 * (j - 26))
                    first_u(EARLY + 2 * (j - 26) + 1)
            pool.wait_ge(lo_ready, (PQ0 + NP // 2) * PS)
            pool.wait_ge(ks_copied, NP + CREDIT)
            pool.iota(count[:, :], pattern=[[1, P]], base=0, channel_multiplier=0,
                      allow_small_or_imprecise_dtypes=True).then_inc(consts_ready, 1)
            pool.wait_ge(consts_ready, 2)

            def multiply(t, unit, par, j):
                pool.wait_ge(u_landed[POOLS], (unit * 2 + (j // NU + 1 + u_extra[POOLS])) * 16)
                nc.gpsimd.tensor_tensor(u_ring[t][POOLS], u_ring[t][POOLS], x2[:, t, :], ALU.mult)\
                    .then_inc(prod_ready, 1)

            def hot_first(t, n, par, ms):
                for m in ms:
                    pool.wait_ge(e_placed, n * TOPK + (t * P + m + 1))
                    carry_wait()
                    nc.gpsimd.tensor_scalar(hot_iw[m % OH], count[:, :], wijT_now[par][:, 1, m:m + 1],
                                            wijT_now[par][:, 0, m:m + 1], ALU.is_equal, ALU.mult).then_inc(iw_pool, 1)

            def take_tokens(t, n, par):
                pool.wait_ge(e_placed, n * TOPK + (t * P + 1))
                nc.gpsimd.tensor_copy(wijT_now[par], wijT[t][:, :, bass.ds(n * TOPK, TOPK)]).then_inc(now_ready, 1)

            def peer_unit(t, unit, par, n=None, t_next=None):
                later = not (isinstance(unit, int) and unit == 0)
                if t == 1:
                    pool.wait_ge(wijT_ready, 1)
                    take_tokens(0, n, par)
                if later:
                    for j in range(NU, TOPK):
                        if j == NU + 2:
                            multiply(t, unit, par, POOLS)
                        gather_u(t, unit, par, j)
                if t == 1:
                    pool.wait_ge(now_ready, n + 1)
                    hot_first(0, n, par, range(OH if t_next is not None else TOPK))
                if t_next is not None:
                    pool.wait_ge(idx_ready, unit + 2)
                    carry_wait()
                for j in range(NU):
                    if later and j == 2:
                        multiply(t, unit, par, POOLS + NU)
                    if t_next is not None:
                        gather_u(t_next, unit + 1, 1 - par, j)
                if t == 1 and t_next is not None:
                    hot_first(0, n, par, range(OH, TOPK))

            for par in range(2):
                peer_unit(0, par, par, t_next=0)
            with pool.Fori(1, PH // 2 - 1) as hp:
                for par in range(2):
                    peer_unit(0, hp * 2 + par, par, t_next=0)
            for par in range(2):
                peer_unit(0, PH - 2 + par, par, t_next=par)
            with pool.Fori(0, PH // 2 - 1) as hp:
                for par in range(2):
                    peer_unit(1, hp * 2 + (PH + par), par, n=hp * 2 + par, t_next=1)
            peer_unit(1, UNITS - 2, 0, n=PH - 2, t_next=1)
            peer_unit(1, UNITS - 1, 1, n=PH - 1)

            pool.wait_ge(wijT_ready, 2)
            with pool.Fori(0, PH // 2) as hp:
                for par in range(2):
                    n = hp * 2 + par
                    take_tokens(1, n, par)
                    pool.wait_ge(now_ready, n + (PH + 1))
                    hot_first(1, n, par, POOL_IW)
            pool.wait_ge(e_placed, 2 * P + OH)
            pool.dma_start(gain3_b, ln3_g[0].partition_broadcast(P)).then_inc(gb_landed, 16)
            pool.dma_start(bias3_b, ln3_b[0].partition_broadcast(P)).then_inc(gb_landed, 16)
            for t in range(NT):
                pool.wait_ge(var_ready, 3 + t)
                nc.gpsimd.tensor_tensor(rstd[:, t:t + 1], veps[:, t:t + 1], nhalf[:, 0:1], ALU.pow).then_inc(rstd_ready, 1)

        @block.vector
        def _(dve):
            steps = Steps(dve, dve_step)

            def chain(ins):
                steps.did(ins)
                steps.wait()

            def turned_lo(dst, nth, groups):
                for g in groups:
                    hi, lo = [r[:, g * 2 * T:(g + 1) * 2 * T] for r in dst]
                    dve.wait_ge(turned_hi, nth + g + 1)
                    nc.vector.tensor_tensor(lo, ps[:, 4 + (nth + g) % 4, :], hi.bitcast(F32),
                                            ALU.subtract).then_inc(turned_taken, 1)

            def split_lo(pair, js):
                for j in js:
                    dve.wait_ge(hi_ready, pair * PS + j + 1)
                    nc.vector.tensor_tensor(w_lo[j % SPLIT], raw[j % RAW], w_hi[j % SPLIT].bitcast(F32),
                                            ALU.subtract).then_inc(lo_ready, 1)

            for n in range(2):
                turned_lo((p0, p4), 0, range(4 * n, 4 * n + 4))
                split_lo(0, range(2 * n, 2 * n + 2))

            dve.wait_ge(small_landed, 64)
            for n in range(2):
                steps.did(nc.vector.tensor_tensor(lam_pr, lam_in[:, 2 * n * QD:(2 * n + 1) * QD],
                                                  lam_in[:, (2 * n + 1) * QD:(2 * n + 2) * QD], ALU.mult))
                steps.wait()
                steps.did(nc.vector.tensor_reduce(lam_s[:, n:n + 1], lam_pr, AX_X, ALU.add))
                steps.wait()
            dve.sem_inc(roped, 1)
            steps.did(nc.vector.tensor_scalar(dfg[:, :], dfg[:, :], 1.0 - LAMBDA_INIT, None, ALU.mult))
            dve.wait_ge(roped, 2)
            chain(nc.vector.tensor_tensor(neg_lam, lam_e[:, 1:2], lam_e[:, 0:1], ALU.subtract))
            steps.did(nc.vector.tensor_scalar(neg_lam, neg_lam, -LAMBDA_INIT, None, ALU.add))

            with dve.Fori(0, IN_PAIRS - 1) as pair:
                split_lo(pair, range(4, 20))
            split_lo(IN_PAIRS - 1, range(4, 8))

            dve.wait_ge(proj_taken, 10 + CREDIT)
            heads = 2 * SBW // QD
            both = ta[:, 0:heads * ROT].rearrange("p (h c) -> p h c", h=heads)
            cross = ta[:, heads * ROT:2 * heads * ROT].rearrange("p (h c) -> p h c", h=heads)
            for t in range(NT):
                part = df_qk[:, t].rearrange("p (h c) -> p h c", c=QD)[:, :, 0:ROT]
                cos_t = cos2[:, t:t + 1, :].to_broadcast([P, heads, ROT])
                sin_t = sin2[:, t:t + 1, :].to_broadcast([P, heads, ROT])
                steps.did(nc.vector.tensor_tensor(both, part, cos_t, ALU.mult))
                steps.did(nc.vector.tensor_tensor(cross[:, :, 0:HR], part[:, :, HR:ROT], sin_t[:, :, 0:HR], ALU.mult))
                steps.did(nc.vector.tensor_tensor(cross[:, :, HR:ROT], part[:, :, 0:HR], sin_t[:, :, HR:ROT], ALU.mult))
                steps.wait()
                steps.did(nc.vector.tensor_tensor(part, both, cross, ALU.add))
                steps.wait()
            dve.sem_inc(roped, 1)

            split_lo(IN_PAIRS - 1, range(8, 20))
            turned_lo((p0, p4), 8, range(8))

            diag_of = lambda a: a.rearrange("p (b c) -> p b c", b=3)[:, 0:3:2, :]
            before2 = before[:, :].unsqueeze(1).to_broadcast([P, 2, P])
            def rms_norm(b, nth, src_bank, sums, root, gain_of, dst):
                dve.wait_ge(ss_ready, nth)
                nc.vector.tensor_scalar(sums, sums, 1.0 / DH, RMS_EPS, ALU.mult, ALU.add).then_inc(ms_ready, 1)
                dve.wait_ge(rms_ready, nth)
                for c in range(4):
                    m = nc.vector.scalar_tensor_tensor(out=dst[:, c, :], in0=ps[:, src_bank, c * P:(c + 1) * P],
                                                       scalar=root[:, c:c + 1], in1=gain_of(c // 2),
                                                       op0=ALU.mult, op1=ALU.mult)
                m.then_inc(o_normed, 1)

            def attention_body(b):
                pair = b + MKV0
                for hh in range(2):
                    dve.wait_ge(e_ready, b * 2 + hh + 1)
                    chain(nc.vector.scalar_tensor_tensor(out=sp_z[hh], in0=e_z[hh], scalar=0.0, in1=sp_z[hh],
                                                         op0=ALU.max, op1=ALU.add))
                    chain(nc.vector.tensor_tensor(e_z[hh], e_z[hh], sp_z[hh], ALU.subtract))
                    nc.vector.tensor_tensor(diag_of(sp_z[hh]), diag_of(sp_z[hh]), before2, ALU.mult)\
                        .then_inc(sp_ready, 1)
                    split_lo(pair, (4 + 2 * hh, 5 + 2 * hh))
                dve.wait_ge(s_ready, b + 1)
                for st in range(2):
                    steps.did(nc.vector.tensor_tensor(s_t0[:, st:4:2, :], ps[:, 6 + st, 0:T].rearrange("p (h c) -> p h c", h=2),
                                                      causal[:, P:T].unsqueeze(1).to_broadcast([P, 2, P]), ALU.add))
                for hh in range(2):
                    steps.did(nc.vector.tensor_tensor(s_t1[hh], ps[:, 4:6, hh * T:(hh + 1) * T],
                                                      causal[:, :].unsqueeze(1).to_broadcast([P, 2, T]), ALU.add))
                steps.wait()
                steps.did(nc.vector.tensor_reduce(mx[:, 0:4], s_t0, AX_X, ALU.max))
                for hh in range(2):
                    steps.did(nc.vector.tensor_reduce(mx[:, 4 + 2 * hh:6 + 2 * hh], s_t1[hh], AX_X, ALU.max))
                steps.wait()
                nc.vector.tensor_scalar(nmx, mx, -DF_SCALE, None, ALU.mult).then_inc(smax_ready, 1)
                for hh in range(2):
                    dve.wait_ge(stick_ready, b * 2 + hh + 1)
                    nc.vector.tensor_tensor(e_z[hh], e_z[hh], ps[:, 2 + hh, 0:ZC], ALU.add).then_inc(wexp_in, 1)
                for hh in range(2):
                    dve.wait_ge(wexp_out, b * 2 + hh + 1)
                    nc.vector.tensor_tensor(diag_of(sp_z[hh]), diag_of(sp_z[hh]), before2, ALU.mult)\
                        .then_inc(w_ready, 1)
                dve.wait_ge(p_ready, b + 1)
                chain(nc.vector.reciprocal(rsum, dsum))
                chain(nc.vector.tensor_scalar(c2, rsum, neg_lam, None, ALU.mult))
                for hh in range(2):
                    p2 = (s_t0[:, 2 * hh + 1, :], s_t1[hh][:, 1, :])
                    p1 = (s_t0[:, 2 * hh, :], s_t1[hh][:, 0, :])
                    for n in range(2):
                        c = 4 * n + 2 * hh
                        steps.did(nc.vector.tensor_scalar(p2[n], p2[n], c2[:, c + 1:c + 2], None, ALU.mult))
                    steps.wait()
                    for n in range(2):
                        c = 4 * n + 2 * hh
                        m = nc.vector.scalar_tensor_tensor(out=p1[n], in0=p1[n], scalar=rsum[:, c:c + 1], in1=p2[n],
                                                           op0=ALU.mult, op1=ALU.add)
                    m.then_inc(pw_ready, 1)
                split_lo(pair, range(8, 12))
                rms_norm(b, b * 2 + 1, 7, ss, rs, lambda hh: sbg[:, bass.ds((b * 2 + hh) * DH, DH)], sb_n)
                split_lo(pair, range(12, 16))
                rms_norm(b, b * 2 + 2, 6, dss, drs, lambda hh: dfg[:, :], df_n)
                mixed_rests(b, 0, 2)
                split_lo(pair, range(16, 20))
                mixed_rests(b, 1, 7)

            def mixed_rests(b, kind, src_bank):
                dve.wait_ge(oT_hi, b * 2 + kind + 1)
                nc.vector.tensor_tensor(mixed_lo[:, kind, :, bass.ds(b * T, T)],
                                        ps[:, src_bank, :].rearrange("p (h t) -> p h t", h=2),
                                        p1[:, bass.ds(b * 2 * T + kind * SBH * T, 2 * T)].bitcast(F32)
                                        .rearrange("p (h t) -> p h t", h=2), ALU.subtract).then_inc(oT_copied, 1)

            with dve.Fori(0, BODIES) as b:
                steps.enter(b, 17)
                attention_body(b)
            steps.leave(BODIES)

            def residual(z, x_old, first_pair):
                with dve.Fori(0, NP // 2) as i:
                    steps.enter(i, 2)
                    for s in range(2):
                        q = i * 2 + s
                        cols = bass.ds(q * BANK, BANK)
                        split_lo(i + first_pair, range(4 + 8 * s, 11 + 8 * s))
                        dve.wait_ge(w_used, (i + first_pair) * PS + (s + 1) * NS)
                        nc.vector.scalar_tensor_tensor(out=z[:, :, cols], in0=x_old[:, :, cols], scalar=ALPHA,
                                                       in1=ps[:, 2 * s:2 * s + 2, :], op0=ALU.mult,
                                                       op1=ALU.add).then_inc(proj_taken, 1)
                        split_lo(i + first_pair, [11 + 8 * s])
                        dve.wait_ge(proj_taken, i * 2 + (2 * first_pair + s + 1 + CREDIT))
                        for t in range(NT):
                            m = nc.vector.bn_stats(small[:, bass.ds(q * 6 + (65 + t * NP * 6), 6)], z[:, t, cols])
                        steps.did(m)
                steps.leave(NP // 2)

            def norm(z, dst, nth):
                steps.wait()
                for t in range(NT):
                    steps.did(nc.vector.bn_aggr(mvar[:, t, :], stats[:, t].rearrange("p q c -> p (q c)")))
                steps.wait()
                nc.vector.tensor_scalar(veps, mvar[:, :, 1], LN_EPS, None, ALU.add).then_inc(var_ready, 1)
                dve.wait_ge(gb_landed, 32 * nth + 32)
                for q in range(NP):
                    cols = slice(q * BANK, (q + 1) * BANK)
                    for t in range(NT):
                        steps.did(nc.vector.scalar_tensor_tensor(out=dst[:, t, cols], in0=z[:, t, cols],
                                                                 scalar=mvar[:, t, 0:1], in1=gain_b[:, cols],
                                                                 op0=ALU.subtract, op1=ALU.mult))
                    if q == 0:
                        dve.wait_ge(rstd_ready, nth + 1)
                    for t in range(NT):
                        steps.wait(but=NT - 1 - t)
                        m = nc.vector.scalar_tensor_tensor(out=dst[:, t, cols], in0=dst[:, t, cols],
                                                           scalar=rstd[:, t:t + 1], in1=bias_b[:, cols],
                                                           op0=ALU.mult, op1=ALU.add)
                    m.then_inc(x_ready, 1)

            dve.wait_ge(z_landed, 16)
            residual(z1, z1, WO0)
            norm(z1, x1, 0)
            with dve.Fori(MQ0, MQ0 + NP // 2) as pair:
                split_lo(pair, range(4, 20))

            for h in range(MH):
                dve.wait_ge(cs_ready, h + 1)
                chain(nc.vector.tensor_reduce(mx[:, 2 * h:2 * h + 2], ps[:, 4 + h, :].rearrange("p (t m) -> p t m", t=NT),
                                              AX_X, ALU.max))
                nc.vector.tensor_scalar(nmx[:, 2 * h:2 * h + 2], mx[:, 2 * h:2 * h + 2], -M_SCALE, None,
                                        ALU.mult).then_inc(cmax_ready, 1)
            for h in range(MH):
                dve.wait_ge(cp_ready, h + 1)
                chain(nc.vector.reciprocal(rsum[:, 2 * h:2 * h + 2], dsum[:, 2 * h:2 * h + 2]))
                for t in range(NT):
                    m = nc.vector.tensor_scalar(c_p[:, h, t, :], c_p[:, h, t, :], rsum[:, 2 * h + t:2 * h + t + 1], None,
                                                ALU.mult)
                m.then_inc(cn_ready, 1)
            for g in range(KB // 2):
                hi, lo = [r[:, g * 2 * T:(g + 1) * 2 * T] for r in (p1, p3)]
                dve.wait_ge(co_hi, g + 1)
                nc.vector.tensor_tensor(lo, ps[:, 4 + g % 4, :], hi.bitcast(F32), ALU.subtract).then_inc(co_copied, 1)
            residual(x1, x1, MO0)
            norm(x1, x2, 1)

            def ordered(ins):
                dve.drain()

            def copy_scores(t, h):
                ordered(nc.vector.tensor_copy(sc, key_scores[:, t, bass.ds(h * 2 * NKEY, 2 * NKEY)]))

            def top16(values, left, best, where):
                ordered(nc.vector.max(best[:, 0:8], values))
                nc.vector.max_index(where[:, 0:8], best[:, 0:8], values)
                ordered(nc.vector.match_replace(left, best[:, 0:8], values, NEG_MAX))
                ordered(nc.vector.max(best[:, 8:16], left))
                ordered(nc.vector.max_index(where[:, 8:16], best[:, 8:16], left))

            def retrieve(unit, par, t, h, finish):
                copy_scores(t, h)
                for n in range(2):
                    c = slice(n * NKEY, (n + 1) * NKEY)
                    top16(sc[:, c], sc_left[:, c], val[:, 16 * n:16 * n + 16], ix[:, 16 * n:16 * n + 16])
                nc.vector.tensor_copy(ixf, ix)
                grid = lambda a: a.rearrange("p (i j) -> p i j", i=TOPK)
                ordered(nc.vector.tensor_tensor(grid(cand), val[:, 0:16].unsqueeze(2).to_broadcast([P, TOPK, TOPK]),
                                              val[:, 16:32].unsqueeze(1).to_broadcast([P, TOPK, TOPK]), ALU.add))
                top16(cand, cand_left, top, pos)
                nc.vector.tensor_scalar(ntop, top[:, 0:1], -1.0, None, ALU.mult).then_inc(top_ready, 1)
                nc.vector.tensor_scalar(ij[:, 0:16], pos, 4, None, ALU.logical_shift_right)
                ordered(nc.vector.tensor_scalar(ij[:, 16:32], pos, 15, None, ALU.bitwise_and))
                ordered(nc.vector.tensor_copy(ijf, ij))
                for n in range(2):
                    ordered(nc.vector.tensor_tensor(grid(hot), ijf[:, 16 * n:16 * n + 16].unsqueeze(2).to_broadcast([P, TOPK, TOPK]),
                                                  iota[:, :].unsqueeze(1).to_broadcast([P, TOPK, TOPK]), ALU.is_equal))
                    ordered(nc.vector.tensor_tensor(grid(hot_v), grid(hot),
                                                  ixf[:, 16 * n:16 * n + 16].unsqueeze(1).to_broadcast([P, TOPK, TOPK]),
                                                  ALU.mult))
                    ordered(nc.vector.tensor_reduce(picked[:, 16 * n:16 * n + 16], grid(hot_v), AX_X, ALU.add))
                finish()
                for n in range(2):
                    nc.vector.tensor_copy(wij[t][1 + n][:, bass.ds(h * TOPK, TOPK)], picked[:, 16 * n:16 * n + 16])
                nc.vector.scalar_tensor_tensor(out=idx[par], in0=picked[:, 0:16], scalar=float(NKEY),
                                               in1=picked[:, 16:32], op0=ALU.mult, op1=ALU.add).then_inc(idx_ready, 1)
                dve.wait_ge(gexp_ready, unit + 1)
                ordered(nc.vector.reciprocal(gsum, gsum))
                ordered(nc.vector.tensor_scalar(gate[par], top, gsum, None, ALU.mult))

            def peer_unit(t, unit, par, h, following):
                for j in range(TOPK):
                    if isinstance(unit, int) and unit == 0:
                        slot, landed = j % EARLY, j // EARLY + 1
                    elif j % NU == POOLS:
                        continue
                    else:
                        slot = j % NU
                        landed = unit * 2 + (j // NU + 1 + u_extra[slot])
                    dve.wait_ge(u_landed[slot], landed * 16)
                    nc.vector.tensor_tensor_reduce(u_ring[t][slot], u_ring[t][slot], x2[:, t, :], 1.0, 0.0,
                                                   ALU.mult, ALU.add, hdot[par][:, j:j + 1]).then_inc(u_used, 1)
                dve.wait_ge(u_used, dots(unit, TOPK - 1))
                dve.sem_inc(h_ready, 1)

                def finish():
                    dve.wait_ge(gelu_ready, unit + 1)
                    nc.vector.tensor_tensor(wij[t][0][:, bass.ds(h * TOPK, TOPK)], act_h[par], gate[par],
                                            ALU.mult).then_inc(a_ready, 1)
                    dve.wait_ge(a_ready, unit + 1)

                if isinstance(unit, int) and unit == 0:
                    dve.wait_ge(ks_copied, NP + CREDIT)
                if following:
                    retrieve(unit + 2, par, *following, finish)
                else:
                    finish()

            dve.wait_ge(ks_copied, 1 + CREDIT)
            for par in range(2):
                retrieve(par, par, 0, par, lambda: None)
            for par in range(2):
                peer_unit(0, par, par, par, (0, 2 + par))
            with dve.Fori(1, PH // 2 - 1) as hp:
                for par in range(2):
                    peer_unit(0, hp * 2 + par, par, hp * 2 + par, (0, hp * 2 + (2 + par)))
            for par in range(2):
                peer_unit(0, PH - 2 + par, par, PH - 2 + par, (1, par))
            with dve.Fori(0, PH // 2 - 1) as hp:
                for par in range(2):
                    peer_unit(1, hp * 2 + (PH + par), par, hp * 2 + par, (1, hp * 2 + (2 + par)))
            for par in range(2):
                peer_unit(1, UNITS - 2 + par, par, PH - 2 + par, None)

            dve.wait_ge(wijT_ready, 2)
            with dve.Fori(0, PH) as n:
                for g in range(4):
                    dve.wait_ge(e_placed, n * TOPK + (P + 4 * g + 4))
                    if 4 * g not in ACT_J:
                        slot = 4 * g % OH * P
                        second = wijT[1][:, 2, bass.ds(n * TOPK + 4 * g, 4)].unsqueeze(2).to_broadcast([P, 4, P])
                        nc.vector.tensor_tensor(ta[:, slot:slot + 4 * P].rearrange("p (c j) -> p c j", c=4),
                                                count[:, :].unsqueeze(1).to_broadcast([P, 4, P]), second,
                                                ALU.is_equal).then_inc(j_dve, 1)
                    for m in range(4 * g, 4 * g + 4):
                        if m not in POOL_IW:
                            w, i = [wijT[1][:, c, bass.ds(n * TOPK + m, 1)] for c in range(2)]
                            nc.vector.tensor_scalar(hot_iw[m % OH], count[:, :], i, w, ALU.is_equal, ALU.mult)\
                                .then_inc(iw_dve, 1)

            def rests(i, b):
                dve.wait_ge(e_hi_ready, i + 1)
                for t in range(NT):
                    c = slice(t * P, (t + 1) * P)
                    m = nc.vector.tensor_tensor(e_lo[b][:, c], experts[t][:, bass.ds(i * P, P)], e_hi[b][:, c].bitcast(F32),
                                                ALU.subtract)
                m.then_inc(e_lo_ready, 1)
                for q in range(4):
                    dve.wait_ge(v_hi_ready, i * 4 + (q + 1))
                    nc.vector.tensor_tensor(v_lo[q], v_raw[2 * b + q // 2][:, q % 2 * QTR:(q % 2 + 1) * QTR],
                                            v_hi[q].bitcast(F32), ALU.subtract).then_inc(v_lo_ready, 1)

            with dve.Fori(0, NKEY // 2) as i:
                for b in range(2):
                    rests(i * 2 + b, b)

            for t in range(NT):
                dve.wait_ge(v_used, NKEY * 4 - 2 + 2 * t)
                chunk = [slice(q * BANK, (q + 1) * BANK) for q in range(NP)]
                for q in range(NP + 1):
                    if q < NP:
                        steps.did(nc.vector.scalar_tensor_tensor(out=x2[:, t, chunk[q]], in0=x2[:, t, chunk[q]], scalar=ALPHA,
                                                                 in1=ps[:, 4 * t + q, :], op0=ALU.mult, op1=ALU.add))
                    if q > 0:
                        steps.wait(but=int(q < NP))
                        steps.did(nc.vector.bn_stats(stats[:, t, q - 1, :], x2[:, t, chunk[q - 1]]))
                steps.wait()
                chain(nc.vector.bn_aggr(mvar[:, t, :], stats[:, t].rearrange("p q c -> p (q c)")))
                nc.vector.tensor_scalar(veps[:, t:t + 1], mvar[:, t, 1:2], LN_EPS, None, ALU.add).then_inc(var_ready, 1)
                dve.wait_ge(gb_landed, 96)
                halves_of = [slice(n * D // 2, (n + 1) * D // 2) for n in range(2)]
                for c in halves_of:
                    steps.did(nc.vector.scalar_tensor_tensor(out=y_out[:, t, c], in0=x2[:, t, c], scalar=mvar[:, t, 0:1],
                                                             in1=gain3_b[:, c], op0=ALU.subtract, op1=ALU.mult))
                dve.wait_ge(rstd_ready, 3 + t)
                for n, c in enumerate(halves_of):
                    steps.wait(but=1 - n)
                    nc.vector.scalar_tensor_tensor(out=y_out[:, t, c], in0=y_out[:, t, c], scalar=rstd[:, t:t + 1],
                                                   in1=bias3_b[:, c], op0=ALU.mult, op1=ALU.add).then_inc(y_ready, 1)


_INS = ["x", "mem", "w_in", "sb_norm_gain", "df_lambda", "df_subln_gain", "w_o", "ln1_gain", "ln1_bias",
        "w_mq", "w_mkv", "w_mo", "ln2_gain", "ln2_bias", "w_pq", "peer_sub_keys", "peer_u", "peer_v",
        "ln3_gain", "ln3_bias"]


def rope_table(tokens, rot):
    import numpy as np

    half = rot // 2
    freq = np.power(np.float32(ROPE_THETA), -np.arange(half, dtype=np.float32) * np.float32(2.0) / np.float32(rot))
    ang = np.arange(tokens, dtype=np.float32)[:, None] * freq.astype(np.float32)[None, :]
    cos, sin = np.cos(ang), np.sin(ang)
    return np.concatenate([cos, cos, -sin, sin], axis=1).astype(np.float32)


def kernel(**inputs):
    import numpy as np
    import concourse.bacc as bacc
    from concourse.bass_utils import run_bass_kernel_spmd as run

    nc = bacc.Bacc("TRN2", target_bir_lowering=False, num_devices=1)
    arrays = {f"in_{n}_dram": np.ascontiguousarray(inputs[n]) for n in _INS}
    _, tokens, width = inputs["x"].shape
    arrays["rope_dram"] = rope_table(tokens, inputs["df_lambda"].shape[2] // 4)
    args = [nc.dram_tensor(n, a.shape, mybir.dt.from_np(a.dtype), kind="ExternalInput").ap()
            for n, a in arrays.items()]
    out = nc.dram_tensor("out_dram", (1, tokens, width), F32, kind="ExternalOutput").ap()
    layer_program(nc, *args, out)
    return run(nc, [arrays], core_ids=[0]).results[0]["out_dram"]
```
